# Optimizing a Trainium2 kernel written in Bass

```python
import jax, jax.numpy as jnp
from jax import lax
import numpy as np

D_MODEL = 1024
BATCH = 1
SEQ = 128
DEPTH = 2
DEC_BATCH = 1
DEC_SEQ = 128
PAST_LEN = 128

GRID_W = 64
HEAD_DIM = 64
W_GROUP = D_MODEL // 4
H_GDN = W_GROUP // HEAD_DIM
H_RET = W_GROUP // HEAD_DIM
H_NAT = W_GROUP // HEAD_DIM
SC_WIDTH = W_GROUP
GDN_CONV = 3
SC_CONV = 3
CHUNK = 64
WIN_ROWS = 8
WIN_COLS = 16
QBLOCK = 128
ROPE_BASE = 10000.0
N_GROUPS = 4
EXPERTS_PER_GROUP = 8
N_EXPERTS = N_GROUPS * EXPERTS_PER_GROUP
TOP_K = 2
EXPERT_FF = 256
EPS = 1e-6
IN_SIZES = (3 * W_GROUP, W_GROUP, 2 * H_GDN, 2 * H_GDN, 3 * W_GROUP, W_GROUP, 3 * W_GROUP, 3 * SC_WIDTH)
IN_WIDTH = 3 * W_GROUP + W_GROUP + 4 * H_GDN + 4 * W_GROUP + 3 * W_GROUP + 3 * SC_WIDTH

kernel_name = 'hybrid_diffusion_parallel_heads_step'

def rms_norm(x, w):
    xf = x.astype(jnp.float32)
    y = xf * lax.rsqrt(jnp.mean(xf * xf, axis=-1, keepdims=True) + EPS)
    return (y * w.astype(jnp.float32)).astype(x.dtype)

def l2_normalize(x):
    xf = x.astype(jnp.float32)
    return xf * lax.rsqrt(jnp.sum(xf * xf, axis=-1, keepdims=True) + EPS)

def head_group_norm(x):
    xf = x.astype(jnp.float32)
    mu = jnp.mean(xf, axis=-1, keepdims=True)
    xc = xf - mu
    return xc * lax.rsqrt(jnp.mean(xc * xc, axis=-1, keepdims=True) + EPS)

def depthwise_conv(x, w):
    k, ch = w.shape
    return lax.conv_general_dilated(x, w[:, None, :].astype(x.dtype), window_strides=(1,),
                                    padding=[(k // 2, k // 2)], dimension_numbers=('NWC', 'WIO', 'NWC'),
                                    feature_group_count=ch)

def axial_rope(x):
    t = jnp.arange(x.shape[1])
    row = (t // GRID_W).astype(jnp.float32)
    col = (t % GRID_W).astype(jnp.float32)
    nf = HEAD_DIM // 4
    inv_freq = jnp.power(ROPE_BASE, -jnp.arange(nf, dtype=jnp.float32) / nf)

    def rotate(xh, pos):
        ang = pos[:, None] * inv_freq[None, :]
        cos = jnp.cos(ang)[:, None, :]
        sin = jnp.sin(ang)[:, None, :]
        x1 = xh[..., :nf].astype(jnp.float32)
        x2 = xh[..., nf:].astype(jnp.float32)
        return jnp.concatenate([x1 * cos - x2 * sin, x2 * cos + x1 * sin], axis=-1)

    half = HEAD_DIM // 2
    return jnp.concatenate([rotate(x[..., :half], row), rotate(x[..., half:], col)], axis=-1).astype(x.dtype)

def to_chunks(a):
    b, t, h, d = a.shape
    return a.reshape(b, t // CHUNK, CHUNK, h, d).transpose(1, 0, 3, 2, 4)

def from_chunks(a):
    n, b, h, c, d = a.shape
    return a.transpose(1, 0, 3, 2, 4).reshape(b, n * c, h, d)

def gated_delta_chunked(q, k, v, log_a, beta, s0):
    dk = q.shape[-1]
    q = to_chunks(q.astype(jnp.float32)) * (dk ** -0.5)
    k = to_chunks(k.astype(jnp.float32))
    v = to_chunks(v.astype(jnp.float32))
    g = to_chunks(log_a[..., None].astype(jnp.float32))[..., 0]
    bt = to_chunks(beta[..., None].astype(jnp.float32))[..., 0]
    gc = jnp.cumsum(g, axis=-1)
    causal = jnp.tril(jnp.ones((CHUNK, CHUNK), bool))
    strict = jnp.tril(jnp.ones((CHUNK, CHUNK), bool), -1)
    decay = jnp.exp(jnp.where(causal, gc[..., :, None] - gc[..., None, :], -jnp.inf))
    kb = k * bt[..., None]
    low = jnp.where(strict, jnp.einsum('nbhcd,nbhed->nbhce', kb, k) * decay, 0.0)
    eye = jnp.eye(CHUNK, dtype=jnp.float32)
    t_inv = lax.linalg.triangular_solve(eye + low, jnp.broadcast_to(eye, low.shape), left_side=True, lower=True)
    u = t_inv @ (v * bt[..., None])
    w = t_inv @ (kb * jnp.exp(gc)[..., None])
    attn = jnp.einsum('nbhcd,nbhed->nbhce', q, k) * decay
    q_dec = q * jnp.exp(gc)[..., None]
    k_dec = k * jnp.exp(gc[..., -1:] - gc)[..., None]
    c_dec = jnp.exp(gc[..., -1])

    def step(s, xs):
        qd, at, ui, wi, kd, cd = xs
        v_new = ui - wi @ s
        o = qd @ s + at @ v_new
        s = s * cd[..., None, None] + jnp.einsum('bhcd,bhce->bhde', kd, v_new)
        return s, o

    s_fin, o = lax.scan(step, s0.astype(jnp.float32), (q_dec, attn, u, w, k_dec, c_dec))
    return from_chunks(o), s_fin

def retention_chunked(q, k, v, log_gamma, s0):
    dk = q.shape[-1]
    q = to_chunks(q.astype(jnp.float32))
    k = to_chunks(k.astype(jnp.float32)) * (dk ** -0.5)
    v = to_chunks(v.astype(jnp.float32))
    idx = jnp.arange(CHUNK, dtype=jnp.float32)
    lg = log_gamma.astype(jnp.float32)[:, None]
    causal = jnp.tril(jnp.ones((CHUNK, CHUNK), bool))
    dmat = jnp.exp(jnp.where(causal, (idx[:, None] - idx[None, :]) * lg[:, :, None], -jnp.inf))
    inner = (jnp.einsum('nbhcd,nbhed->nbhce', q, k) * dmat) @ v
    k_dec = jnp.exp((CHUNK - 1 - idx) * lg)
    kv = jnp.einsum('nbhcd,nbhce->nbhde', k * k_dec[..., None], v)
    c_dec = jnp.exp(CHUNK * lg)[:, :, None]

    def step(s, kv_c):
        return s * c_dec + kv_c, s

    s_fin, s_prev = lax.scan(step, s0.astype(jnp.float32), kv)
    cross = jnp.exp((idx + 1.0) * lg)
    o = inner + jnp.einsum('nbhcd,nbhde->nbhce', q, s_prev) * cross[..., None]
    return from_chunks(o), s_fin

def context_attention(q, k, v):
    b, l, h, d = q.shape
    qb = q.reshape(b, l // QBLOCK, QBLOCK, h, d).transpose(1, 0, 2, 3, 4)

    def block(qi):
        s = jnp.einsum('bqhd,blhd->bhql', qi, k).astype(jnp.float32) * (d ** -0.5)
        p = jax.nn.softmax(s, axis=-1).astype(v.dtype)
        return jnp.einsum('bhql,blhd->bqhd', p, v)

    o = lax.map(block, qb)
    return o.transpose(1, 0, 2, 3, 4).reshape(b, l, h, d)

def neighbourhood_attention(q, k, v, ck, cv, rpb):
    b, n, h, d = q.shape
    rows_n = n // GRID_W
    kh = min(WIN_ROWS, rows_n)
    qg = q.reshape(b, rows_n, GRID_W, h, d).transpose(1, 0, 2, 3, 4)
    kg = k.reshape(b, rows_n, GRID_W, h, d)
    vg = v.reshape(b, rows_n, GRID_W, h, d)
    cols = jnp.arange(GRID_W)
    c0 = jnp.clip(cols - WIN_COLS // 2, 0, GRID_W - WIN_COLS)
    col_in = (cols[None, :] >= c0[:, None]) & (cols[None, :] < c0[:, None] + WIN_COLS)
    col_idx = jnp.clip(cols[None, :] - cols[:, None], -(WIN_COLS - 1), WIN_COLS - 1) + WIN_COLS - 1
    rows = jnp.arange(rows_n)
    r0 = jnp.clip(rows - kh // 2, 0, rows_n - kh)
    scale = d ** -0.5

    def one_row(xs):
        q_r, r, r0_r = xs
        kb = lax.dynamic_slice_in_dim(kg, r0_r, kh, axis=1)
        vb = lax.dynamic_slice_in_dim(vg, r0_r, kh, axis=1)
        row_idx = r0_r + jnp.arange(kh) - r + WIN_ROWS - 1
        bias = rpb[:, row_idx[None, :, None], col_idx[:, None, :]].astype(jnp.float32)
        s_loc = jnp.einsum('bqhd,bikhd->bhqik', q_r, kb).astype(jnp.float32) * scale + bias
        s_loc = jnp.where(col_in[:, None, :], s_loc, -jnp.inf)
        s_ctx = jnp.einsum('bqhd,blhd->bhql', q_r, ck).astype(jnp.float32) * scale
        s = jnp.concatenate([s_loc.reshape(b, h, GRID_W, kh * GRID_W), s_ctx], axis=-1)
        p = jax.nn.softmax(s, axis=-1).astype(v.dtype)
        p_loc = p[..., :kh * GRID_W].reshape(b, h, GRID_W, kh, GRID_W)
        p_ctx = p[..., kh * GRID_W:]
        return jnp.einsum('bhqik,bikhd->bqhd', p_loc, vb) + jnp.einsum('bhql,blhd->bqhd', p_ctx, cv)

    o = lax.map(one_row, (qg, rows, r0))
    return o.transpose(1, 0, 2, 3, 4).reshape(b, n, h, d)

def token_mixer(h, p, cache):
    b, t, _ = h.shape
    latent = cache is not None
    split_at = [int(i) for i in np.cumsum(IN_SIZES)[:-1]]
    a_qkv, a_z, a_dec, a_beta, r_qkv, r_g, n_qkv, s_bcx = jnp.split(h @ p['w_in'], split_at, axis=-1)
    heads = lambda a: a.reshape(b, t, -1, HEAD_DIM)
    flip = lambda a: jnp.flip(a, axis=1)

    a_qkv = jax.nn.silu(depthwise_conv(a_qkv, p['gdn_conv_w']))
    aq, ak, av = jnp.split(a_qkv, 3, axis=-1)
    aq, ak, av = l2_normalize(heads(aq)), l2_normalize(heads(ak)), heads(av)
    log_a = -jnp.exp(p['gdn_a_log'].astype(jnp.float32)) * jax.nn.softplus(
        a_dec.reshape(b, t, 2, H_GDN).astype(jnp.float32) + p['gdn_dt_bias'].astype(jnp.float32))
    beta = jax.nn.sigmoid(a_beta.reshape(b, t, 2, H_GDN).astype(jnp.float32))
    s_gdn = cache[0] if latent else jnp.zeros((b, 2, H_GDN, HEAD_DIM, HEAD_DIM), jnp.float32)
    o_f, gdn_f = gated_delta_chunked(aq, ak, av, log_a[:, :, 0], beta[:, :, 0], s_gdn[:, 0])
    o_b, gdn_b = gated_delta_chunked(flip(aq), flip(ak), flip(av), flip(log_a[:, :, 1]), flip(beta[:, :, 1]), s_gdn[:, 1])
    o_gdn = rms_norm(o_f + flip(o_b), p['gdn_norm_w']) * jax.nn.silu(heads(a_z).astype(jnp.float32))

    rq, rk, rv = [heads(a) for a in jnp.split(r_qkv, 3, axis=-1)]
    if latent:
        rq, rk = axial_rope(rq), axial_rope(rk)
    log_g = jax.nn.log_sigmoid(p['ret_gamma_logit'].astype(jnp.float32))
    s_ret = cache[1] if latent else jnp.zeros((b, 2, H_RET, HEAD_DIM, HEAD_DIM), jnp.float32)
    ro_f, ret_f = retention_chunked(rq, rk, rv, log_g[0], s_ret[:, 0])
    ro_b, ret_b = retention_chunked(flip(rq), flip(rk), flip(rv), log_g[1], s_ret[:, 1])
    o_ret = head_group_norm(ro_f + flip(ro_b)) * jax.nn.silu(heads(r_g).astype(jnp.float32))

    nq, nk, nv = [heads(a) for a in jnp.split(n_qkv, 3, axis=-1)]
    nq = rms_norm(nq, p['nat_q_norm_w'])
    nk = rms_norm(nk, p['nat_k_norm_w'])
    if latent:
        o_nat = neighbourhood_attention(nq, nk, nv, cache[2], cache[3], p['nat_rpb'])
    else:
        o_nat = context_attention(nq, nk, nv)

    sb, sc, sx = jnp.split(s_bcx, 3, axis=-1)
    o_sc = sb * depthwise_conv(sc * sx, p['sc_conv_w'])

    mixed = jnp.concatenate([o_gdn.reshape(b, t, -1).astype(h.dtype), o_ret.reshape(b, t, -1).astype(h.dtype),
                             o_nat.reshape(b, t, -1).astype(h.dtype), o_sc], axis=-1)
    out = mixed @ p['w_out']
    if latent:
        return out, None
    return out, (jnp.stack([gdn_f, gdn_b], axis=1), jnp.stack([ret_f, ret_b], axis=1), nk, nv)

def hier_moe(h, p):
    b, t, d = h.shape
    x = h.reshape(b * t, d)
    gl = (x @ p['router_group_w'] + p['router_group_b']).astype(jnp.float32)
    gp = jax.nn.softmax(gl, axis=-1)
    gw, gsel = lax.top_k(gp, 1)
    el = (x @ p['router_expert_w'] + p['router_expert_b']).astype(jnp.float32).reshape(-1, N_GROUPS, EXPERTS_PER_GROUP)
    el = jnp.take_along_axis(el, gsel[:, :, None], axis=1)[:, 0]
    tw, ti = lax.top_k(jax.nn.softmax(el, axis=-1), TOP_K)
    tw = tw / jnp.sum(tw, axis=-1, keepdims=True)
    eid = gsel * EXPERTS_PER_GROUP + ti
    combine = jnp.sum(jax.nn.one_hot(eid, N_EXPERTS, dtype=jnp.float32) * (gw * tw)[..., None], axis=1)
    hg = jnp.einsum('nd,edf->nef', x, p['moe_w_gate'])
    hu = jnp.einsum('nd,edf->nef', x, p['moe_w_up'])
    act = jax.nn.silu(hg) * hu * combine.astype(x.dtype)[..., None]
    y = jnp.einsum('nef,efd->nd', act, p['moe_w_down'])
    return y.reshape(b, t, d)

def trunk_layer(x, cond, p, cache):
    ada = jax.nn.silu(cond) @ p['ada_w'] + p['ada_b']
    sh_m, sc_m, g_m, sh_f, sc_f, g_f = jnp.split(ada[:, None, :], 6, axis=-1)
    hm = rms_norm(x, p['norm_mix_w']) * (1.0 + sc_m) + sh_m
    m, st = token_mixer(hm, p, cache)
    x = x + g_m * m
    hf = rms_norm(x, p['norm_ffn_w']) * (1.0 + sc_f) + sh_f
    x = x + g_f * hier_moe(hf, p)
    return x, st

def setup_inputs(seed: int = 0) -> dict:
    key = jax.random.key(seed)
    ks = iter(jax.random.split(key, 48))
    f32 = jnp.float32
    nrm = lambda shape, s: jax.random.normal(next(ks), shape, f32) * s
    x_prompt = nrm((BATCH, SEQ, D_MODEL), 1.0)
    x_sample = nrm((DEC_BATCH, DEC_SEQ, D_MODEL), 1.0)
    state_gdn = nrm((DEC_BATCH, DEPTH, 2, H_GDN, HEAD_DIM, HEAD_DIM), 0.3)
    state_ret = nrm((DEC_BATCH, DEPTH, 2, H_RET, HEAD_DIM, HEAD_DIM), 1.0)
    cache_nat_k = nrm((DEC_BATCH, DEPTH, PAST_LEN, H_NAT, HEAD_DIM), 1.0)
    cache_nat_v = nrm((DEC_BATCH, DEPTH, PAST_LEN, H_NAT, HEAD_DIM), 1.0)
    c = nrm((DEC_BATCH, D_MODEL), 1.0)
    c_ctx = nrm((D_MODEL,), 1.0)
    ada_w = nrm((DEPTH, D_MODEL, 6 * D_MODEL), 0.5 * D_MODEL ** -0.5)
    ada_b = nrm((DEPTH, 6 * D_MODEL), 0.01)
    norm_mix_w = 1.0 + nrm((DEPTH, D_MODEL), 0.02)
    norm_ffn_w = 1.0 + nrm((DEPTH, D_MODEL), 0.02)
    w_in = nrm((DEPTH, D_MODEL, IN_WIDTH), D_MODEL ** -0.5)
    gdn_conv_w = nrm((DEPTH, GDN_CONV, 3 * W_GROUP), GDN_CONV ** -0.5)
    gdn_a_log = jnp.log(jax.random.uniform(next(ks), (DEPTH, 2, H_GDN), f32, 1.0, 16.0))
    dt = jnp.exp(jax.random.uniform(next(ks), (DEPTH, 2, H_GDN), f32, float(np.log(1e-3)), float(np.log(1e-1))))
    gdn_dt_bias = dt + jnp.log(-jnp.expm1(-dt))
    gdn_norm_w = 1.0 + nrm((DEPTH, HEAD_DIM), 0.02)
    ret_logit_base = jnp.log(jnp.power(2.0, 5.0 + jnp.arange(H_RET, dtype=f32)) - 1.0)
    ret_gamma_logit = ret_logit_base + nrm((DEPTH, 2, H_RET), 0.1)
    nat_q_norm_w = 1.0 + nrm((DEPTH, HEAD_DIM), 0.02)
    nat_k_norm_w = 1.0 + nrm((DEPTH, HEAD_DIM), 0.02)
    nat_rpb = nrm((DEPTH, H_NAT, 2 * WIN_ROWS - 1, 2 * WIN_COLS - 1), 0.1)
    sc_conv_w = nrm((DEPTH, SC_CONV, SC_WIDTH), SC_CONV ** -0.5)
    w_out = nrm((DEPTH, D_MODEL, D_MODEL), D_MODEL ** -0.5)
    router_group_w = nrm((DEPTH, D_MODEL, N_GROUPS), D_MODEL ** -0.5)
    router_group_b = nrm((DEPTH, N_GROUPS), 0.01)
    router_expert_w = nrm((DEPTH, D_MODEL, N_EXPERTS), D_MODEL ** -0.5)
    router_expert_b = nrm((DEPTH, N_EXPERTS), 0.01)
    moe_w_gate = nrm((DEPTH, N_EXPERTS, D_MODEL, EXPERT_FF), D_MODEL ** -0.5)
    moe_w_up = nrm((DEPTH, N_EXPERTS, D_MODEL, EXPERT_FF), D_MODEL ** -0.5)
    moe_w_down = nrm((DEPTH, N_EXPERTS, EXPERT_FF, D_MODEL), EXPERT_FF ** -0.5)
    return {'x_prompt': x_prompt, 'x_sample': x_sample, 'state_gdn': state_gdn, 'state_ret': state_ret,
            'cache_nat_k': cache_nat_k, 'cache_nat_v': cache_nat_v, 'c': c, 'c_ctx': c_ctx,
            'ada_w': ada_w, 'ada_b': ada_b, 'norm_mix_w': norm_mix_w, 'norm_ffn_w': norm_ffn_w, 'w_in': w_in,
            'gdn_conv_w': gdn_conv_w, 'gdn_a_log': gdn_a_log, 'gdn_dt_bias': gdn_dt_bias, 'gdn_norm_w': gdn_norm_w,
            'ret_gamma_logit': ret_gamma_logit, 'nat_q_norm_w': nat_q_norm_w, 'nat_k_norm_w': nat_k_norm_w,
            'nat_rpb': nat_rpb, 'sc_conv_w': sc_conv_w, 'w_out': w_out, 'router_group_w': router_group_w,
            'router_group_b': router_group_b, 'router_expert_w': router_expert_w, 'router_expert_b': router_expert_b,
            'moe_w_gate': moe_w_gate, 'moe_w_up': moe_w_up, 'moe_w_down': moe_w_down}

def reference(x_prompt, x_sample, state_gdn, state_ret, cache_nat_k, cache_nat_v, c, c_ctx,
              ada_w, ada_b, norm_mix_w, norm_ffn_w, w_in, gdn_conv_w, gdn_a_log, gdn_dt_bias, gdn_norm_w,
              ret_gamma_logit, nat_q_norm_w, nat_k_norm_w, nat_rpb, sc_conv_w, w_out,
              router_group_w, router_group_b, router_expert_w, router_expert_b,
              moe_w_gate, moe_w_up, moe_w_down):
    y_p = x_prompt
    y_s = x_sample
    cond_ctx = c_ctx[None, :]
    gdn_list, ret_list, k_list, v_list = [], [], [], []
    for l in range(DEPTH):
        p = {'ada_w': ada_w[l], 'ada_b': ada_b[l], 'norm_mix_w': norm_mix_w[l], 'norm_ffn_w': norm_ffn_w[l],
             'w_in': w_in[l], 'gdn_conv_w': gdn_conv_w[l], 'gdn_a_log': gdn_a_log[l], 'gdn_dt_bias': gdn_dt_bias[l],
             'gdn_norm_w': gdn_norm_w[l], 'ret_gamma_logit': ret_gamma_logit[l], 'nat_q_norm_w': nat_q_norm_w[l],
             'nat_k_norm_w': nat_k_norm_w[l], 'nat_rpb': nat_rpb[l], 'sc_conv_w': sc_conv_w[l], 'w_out': w_out[l],
             'router_group_w': router_group_w[l], 'router_group_b': router_group_b[l],
             'router_expert_w': router_expert_w[l], 'router_expert_b': router_expert_b[l],
             'moe_w_gate': moe_w_gate[l], 'moe_w_up': moe_w_up[l], 'moe_w_down': moe_w_down[l]}
        y_p, (s_g, s_r, n_k, n_v) = trunk_layer(y_p, cond_ctx, p, None)
        gdn_list.append(s_g)
        ret_list.append(s_r)
        k_list.append(n_k)
        v_list.append(n_v)
        cache_l = (state_gdn[:, l], state_ret[:, l], cache_nat_k[:, l], cache_nat_v[:, l])
        y_s, _ = trunk_layer(y_s, c, p, cache_l)
    new_state_gdn = jnp.stack(gdn_list, axis=1)
    new_state_ret = jnp.stack(ret_list, axis=1)
    new_cache_nat_k = jnp.stack(k_list, axis=1)
    new_cache_nat_v = jnp.stack(v_list, axis=1)
    return (y_p, y_s, new_state_gdn, new_state_ret, new_cache_nat_k, new_cache_nat_v)


_drawn_inputs = setup_inputs


def setup_inputs(seed=0):
    import zlib

    import numpy as np

    out = dict(_drawn_inputs(seed))
    spreads = {}
    factors = {'norm_ffn_w': 2.953,
     'gdn_norm_w': 5.645,
     'nat_q_norm_w': 8.0,
     'nat_k_norm_w': 2.946,
     'nat_rpb': 8.0,
     'router_group_b': 7.421,
     'router_expert_b': 4.281}
    for name, (base, spread) in spreads.items():
        noise = np.random.default_rng([zlib.crc32(name.encode()), seed]).standard_normal(out[name].shape)
        drawn = base * np.exp(spread * noise) if base else spread * noise
        out[name] = __import__('jax').numpy.asarray(drawn.astype(out[name].dtype))
    for name, factor in factors.items():
        out[name] = (out[name] * factor).astype(out[name].dtype)
    return out
```

```python
import math
from contextlib import ExitStack

import numpy as np

import concourse.bass as bass
from concourse import mybir

F32 = mybir.dt.float32
ACT = mybir.ActivationFunctionType
ALU = mybir.AluOpType
AX = mybir.AxisListType

P = 128
D_MODEL, DEPTH = 1024, 2
KT = D_MODEL // P
NS = 2
TOK = NS * P
HEADS, HD = 4, 64
GRID_W, WIN_ROWS, WIN_COLS = 64, 8, 16
N_GROUPS, PER_GROUP, FF = 4, 8, 256
N_EXPERTS = N_GROUPS * PER_GROUP
ROUTER = N_GROUPS + N_EXPERTS
EPS = 1e-6
BIG = 1e30
QK_SCALE = HD ** -0.5
LEVELS = 7

RING, SLOT = 4, 6144
ADA_SLOTS, IN_SLOTS, OUT_SLOTS = 8, 5, 3
HEAD_SLOTS = ADA_SLOTS + IN_SLOTS + OUT_SLOTS
TOKCOLS = 16 + 2 * HEADS * HD
OUT_TILES = (3, 3, 2)
assert HEAD_SLOTS % RING == 0 and N_EXPERTS % RING == 0


def layout(*parts):
    at, out = 0, {}
    for name, width in parts:
        out[name] = slice(at, at + width)
        at += width
    return out, at


CONST, CONST_W = layout(
    ("ident", P), ("zeros", P), ("ones", P), ("blockones", P), ("upto_f", P), ("upto_b", P), ("negupto_f", P), ("negupto_b", P),
    ("after_f", P), ("after_b", P), ("rot", P), ("cos", P), ("sin", P), ("lag_f", P), ("lag_b", P),
    ("cross_f", P), ("cross_b", P), ("colmask", GRID_W), ("idx", 2), ("prio", PER_GROUP),
    ("levels", 2 * LEVELS * P))
PARAM, PARAM_W = layout(
    ("norm_mix", KT), ("norm_ffn", KT), ("ada_b", 48), ("conv_gdn", 18), ("conv_sc", 6), ("gdn_norm", 1),
    ("q_norm", 1), ("k_norm", 1), ("dt_bias", 8), ("a_log", 8), ("gamma_cols", 8), ("gamma_rows", 4),
    ("router_b", ROUTER), ("router_w", KT * ROUTER), ("nat_bias", HEADS * 2 * GRID_W),
    ("ck", HEADS * P), ("cv", HEADS * P), ("s_gdn", 4 * P), ("s_ret", 4 * P))
ARENA, ARENA_W = layout(
    ("raw", 6 * 2 * 130), ("qkv", 6 * TOK), ("zg", 2 * TOK), ("gpad", 8 * 256), ("vtok", 2 * 256), ("zr", 2 * TOK),
    ("natqk", 4 * TOK), ("retqk", 4 * TOK), ("sb", 2 * TOK), ("sx", 2 * TOK), ("ub", 2 * 2 * 130),
    ("vp", 2 * 2 * 512), ("norm", 2048), ("npad", 4 * 256), ("rpad", 4 * 256))
GROUP_W = 8 * 512

PER = dict(
    ada_mm=8, ada_dve=1, norm_sq=2, norm_mm=2, norm_rs=2, h_scaled=2, h_act=2, h_dve=2,
    proj_mm=15, proj_act=10, proj_dve=5, conv_dve=1, silu_act=1, sc_dve=1,
    sp_in=1, sp_act=1, gates_dve=1,
    qk_sq=1, qk_mm=1, qk_rs=1, qk_dve=1, pad_act=1, pad_pool=1, rope_mm=1, rope_dve=1, rpad_act=1, rpad_pool=1,
    zeroed=1, param_dma=16, layer_done=1,
    nat_mm=1, nat_max=1, nat_exp=1, nat_p=1, nat_tr=1, nat_pt=1, nat_o=1, nat_out=1,
    ret_exp=1, ret_mm=1, ret_a=1, ret_kt=1, ret_kd=1, ret_o=1, ret_sf=1, ret_st=1, ret_og=1,
    ret_mean=1, ret_sq=1, ret_var=1, ret_rs=1, ret_out=1,
    vnp_zero=1, gr_mm=2, gr_min=4, gr_exp=4, gr_dec=2, gcol_mm=2, gcol_exp=2, vt_mm=2, vt_act=2,
    ks_mm=2, z_dve=2, inv_c=28, inv_dmm=28, inv_dev=24, inv_umm=24, inv_upd=28,
    vn_mm=4, vn_dve=4, qd_g=1, qd_mm=1, qd_exp=1, qd_dve=1, kd_dve=1, gs_mm=1, gs_st=1, go_mm=2, go_dve=2,
    gn_sq=1, gn_mm=1, gn_rs=1, gn_out=1,
    out_mm=3, res_dve=1, route_mm=1, route_exp1=1, route_d1=1, route_d2=1, route_exp2=1, route_dve=1,
    cb_mm=16, cb_act=8, cb_dve=8, gu_mm=32, silu=32, prod=32, act_dve=32, down_mm=32,
)


def build_trunk(nc, src, dst):
    with ExitStack() as ctx:
        def sb(name, *shape):
            return ctx.enter_context(nc.sbuf_tensor(name, list(shape), F32))

        ring = sb("ring", P, RING, SLOT)
        xT = sb("xT", P, KT, TOK)
        hT = sb("hT", P, KT, TOK)
        const = sb("const", P, CONST_W)
        param = sb("param", P, PARAM_W)
        arena = sb("arena", P, ARENA_W)
        condT = sb("condT", P, KT, NS)
        adaT = sb("adaT", P, 48, NS)
        scale1 = sb("scale1", P, 2, KT, NS)
        rstd = sb("rstd", P, TOK)
        gin = sb("gin", P, 2, 16)
        spx = sb("spx", P, 28)
        spa = sb("spa", P, 28)
        spe = sb("spe", P, 28)
        beta = sb("beta", P, 2, 8)
        nega = sb("nega", P, 8)
        gdec = sb("gdec", P, 2, 8)
        lg = sb("lg", P, 12)
        kdc = sb("kdc", P, 8)
        egc = sb("egc", P, 16)
        natm = sb("natm", P, 12)
        natsum = sb("natsum", P, 12)
        state = sb("state", P, 2, 2, HD)
        state_flat = state[:].rearrange("p d j n -> p (d j n)")
        rt = state_flat[:, 0:2 * ROUTER].rearrange("p (s n) -> p s n", s=2)
        rs_ = state_flat[:, 2 * ROUTER:2 * ROUTER + 120]
        comb = sb("comb", P, 2, N_EXPERTS)
        ps = ctx.enter_context(nc.psum_tensor("ps", [P, 8, 512], F32))

        sem = {name: ctx.enter_context(nc.semaphore(name)) for name in PER}
        slot_in = [ctx.enter_context(nc.semaphore(f"slot_in{j}")) for j in range(RING)]
        const_in = ctx.enter_context(nc.semaphore("const_in"))
        cond_e = ctx.enter_context(nc.semaphore("cond_silu"))
        state_out = ctx.enter_context(nc.semaphore("state_out"))
        kv_out = ctx.enter_context(nc.semaphore("kv_out"))
        y_out = ctx.enter_context(nc.semaphore("y_out"))
        chain_dve = ctx.enter_context(nc.semaphore("chain_dve"))
        chain_act = ctx.enter_context(nc.semaphore("chain_act"))

        def C(name):
            return const[:, CONST[name]]

        def Q(name):
            return param[:, PARAM[name]]

        def A(name):
            return arena[:, ARENA[name]]

        def bc(ap, *shape):
            return ap.broadcast_to([P, *shape])

        raw = A("raw").rearrange("p (m s t) -> p m s t", m=6, s=2)
        qkv = A("qkv").rearrange("p (m t) -> p m t", m=6)
        zg, zr = A("zg"), A("zr")
        og = A("zr").rearrange("p (j s c) -> p j s c", j=2, s=2)
        gpad = A("gpad").rearrange("p (t s i c) -> p t s i c", t=4, s=2, i=2)
        vtok = A("vtok").rearrange("p (s n) -> p s n", s=2)
        natqk = A("natqk").rearrange("p (m t) -> p m t", m=4)
        retqk = A("retqk").rearrange("p (m t) -> p m t", m=4)
        sbT, sxT = A("sb").rearrange("p (m s t) -> p m s t", m=2, s=2), A("sx").rearrange("p (m s t) -> p m s t", m=2, s=2)
        ub = A("ub").rearrange("p (m s t) -> p m s t", m=2, s=2)
        vp = A("vp").rearrange("p (s r j n) -> p s r j n", s=2, r=2, j=2)
        norm = A("norm")
        npad = A("npad").rearrange("p (j s i c) -> p j s i c", j=2, s=2, i=2)
        rpad = A("rpad").rearrange("p (j s i c) -> p j s i c", j=2, s=2, i=2)
        levels = C("levels").rearrange("p (d b c) -> p d b c", d=2, b=LEVELS)
        ident = C("ident")
        g0 = ARENA["natqk"].start

        def group(g, part):
            at = g0 + g * GROUP_W + part * 512
            return arena[:, at:at + 512].rearrange("p (h c) -> p h c", h=HEADS)

        tail = g0 + 2 * GROUP_W
        z = arena[:, tail:tail + 512].rearrange("p (g n) -> p g n", g=2)
        kdg = arena[:, tail + 512:tail + 1024].rearrange("p (g n) -> p g n", g=2)
        qdec = arena[:, tail + 1024:tail + 1536].rearrange("p (g j c) -> p g j c", g=2, j=2)
        assert tail + 1536 <= ARENA_W
        cb = arena[:, 0:N_EXPERTS * TOK].rearrange("p (e t) -> p e t", e=N_EXPERTS)
        moe0 = N_EXPERTS * TOK
        sg = arena[:, moe0:moe0 + 1024].rearrange("p (b f t) -> p b f t", b=2, f=2)
        gated = arena[:, moe0 + 1024:moe0 + 2048].rearrange("p (b f t) -> p b f t", b=2, f=2)
        nat_s = norm[:, 0:1536]
        nat_t = A("raw")[:, 0:1536]
        ef = arena[:, ARENA["sb"].start:ARENA["sb"].start + 512].rearrange("p (h c) -> p h c", h=HEADS)
        eb = arena[:, ARENA["sb"].start + 512:ARENA["sb"].start + 1024].rearrange("p (h c) -> p h c", h=HEADS)
        qx = arena[:, ARENA["ub"].start:ARENA["ub"].start + 512].rearrange("p (d j c) -> p d j c", d=2, j=2)
        ret_a = norm[:, 0:1024].rearrange("p (s h c) -> p s h c", s=2, h=HEADS)
        ret_kd = norm[:, 1024:1536].rearrange("p (d n) -> p d n", d=2)
        qx_in = norm[:, 1536:2048].rearrange("p (d j c) -> p d j c", d=2, j=2)
        upto = [C("upto_f"), C("upto_b")]
        negupto = [C("negupto_f"), C("negupto_b")]
        after = [C("after_f"), C("after_b")]
        s_gdn = Q("s_gdn").rearrange("p (d j c) -> p d j c", d=2, j=2)
        s_ret = Q("s_ret").rearrange("p (d j c) -> p d j c", d=2, j=2)
        ck = Q("ck").rearrange("p (h c) -> p h c", h=HEADS)
        cv = Q("cv").rearrange("p (h c) -> p h c", h=HEADS)

        def bank(b, width=512):
            return ps[:, b, 0:width]

        def heads(ap):
            return ap.rearrange("p (h c) -> p h c", h=HEADS)

        def proj_bank(u):
            return (u + 2) % 8

        block = ctx.enter_context(nc.Block())

        def rise(layer, name, n):
            return layer * PER[name] + n

        class Links:

            def __init__(self):
                self.count = 0

            def next(self):
                self.count += 1
                return self.count

            def restart(self):
                self.count = 0

        @block.sync
        def _(sp):
            sp.dma_start(condT[:], src["condT"]).then_inc(const_in, 16)
            sp.dma_start(const[:], src["const"]).then_inc(const_in, 16)
            sp.dma_start(xT[:], src["xT"]).then_inc(const_in, 16)

            def ring_in(n, what):
                rows, width = what
                sp.dma_start(ring[:, n % RING, 0:width], rows).then_inc(slot_in[n % RING], 16)

            def head_slot(l, i):
                if i < ADA_SLOTS:
                    return src["ada_w"][l, i], SLOT
                i -= ADA_SLOTS
                if i == 1:
                    return src["w_tok"][l], KT * TOKCOLS
                if i < IN_SLOTS:
                    return src["w_feat"][l, i - (i > 1)], SLOT
                i -= IN_SLOTS
                at = KT * P * sum(OUT_TILES[:i])
                width = KT * P * OUT_TILES[i]
                return src["w_out"][l][:, at:at + width], width

            def slot_free(l, i):
                if i < ADA_SLOTS:
                    sp.wait_ge(sem["ada_mm"], l * PER["ada_mm"] + i + 1)
                elif i < ADA_SLOTS + IN_SLOTS:
                    sp.wait_ge(sem["proj_mm"], l * PER["proj_mm"] + (3, 6, 9, 12, 15)[i - ADA_SLOTS])
                elif i < HEAD_SLOTS:
                    sp.wait_ge(sem["out_mm"], l * PER["out_mm"] + i - ADA_SLOTS - IN_SLOTS + 1)
                else:
                    sp.wait_ge(sem["down_mm"], l * PER["down_mm"] + i - HEAD_SLOTS + 1)

            for l in range(DEPTH):
                for i in range(HEAD_SLOTS):
                    if i >= RING:
                        slot_free(l, i - RING)
                    elif l > 0:
                        slot_free(l - 1, HEAD_SLOTS + N_EXPERTS + i - RING)
                    ring_in(i, head_slot(l, i))
                    if i == RING - 1:
                        if l > 0:
                            sp.wait_ge(sem["layer_done"], l + 1)
                        sp.dma_start(param[:], src["param"][l]).then_inc(sem["param_dma"], 16)
                for e in range(RING):
                    slot_free(l, HEAD_SLOTS - RING + e)
                    ring_in(e, (src["moe"][l, e], SLOT))
                with sp.Fori(1, N_EXPERTS // RING) as turn:
                    e4 = turn * RING
                    for j in range(RING):
                        sp.wait_ge(sem["down_mm"], e4 + (l * PER["down_mm"] + j - RING + 1))
                        rows = src["moe"][l, bass.ds(e4 + j, 1)].rearrange("o p n -> (o p) n")
                        ring_in(j, (rows, SLOT))
            sp.wait_ge(sem["layer_done"], DEPTH + 1)
            sp.dma_start(dst["yT"], xT[:]).then_inc(y_out, 16)
            sp.wait_ge(y_out, 16)

        @block.tensor
        def _(pe):
            mm = nc.tensor.matmul

            def in_slot(l, i):
                pe.wait_ge(slot_in[i % RING], l * (16 * (HEAD_SLOTS + N_EXPERTS) // RING) + 16 * (i // RING + 1))

            with pe.Fori(0, DEPTH) as l:
                pe.wait_ge(cond_e, 1)
                pe.wait_ge(sem["layer_done"], rise(l, "layer_done", 1))
                for i in range(ADA_SLOTS):
                    in_slot(l, i)
                    for m in range(6):
                        for k in range(KT):
                            last = mm(ps[:, 0, (6 * i + m) * 2:(6 * i + m) * 2 + 2],
                                      ring[:, i % RING, k * 768 + m * P:k * 768 + (m + 1) * P],
                                      condT[:, k, :], start=k == 0, stop=k == KT - 1)
                    last.then_inc(sem["ada_mm"], 1)

                def norm_sum(n):
                    pe.wait_ge(sem["norm_sq"], rise(l, "norm_sq", n))
                    sq = norm.rearrange("p (k t) -> p k t", k=KT)
                    for k in range(KT):
                        last = mm(bank(1, TOK), C("ones"), sq[:, k, :], start=k == 0, stop=k == KT - 1)
                    last.then_inc(sem["norm_mm"], 1)

                norm_sum(1)
                pe.wait_ge(sem["h_act"], rise(l, "h_act", 1))
                pe.wait_ge(sem["h_dve"], rise(l, "h_dve", 1))
                free_of = {8: ("proj_act", 1), 9: ("proj_act", 2), 10: ("proj_act", 3), 11: ("proj_dve", 1),
                           12: ("proj_dve", 2), 13: ("proj_dve", 3), 14: ("proj_act", 4)}
                u = 0
                for i in range(IN_SLOTS):
                    in_slot(l, ADA_SLOTS + i)
                    slot = ring[:, (ADA_SLOTS + i) % RING, :]
                    if i == 1:
                        for s in range(NS):
                            for k in range(KT):
                                last = mm(bank(proj_bank(3 + s)), hT[:, k, s * P:(s + 1) * P],
                                          slot[:, k * TOKCOLS + 16:(k + 1) * TOKCOLS], start=k == 0, stop=k == KT - 1)
                            last.then_inc(sem["proj_mm"], 1)
                        for s in range(NS):
                            for k in range(KT):
                                last = mm(ps[:, proj_bank(5), 16 * s:16 * s + 16], hT[:, k, s * P:(s + 1) * P],
                                          slot[:, k * TOKCOLS:k * TOKCOLS + 16], start=k == 0, stop=k == KT - 1)
                        last.then_inc(sem["proj_mm"], 1)
                        u += 3
                        continue
                    for pair in range(3):
                        if u in free_of:
                            name, n = free_of[u]
                            pe.wait_ge(sem[name], rise(l, name, n))
                        for m in range(2):
                            for k in range(KT):
                                at = k * 768 + (2 * pair + m) * P
                                last = mm(ps[:, proj_bank(u), m * TOK:(m + 1) * TOK], slot[:, at:at + P],
                                          hT[:, k, :], start=k == 0, stop=k == KT - 1)
                        last.then_inc(sem["proj_mm"], 1)
                        u += 1
                pe.wait_ge(sem["proj_act"], rise(l, "proj_act", 10))
                pe.wait_ge(sem["proj_dve"], rise(l, "proj_dve", 5))
                pe.wait_ge(sem["qk_sq"], rise(l, "qk_sq", 1))
                for b in range(4):
                    last = mm(bank(b), C("blockones"), norm[:, b * 512:(b + 1) * 512], start=True, stop=True)
                last.then_inc(sem["qk_mm"], 1)
                mm(bank(4), C("rot"), retqk[:, :, P:TOK], start=True, stop=True).then_inc(sem["rope_mm"], 1)

                pe.wait_ge(sem["pad_act"], rise(l, "pad_act", 1))
                pe.wait_ge(sem["pad_pool"], rise(l, "pad_pool", 1))
                pe.wait_ge(sem["qk_dve"], rise(l, "qk_dve", 1))
                for s in range(NS):
                    for j in range(2):
                        last = mm(ps[:, s, j * 256:(j + 1) * 256], natqk[:, j, s * P:(s + 1) * P],
                                  npad[:, j, s].rearrange("p i c -> p (i c)"), start=True, stop=True)
                for j in range(2):
                    last = mm(ps[:, 2, j * 256:(j + 1) * 256], natqk[:, j, P:TOK],
                              Q("ck")[:, j * 256:(j + 1) * 256], start=True, stop=True)
                last.then_inc(sem["nat_mm"], 1)
                pe.wait_ge(sem["rpad_act"], rise(l, "rpad_act", 1))
                pe.wait_ge(sem["rpad_pool"], rise(l, "rpad_pool", 1))
                for s in range(NS):
                    for j in range(2):
                        last = mm(ps[:, 6 + s, j * 256:(j + 1) * 256], retqk[:, 2 + j, s * P:(s + 1) * P],
                                  rpad[:, j, s].rearrange("p i c -> p (i c)"), start=True, stop=True)
                last.then_inc(sem["ret_mm"], 1)
                for j in range(2):
                    last = nc.tensor.transpose(ps[:, 5, j * P:(j + 1) * P], retqk[:, 2 + j, 0:P], ident)
                last.then_inc(sem["ret_kt"], 1)
                pe.wait_ge(sem["nat_p"], rise(l, "nat_p", 1))
                for b in range(3):
                    for h in range(HEADS):
                        last = nc.tensor.transpose(ps[:, b, h * P:(h + 1) * P],
                                                   nat_s[:, (b * HEADS + h) * P:(b * HEADS + h + 1) * P], ident)
                last.then_inc(sem["nat_tr"], 1)
                pe.wait_ge(sem["nat_pt"], rise(l, "nat_pt", 1))
                for j in range(2):
                    for s in range(NS):
                        parts = [(vp[:, s, 1, j, i * P:(i + 1) * P], nat_t[:, (s * HEADS + 2 * j + i) * P:(s * HEADS + 2 * j + i + 1) * P])
                                 for i in range(2)]
                        if s == 1:
                            parts += [(cv[:, 2 * j + i, :], nat_t[:, (2 * HEADS + 2 * j + i) * P:(2 * HEADS + 2 * j + i + 1) * P])
                                      for i in range(2)]
                        for n, (v, p) in enumerate(parts):
                            last = mm(ps[:, 3, j * 256 + s * P:j * 256 + (s + 1) * P], v, p,
                                      start=n == 0, stop=n == len(parts) - 1)
                last.then_inc(sem["nat_o"], 1)
                pe.wait_ge(sem["ret_a"], rise(l, "ret_a", 1))
                for j in range(2):
                    for s in range(NS):
                        parts = [(vp[:, s, 0, j, i * P:(i + 1) * P], ret_a[:, s, 2 * j + i, :]) for i in range(2)]
                        if s == 1:
                            parts += [(s_ret[:, d, j, :], qx[:, d, j, :]) for d in range(2)]
                        for n, (v, p) in enumerate(parts):
                            last = mm(ps[:, 4, j * 256 + s * P:j * 256 + (s + 1) * P], v, p,
                                      start=n == 0, stop=n == len(parts) - 1)
                last.then_inc(sem["ret_o"], 1)
                pe.wait_ge(sem["ret_kd"], rise(l, "ret_kd", 1))
                for d in range(2):
                    for j in range(2):
                        last = mm(ps[:, d, j * 256:(j + 1) * 256], ret_kd[:, d, j * P:(j + 1) * P],
                                  vp[:, 0, 0, j, :], start=True, stop=True)
                last.then_inc(sem["ret_sf"], 1)
                pe.wait_ge(sem["ret_og"], rise(l, "ret_og", 1))
                mm(bank(2), C("blockones"), ef.rearrange("p h c -> p (h c)"), start=True, stop=True).then_inc(sem["ret_mean"], 1)
                pe.wait_ge(sem["ret_sq"], rise(l, "ret_sq", 1))
                pe.wait_ge(sem["nat_out"], rise(l, "nat_out", 1))
                mm(bank(3), C("blockones"), eb.rearrange("p h c -> p (h c)"), start=True, stop=True).then_inc(sem["ret_var"], 1)
                pe.wait_ge(sem["ret_out"], rise(l, "ret_out", 1))
                pe.wait_ge(sem["ret_st"], rise(l, "ret_st", 1))

                for s in range(NS):
                    tk = slice(s * P, (s + 1) * P)
                    if s == 1:
                        pe.wait_ge(sem["go_dve"], rise(l, "go_dve", 1))
                        pe.wait_ge(sem["gs_st"], rise(l, "gs_st", 1))
                    for d in range(2):
                        for h in range(HEADS):
                            gcol = gdec[:, s, d * 4 + h:d * 4 + h + 1]
                            mm(ps[:, 2 + d, h * P:(h + 1) * P], bc(gcol, P), upto[d], start=True, stop=False)
                            mm(ps[:, 2 + d, h * P:(h + 1) * P], negupto[d], bc(gcol, P), start=False, stop=True)
                        for h in range(HEADS):
                            bcol = beta[:, s, d * 4 + h:d * 4 + h + 1]
                            last = mm(ps[:, 4 + d, h * P:(h + 1) * P], bc(bcol, P), ident, start=True, stop=True)
                    for j in range(2):
                        last = mm(bank(j), qkv[:, 2 + j, tk], gpad[:, j::2, s, :, :].rearrange("p t i c -> p t (i c)"),
                                  start=True, stop=True)
                    last.then_inc(sem["gr_mm"], 1)
                    for d in range(2):
                        mm(ps[:, 6, d * 4:d * 4 + 4], upto[d], gdec[:, s, d * 4:d * 4 + 4], start=True, stop=True)
                        last = mm(ps[:, 6, 8 + d * 4:12 + d * 4], after[d], gdec[:, s, d * 4:d * 4 + 4], start=True, stop=True)
                    last.then_inc(sem["gcol_mm"], 1)
                    for j in range(2):
                        last = nc.tensor.transpose(ps[:, 7, j * P:(j + 1) * P], qkv[:, 4 + j, tk], ident)
                    last.then_inc(sem["vt_mm"], 1)
                    pe.wait_ge(sem["gcol_exp"], rise(l, "gcol_exp", s + 1))
                    if s == 0:
                        for j in range(2):
                            last = nc.tensor.transpose(ps[:, 7, (2 + j) * P:(3 + j) * P], qkv[:, 2 + j, tk], ident)
                        last.then_inc(sem["ks_mm"], 1)
                    else:
                        for d in range(2):
                            for j in range(2):
                                last = mm(ps[:, 6, d * 256 + j * P:d * 256 + (j + 1) * P], qkv[:, 2 + j, tk],
                                          s_gdn[:, d, j, :], start=True, stop=True)
                        last.then_inc(sem["ks_mm"], 1)
                        pe.wait_ge(sem["vt_act"], rise(l, "vt_act", 2))
                        pe.wait_ge(sem["qd_g"], rise(l, "qd_g", 1))
                        for d in range(2):
                            for j in range(2):
                                last = mm(ps[:, 7, (2 * d + j) * P:(2 * d + j + 1) * P], qdec[:, d, j, :], upto[d], start=True, stop=True)
                        last.then_inc(sem["qd_mm"], 1)
                    for b in range(LEVELS):
                        for g in range(2):
                            n = (s * LEVELS + b) * 2 + g + 1
                            m = (s * (LEVELS - 1) + b - 1) * 2 + g + 1
                            pe.wait_ge(sem["inv_c"], rise(l, "inv_c", n))
                            name = "inv_upd" if b else "gr_dec"
                            pe.wait_ge(sem[name], rise(l, name, n - 2 if b else s + 1))
                            for h in range(HEADS):
                                last = mm(ps[:, 2 + g, h * P:(h + 1) * P], group(g, 6)[:, h, :],
                                          group(g, 3)[:, h, :] if b else ident, start=True, stop=True)
                            last.then_inc(sem["inv_dmm"], 1)
                        if b == 0:
                            continue
                        for g in range(2):
                            m = (s * (LEVELS - 1) + b - 1) * 2 + g + 1
                            pe.wait_ge(sem["inv_dev"], rise(l, "inv_dev", m))
                            for h in range(HEADS):
                                if b < LEVELS - 1:
                                    mm(ps[:, 4 + g, h * P:(h + 1) * P], group(g, 4)[:, h, :], group(g, 5)[:, h, :],
                                       start=True, stop=True)
                            for h in range(HEADS):
                                last = mm(ps[:, g, h * P:(h + 1) * P], group(g, 5)[:, h, :], group(g, 4)[:, h, :],
                                          start=True, stop=True)
                            last.then_inc(sem["inv_umm"], 1)
                    pe.wait_ge(sem["z_dve"], rise(l, "z_dve", s + 1))
                    for g in range(2):
                        pe.wait_ge(sem["inv_upd"], rise(l, "inv_upd", (s * LEVELS + LEVELS - 1) * 2 + g + 1))
                        for h in range(HEADS):
                            last = mm(ps[:, 2 + g, h * HD:(h + 1) * HD], group(g, 4)[:, h, :],
                                      z[:, g, h * HD:(h + 1) * HD], start=True, stop=True)
                        last.then_inc(sem["vn_mm"], 1)
                    pe.wait_ge(sem["vn_dve"], rise(l, "vn_dve", 2 * s + 2))
                    if s == 1:
                        pe.wait_ge(sem["qd_dve"], rise(l, "qd_dve", 1))
                    for j in range(2):
                        parts = [(group(g, 7)[:, 2 * j + i, :], group(g, 1)[:, 2 * j + i, :]) for g in range(2) for i in range(2)]
                        if s == 1:
                            parts += [(s_gdn[:, d, j, :], qdec[:, d, j, :]) for d in range(2)]
                        for n, (v, p) in enumerate(parts):
                            last = mm(ps[:, 6, j * P:(j + 1) * P], v, p, start=n == 0, stop=n == len(parts) - 1)
                    last.then_inc(sem["go_mm"], 1)
                    if s == 0:
                        pe.wait_ge(sem["kd_dve"], rise(l, "kd_dve", 1))
                        for g in range(2):
                            for j in range(2):
                                last = mm(ps[:, 4 + g, j * 256:(j + 1) * 256], kdg[:, g, j * P:(j + 1) * P],
                                          group(g, 7)[:, 2 * j:2 * j + 2, :].rearrange("p i c -> p (i c)"),
                                          start=True, stop=True)
                        last.then_inc(sem["gs_mm"], 1)
                pe.wait_ge(sem["gn_sq"], rise(l, "gn_sq", 1))
                mm(bank(7), C("blockones"), group(0, 3).rearrange("p h c -> p (h c)"), start=True, stop=True).then_inc(sem["gn_mm"], 1)

                pe.wait_ge(sem["gn_out"], rise(l, "gn_out", 1))
                pe.wait_ge(sem["nat_out"], rise(l, "nat_out", 1))
                pe.wait_ge(sem["sc_dve"], rise(l, "sc_dve", 1))
                f = 0
                for i, tiles in enumerate(OUT_TILES):
                    in_slot(l, ADA_SLOTS + IN_SLOTS + i)
                    slot = ring[:, (ADA_SLOTS + IN_SLOTS + i) % RING, :]
                    for m in range(tiles):
                        for k in range(KT):
                            at = (k * tiles + m) * P
                            last = mm(ps[:, f // 2, (f % 2) * TOK:(f % 2 + 1) * TOK], slot[:, at:at + P],
                                      hT[:, k, :], start=k == 0, stop=k == KT - 1)
                        f += 1
                    last.then_inc(sem["out_mm"], 1)
                pe.wait_ge(sem["res_dve"], rise(l, "res_dve", 1))
                norm_sum(2)
                pe.wait_ge(sem["h_act"], rise(l, "h_act", 2))
                pe.wait_ge(sem["h_dve"], rise(l, "h_dve", 2))
                rw = Q("router_w").rearrange("p (k n) -> p k n", k=KT)
                for s in range(NS):
                    for k in range(KT):
                        last = mm(ps[:, 0, 64 * s:64 * s + ROUTER], hT[:, k, s * P:(s + 1) * P], rw[:, k, :],
                                  start=k == 0, stop=k == KT - 1)
                last.then_inc(sem["route_mm"], 1)
                pe.wait_ge(sem["route_dve"], rise(l, "route_dve", 1))
                for q in range(N_EXPERTS // 2):
                    b = q % 4
                    if q >= 4:
                        name = "cb_dve" if q % 2 else "cb_act"
                        pe.wait_ge(sem[name], rise(l, name, (q - 4) // 2 + 1))
                    for n in range(4):
                        last = mm(ps[:, b, n * P:(n + 1) * P], bc(comb[:, n % 2, 2 * q + n // 2:2 * q + n // 2 + 1], P), ident,
                                  start=True, stop=True)
                    last.then_inc(sem["cb_mm"], 1)
                pe.wait_ge(sem["cb_act"], rise(l, "cb_act", 8))
                pe.wait_ge(sem["cb_dve"], rise(l, "cb_dve", 8))
                for b in range(4):
                    mm(bank(b), C("zeros"), const[:, 0:512], start=True, stop=False, skip_group_check=True)

                def gate_up(e, j):
                    slot = ring[:, j, :]
                    for which in range(2):
                        for fblk in range(2):
                            for k in range(KT):
                                at = which * 2048 + k * FF + fblk * P
                                last = mm(ps[:, 4 + 2 * (j % 2) + which, fblk * TOK:(fblk + 1) * TOK], slot[:, at:at + P],
                                          hT[:, k, :], start=k == 0, stop=k == KT - 1)
                    last.then_inc(sem["gu_mm"], 1)

                def down(e, j, final=False):
                    slot = ring[:, j, :]
                    for f8 in range(KT):
                        for kk in range(2):
                            at = 4096 + kk * D_MODEL + f8 * P
                            last = mm(ps[:, f8 // 2, (f8 % 2) * TOK:(f8 % 2 + 1) * TOK], slot[:, at:at + P],
                                      gated[:, j % 2, kk, :], start=False, stop=final and f8 % 2 == 1 and kk == 1,
                                      skip_group_check=True)
                    last.then_inc(sem["down_mm"], 1)

                def expert_in(e, j):
                    pe.wait_ge(slot_in[j], (l * ((HEAD_SLOTS + N_EXPERTS) // RING) + HEAD_SLOTS // RING + 1) * 16 + (e - j) * (16 // RING))

                expert_in(0, 0)
                gate_up(0, 0)

                def experts(e0, tail):
                    for j in range(RING):
                        e = e0 + j
                        nxt = (j + 1) % RING
                        if not (tail and j == RING - 1):
                            expert_in(e + 1, nxt)
                            if not (tail is None and j == 0):
                                pe.wait_ge(sem["act_dve"], rise(l, "act_dve", e))
                            gate_up(e + 1, nxt)
                        pe.wait_ge(sem["act_dve"], rise(l, "act_dve", e + 1))
                        down(e, j, final=bool(tail) and j == RING - 1)

                experts(0, None)
                with pe.Fori(1, N_EXPERTS // RING - 1) as turn:
                    experts(turn * RING, False)
                experts(N_EXPERTS - RING, True)

        @block.scalar
        def _(act):
            go = nc.scalar.activation
            act.wait_ge(const_in, 48)
            go(condT[:], condT[:], ACT.Silu).then_inc(cond_e, 1)
            with act.Fori(0, DEPTH) as l:
                links = Links()

                def norm_stats(n):
                    name = "layer_done" if n == 1 else "res_dve"
                    act.wait_ge(sem[name], rise(l, name, 1))
                    go(norm, xT[:].rearrange("p k t -> p (k t)"), ACT.Square).then_inc(sem["norm_sq"], 1)
                    act.wait_ge(sem["norm_mm"], rise(l, "norm_mm", n))
                    go(rstd[:], bank(1, TOK), ACT.Ln, bias=EPS, scale=1.0 / D_MODEL).then_inc(chain_act, 1)
                    act.wait_ge(chain_act, links.next())
                    go(rstd[:], rstd[:], ACT.Exp, scale=-0.5).then_inc(sem["norm_rs"], 1)
                    act.wait_ge(sem["h_scaled"], rise(l, "h_scaled", n))
                    which, sh = (0, 0) if n == 1 else (1, 24)
                    for k in range(4, KT):
                        for s in range(NS):
                            t = hT[:, k, s * P:(s + 1) * P]
                            last = go(t, t, ACT.Identity, bias=adaT[:, sh + k, s:s + 1], scale=scale1[:, which, k, s:s + 1])
                    last.then_inc(sem["h_act"], 1)

                norm_stats(1)
                act.wait_ge(sem["zeroed"], rise(l, "zeroed", 1))
                for u in range(3):
                    act.wait_ge(sem["proj_mm"], rise(l, "proj_mm", u + 1))
                    go(raw[:, 2 * u:2 * u + 2, :, 1:129].rearrange("p m s t -> p (m s) t"),
                       bank(proj_bank(u)).rearrange("p (m t) -> p m t", m=4), ACT.Copy).then_inc(sem["proj_act"], 1)
                act.wait_ge(sem["sp_in"], rise(l, "sp_in", 1))
                go(spe[:], spa[:], ACT.Exp, scale=-1.0).then_inc(chain_act, 1)
                act.wait_ge(chain_act, links.next())
                go(spe[:], spe[:], ACT.Ln, bias=1.0).then_inc(chain_act, 1)
                act.wait_ge(chain_act, links.next())
                go(beta[:], gin[:, :, 8:16], ACT.Exp, scale=-1.0).then_inc(chain_act, 1)
                act.wait_ge(chain_act, links.next())
                go(nega[:], Q("a_log"), ACT.Exp).then_inc(sem["sp_act"], 1)

                def copy_unit(u, out):
                    act.wait_ge(sem["proj_mm"], rise(l, "proj_mm", u + 1))
                    go(out, bank(proj_bank(u)), ACT.Copy).then_inc(sem["proj_act"], 1)

                copy_unit(6, A("natqk")[:, 0:512])
                copy_unit(7, A("natqk")[:, 512:1024])
                act.wait_ge(sem["proj_mm"], rise(l, "proj_mm", 9))
                go(zr, bank(proj_bank(8)), ACT.Silu).then_inc(sem["proj_act"], 1)
                copy_unit(9, A("retqk")[:, 0:512])
                copy_unit(10, A("retqk")[:, 512:1024])
                act.wait_ge(sem["proj_mm"], rise(l, "proj_mm", 12))
                go(zg, bank(proj_bank(11)), ACT.Silu).then_inc(sem["proj_act"], 1)
                act.wait_ge(sem["conv_dve"], rise(l, "conv_dve", 1))
                go(A("qkv"), A("qkv"), ACT.Silu).then_inc(sem["silu_act"], 1)
                copy_unit(13, A("sx"))
                act.wait_ge(sem["qk_mm"], rise(l, "qk_mm", 1))
                go(norm[:, 0:1024], ps[:, 0:2, :].rearrange("p b n -> p (b n)"), ACT.Ln, bias=EPS).then_inc(chain_act, 1)
                act.wait_ge(chain_act, links.next())
                go(norm[:, 1024:2048], ps[:, 2:4, :].rearrange("p b n -> p (b n)"), ACT.Ln, bias=EPS, scale=1.0 / HD).then_inc(chain_act, 1)
                act.wait_ge(chain_act, links.next())
                go(norm[:, 0:512], norm[:, 0:512], ACT.Exp, scale=-0.5, bias=math.log(QK_SCALE))
                go(norm[:, 512:2048], norm[:, 512:2048], ACT.Exp, scale=-0.5).then_inc(sem["qk_rs"], 1)
                act.wait_ge(sem["qk_dve"], rise(l, "qk_dve", 1))
                go(gpad[0:64, :, :, 0, :].rearrange("p t s c -> p (t s) c"),
                   qkv[0:64, 0:4, :].rearrange("p m (s c) -> p (m s) c", s=2), ACT.Copy)
                go(npad[0:64, :, :, 0, :].rearrange("p j s c -> p (j s) c"),
                   natqk[0:64, 2:4, :].rearrange("p m (s c) -> p (m s) c", s=2), ACT.Copy).then_inc(sem["pad_act"], 1)
                act.wait_ge(sem["rope_dve"], rise(l, "rope_dve", 1))
                go(rpad[0:64, :, :, 0, :].rearrange("p j s c -> p (j s) c"),
                   retqk[0:64, 0:2, :].rearrange("p m (s c) -> p (m s) c", s=2), ACT.Copy).then_inc(sem["rpad_act"], 1)
                act.wait_ge(sem["gates_dve"], rise(l, "gates_dve", 1))
                act.wait_ge(sem["sc_dve"], rise(l, "sc_dve", 1))
                for h in range(HEADS):
                    go(ef[:, h, :], C("lag_f"), ACT.Exp, scale=lg[:, h:h + 1])
                    go(eb[:, h, :], C("lag_b"), ACT.Exp, scale=lg[:, 4 + h:5 + h])
                go(kdc[:], kdc[:], ACT.Exp, bias=math.log(QK_SCALE))
                for d, x in enumerate(("cross_f", "cross_b")):
                    for j in range(2):
                        last = go(qx[:, d, j, :], C(x), ACT.Exp, scale=lg[:, 8 + 2 * d + j:9 + 2 * d + j])
                last.then_inc(sem["ret_exp"], 1)
                act.wait_ge(sem["nat_max"], rise(l, "nat_max", 1))
                for n in range(HEADS):
                    t = nat_s[:, n * P:(n + 1) * P]
                    go(t, t, ACT.Exp, bias=natm[:, n:n + 1], accum_out=natsum[:, n:n + 1])
                for h in range(HEADS):
                    for part in range(2):
                        n = HEADS * (1 + part) + h
                        t = nat_s[:, n * P:(n + 1) * P]
                        last = go(t, t, ACT.Exp, bias=natm[:, 4 + h:5 + h], accum_out=natsum[:, n:n + 1])
                last.then_inc(sem["nat_exp"], 1)
                act.wait_ge(sem["nat_tr"], rise(l, "nat_tr", 1))
                go(nat_t, ps[:, 0:3, :].rearrange("p b n -> p (b n)"), ACT.Copy).then_inc(sem["nat_pt"], 1)
                act.wait_ge(sem["nat_o"], rise(l, "nat_o", 1))
                act.wait_ge(sem["proj_mm"], rise(l, "proj_mm", 15))
                go(hT[:, 4:6, :].rearrange("p m t -> p (m t)"), bank(3), ACT.Copy).then_inc(sem["nat_out"], 1)
                act.wait_ge(sem["ret_var"], rise(l, "ret_var", 1))
                go(qx[:].rearrange("p d j c -> p (d j c)"), bank(3), ACT.Ln, bias=EPS, scale=1.0 / HD).then_inc(chain_act, 1)
                act.wait_ge(chain_act, links.next())
                go(qx[:].rearrange("p d j c -> p (d j c)"), qx[:].rearrange("p d j c -> p (d j c)"), ACT.Exp, scale=-0.5).then_inc(sem["ret_rs"], 1)

                for s in range(NS):
                    act.wait_ge(sem["gcol_mm"], rise(l, "gcol_mm", s + 1))
                    go(egc[:], ps[:, 6, 0:16], ACT.Exp).then_inc(sem["gcol_exp"], 1)
                    for d in range(2):
                        act.wait_ge(sem["gr_min"], rise(l, "gr_min", 2 * s + d + 1))
                        m = group(d, 0).rearrange("p h c -> p (h c)")
                        go(m, m, ACT.Exp).then_inc(sem["gr_exp"], 1)
                    act.wait_ge(sem["vt_mm"], rise(l, "vt_mm", s + 1))
                    if s == 0:
                        act.wait_ge(sem["ks_mm"], rise(l, "ks_mm", 1))
                    go(vtok[:, s, :], ps[:, 7, 0:256], ACT.Copy).then_inc(sem["vt_act"], 1)
                    if s == 1:
                        act.wait_ge(sem["qd_mm"], rise(l, "qd_mm", 1))
                        go(qdec.rearrange("p g j c -> p (g j c)"), bank(7), ACT.Exp).then_inc(sem["qd_exp"], 1)
                    for b in range(1, LEVELS):
                        for g in range(2):
                            act.wait_ge(sem["inv_dmm"], rise(l, "inv_dmm", (s * LEVELS + b) * 2 + g + 1))
                            go(group(g, 5).rearrange("p h c -> p (h c)"), bank(2 + g), ACT.Copy).then_inc(sem["inv_dev"], 1)
                act.wait_ge(sem["go_dve"], rise(l, "go_dve", 2))
                go(group(0, 3).rearrange("p h c -> p (h c)"), og.rearrange("p j s c -> p (j s c)"), ACT.Square).then_inc(sem["gn_sq"], 1)
                act.wait_ge(sem["gn_mm"], rise(l, "gn_mm", 1))
                t = group(0, 4).rearrange("p h c -> p (h c)")
                go(t, bank(7), ACT.Ln, bias=EPS, scale=1.0 / HD).then_inc(chain_act, 1)
                act.wait_ge(chain_act, links.next())
                go(t, t, ACT.Exp, scale=-0.5).then_inc(sem["gn_rs"], 1)

                norm_stats(2)
                act.wait_ge(sem["route_d1"], rise(l, "route_d1", 1))
                go(rs_[:, 0:8], rs_[:, 0:8], ACT.Exp).then_inc(sem["route_exp1"], 1)
                act.wait_ge(sem["route_d2"], rise(l, "route_d2", 1))
                go(rs_[:, 12:14], rs_[:, 12:14], ACT.Exp).then_inc(sem["route_exp2"], 1)
                for q in range(0, N_EXPERTS // 2, 2):
                    act.wait_ge(sem["cb_mm"], rise(l, "cb_mm", q + 1))
                    go(cb[:, 2 * q:2 * q + 2, :].rearrange("p e t -> p (e t)"), bank(q % 4), ACT.Copy).then_inc(sem["cb_act"], 1)
                act.sem_clear(chain_act)
                links.restart()
                with act.Fori(0, N_EXPERTS // 2) as turn:
                    e2 = turn * 2
                    for j in range(2):
                        act.wait_ge(sem["gu_mm"], rise(l, "gu_mm", e2 + (j + 1)))
                        go(sg[:, j].rearrange("p f t -> p (f t)"), bank(4 + 2 * j), ACT.Silu).then_inc(sem["silu"], 1)

        @block.vector
        def _(dve):
            V = nc.vector
            tt, ts, stt, copy = V.tensor_tensor, V.tensor_scalar, V.scalar_tensor_tensor, V.tensor_copy
            dve.wait_ge(const_in, 48)
            V.memset(natm[:], 0.0).then_inc(sem["layer_done"], 1)
            with dve.Fori(0, DEPTH) as l:
                links = Links()
                dve.wait_ge(sem["layer_done"], rise(l, "layer_done", 1))
                dve.wait_ge(sem["param_dma"], rise(l, "param_dma", 16))
                tt(Q("nat_bias").rearrange("p (a c) -> p a c", c=GRID_W), Q("nat_bias").rearrange("p (a c) -> p a c", c=GRID_W),
                          bc(C("colmask").unsqueeze(1), 2 * HEADS, GRID_W), ALU.add).then_inc(chain_dve, 1)
                dve.wait_ge(chain_dve, links.next())
                dve.wait_ge(sem["ada_mm"], rise(l, "ada_mm", ADA_SLOTS))
                tt(adaT[:], ps[:, 0, 0:96].rearrange("p (m s) -> p m s", s=NS), bc(Q("ada_b").unsqueeze(2), 48, NS), ALU.add).then_inc(chain_dve, 1)
                dve.wait_ge(chain_dve, links.next())
                for n, (at, name) in enumerate(((8, "norm_mix"), (32, "norm_ffn"))):
                    stt(scale1[:, n], adaT[:, at:at + KT, :], 1.0, bc(Q(name).unsqueeze(2), KT, NS), ALU.add, ALU.mult).then_inc(chain_dve, 1)
                    dve.wait_ge(chain_dve, links.next())

                def modulate(n):
                    dve.wait_ge(sem["norm_rs"], rise(l, "norm_rs", n))
                    tt(hT[:], xT[:], bc(rstd[:].unsqueeze(1), KT, TOK), ALU.mult).then_inc(sem["h_scaled"], 1)
                    dve.wait_ge(sem["h_scaled"], rise(l, "h_scaled", n))
                    which, sh = (0, 0) if n == 1 else (1, 24)
                    for k in range(4):
                        for s in range(NS):
                            t = hT[:, k, s * P:(s + 1) * P]
                            last = ts(t, t, scale1[:, which, k, s:s + 1], adaT[:, sh + k, s:s + 1], ALU.mult, ALU.add)
                    last.then_inc(sem["h_dve"], 1)

                modulate(1)
                dve.wait_ge(sem["zeroed"], rise(l, "zeroed", 1))
                for s in range(NS):
                    dve.wait_ge(sem["proj_mm"], rise(l, "proj_mm", 4 + s))
                    v_in = bank(proj_bank(3 + s)).rearrange("p (a i d) -> p a i d", i=2, d=HD)
                    v_out = vp[:, s].rearrange("p r j n -> p (r j) n")
                    copy(v_out[:, :, 0:HD], v_in[:, :, 0, :])
                    copy(v_out[:, :, P + HD:256], v_in[:, :, 1, :]).then_inc(sem["proj_dve"], 1)
                dve.wait_ge(sem["proj_mm"], rise(l, "proj_mm", 6))
                copy(gin[:], ps[:, proj_bank(5), 0:32].rearrange("p (s n) -> p s n", s=2)).then_inc(sem["proj_dve"], 1)
                dve.wait_ge(sem["proj_dve"], rise(l, "proj_dve", 3))
                tt(spx[:, 0:16].rearrange("p (s n) -> p s n", s=2), gin[:, :, 0:8], bc(Q("dt_bias").unsqueeze(1), 2, 8), ALU.add)
                gam = param[:, PARAM["gamma_cols"].start:PARAM["gamma_rows"].stop]
                ts(spx[:, 16:28], gam, -1.0, None, ALU.mult).then_inc(chain_dve, 1)
                dve.wait_ge(chain_dve, links.next())
                stt(spa[:], spx[:], -1.0, spx[:], ALU.mult, ALU.max).then_inc(sem["sp_in"], 1)

                def conv(out, inp, taps, tiles, at=0):
                    for tap in range(3):
                        for m in range(tiles):
                            k = taps[:, 3 * m + tap:3 * m + tap + 1]
                            t = inp[:, m, :, tap:tap + P]
                            o = out(m)
                            last = ts(o, t, k, None, ALU.mult) if tap == 0 else stt(o, t, k, o, ALU.mult, ALU.add)
                        if tap < 2:
                            last.then_inc(chain_dve, 1)
                            dve.wait_ge(chain_dve, links.next())
                    return last

                dve.wait_ge(sem["proj_act"], rise(l, "proj_act", 3))
                conv(lambda m: qkv[:, m, :].rearrange("p (s t) -> p s t", s=2), raw, Q("conv_gdn"), 6).then_inc(sem["conv_dve"], 1)
                dve.wait_ge(sem["sp_act"], rise(l, "sp_act", 1))
                stt(spx[:], spx[:], 0.0, spe[:], ALU.max, ALU.add).then_inc(chain_dve, 1)
                dve.wait_ge(chain_dve, links.next())
                stt(gdec[:], spx[:, 0:16].rearrange("p (s n) -> p s n", s=2), -1.0, bc(nega[:].unsqueeze(1), 2, 8), ALU.mult, ALU.mult)
                ts(lg[:], spx[:, 16:28], -1.0, None, ALU.mult)
                ts(beta[:], beta[:], 1.0, None, ALU.add).then_inc(chain_dve, 1)
                dve.wait_ge(chain_dve, links.next())
                V.reciprocal(beta[:], beta[:]).then_inc(chain_dve, 1)
                dve.wait_ge(chain_dve, links.next())
                for d in range(2):
                    last = ts(kdc[:, 4 * d:4 * d + 4], lg[:, 4 * d:4 * d + 4], C("idx")[:, d:d + 1], None, ALU.mult)
                last.then_inc(sem["gates_dve"], 1)
                dve.wait_ge(sem["proj_mm"], rise(l, "proj_mm", 13))
                copy(A("sb"), bank(proj_bank(12))).then_inc(sem["proj_dve"], 1)
                dve.wait_ge(sem["silu_act"], rise(l, "silu_act", 1))
                tt(norm[:, 0:1024], A("qkv")[:, 0:1024], A("qkv")[:, 0:1024], ALU.mult)
                dve.wait_ge(sem["proj_act"], rise(l, "proj_act", 5))
                tt(norm[:, 1024:2048], A("natqk"), A("natqk"), ALU.mult).then_inc(sem["qk_sq"], 1)
                dve.wait_ge(sem["proj_mm"], rise(l, "proj_mm", 15))
                dve.wait_ge(sem["proj_act"], rise(l, "proj_act", 10))
                tt(ub[:, :, :, 1:129].rearrange("p m s t -> p (m s) t"), bank(proj_bank(14)).rearrange("p (m t) -> p m t", m=4),
                   sxT.rearrange("p m s t -> p (m s) t"), ALU.mult).then_inc(sem["proj_dve"], 1)
                dve.wait_ge(sem["proj_dve"], rise(l, "proj_dve", 5))
                conv(lambda m: hT[:, 6 + m, :].rearrange("p (s t) -> p s t", s=2), ub, Q("conv_sc"), 2).then_inc(chain_dve, 1)
                dve.wait_ge(chain_dve, links.next())
                mix_sc = hT[:, 6:8, :].rearrange("p m t -> p (m t)")
                tt(mix_sc, mix_sc, A("sb"), ALU.mult).then_inc(sem["sc_dve"], 1)
                dve.wait_ge(sem["qk_rs"], rise(l, "qk_rs", 1))
                dve.wait_ge(sem["sc_dve"], rise(l, "sc_dve", 1))
                tt(A("qkv")[:, 0:1024], A("qkv")[:, 0:1024], norm[:, 0:1024], ALU.mult)
                stt(A("natqk")[:, 0:512], A("natqk")[:, 0:512], Q("q_norm"), norm[:, 1024:1536], ALU.mult, ALU.mult)
                stt(A("natqk")[:, 512:1024], A("natqk")[:, 512:1024], Q("k_norm"), norm[:, 1536:2048], ALU.mult, ALU.mult).then_inc(sem["qk_dve"], 1)
                dve.wait_ge(sem["rope_mm"], rise(l, "rope_mm", 1))
                dve.wait_ge(sem["qk_dve"], rise(l, "qk_dve", 1))
                rsin = norm[:, 0:512].rearrange("p (m t) -> p m t", m=4)
                tt(rsin, bank(4).rearrange("p (m t) -> p m t", m=4), bc(C("sin").unsqueeze(1), 4, P), ALU.mult)
                tt(retqk[:, :, P:TOK], retqk[:, :, P:TOK], bc(C("cos").unsqueeze(1), 4, P), ALU.mult).then_inc(chain_dve, 1)
                dve.wait_ge(chain_dve, links.next())
                tt(retqk[:, :, P:TOK], retqk[:, :, P:TOK], rsin, ALU.add).then_inc(sem["rope_dve"], 1)

                dve.wait_ge(sem["rope_dve"], rise(l, "rope_dve", 1))
                dve.wait_ge(sem["nat_mm"], rise(l, "nat_mm", 1))
                ts(nat_s[:, 0:512], bank(0), QK_SCALE, None, ALU.mult)
                stt(nat_s[:, 512:1024], bank(1), QK_SCALE, Q("nat_bias"), ALU.mult, ALU.add)
                ts(nat_s[:, 1024:1536], bank(2), QK_SCALE, None, ALU.mult).then_inc(chain_dve, 1)
                dve.wait_ge(chain_dve, links.next())
                V.tensor_reduce(natm[:], nat_s.rearrange("p (n k) -> p n k", k=P), AX.X, ALU.max).then_inc(chain_dve, 1)
                dve.wait_ge(chain_dve, links.next())
                tt(natm[:, 4:8], natm[:, 4:8], natm[:, 8:12], ALU.max).then_inc(chain_dve, 1)
                dve.wait_ge(chain_dve, links.next())
                ts(natm[:, 0:8], natm[:, 0:8], -1.0, None, ALU.mult).then_inc(sem["nat_max"], 1)
                dve.wait_ge(sem["nat_exp"], rise(l, "nat_exp", 1))
                tt(natsum[:, 4:8], natsum[:, 4:8], natsum[:, 8:12], ALU.add).then_inc(chain_dve, 1)
                dve.wait_ge(chain_dve, links.next())
                V.reciprocal(natsum[:, 0:8], natsum[:, 0:8]).then_inc(chain_dve, 1)
                dve.wait_ge(chain_dve, links.next())
                for n, r in enumerate((0, 4, 4)):
                    t = heads(nat_s[:, n * 512:(n + 1) * 512])
                    last = tt(t, t, bc(natsum[:, r:r + 4].unsqueeze(2), 4, P), ALU.mult)
                last.then_inc(sem["nat_p"], 1)

                dve.wait_ge(sem["ret_exp"], rise(l, "ret_exp", 1))
                stt(ef, ef, QK_SCALE, bc(upto[0].unsqueeze(1), HEADS, P), ALU.mult, ALU.mult)
                stt(eb, eb, QK_SCALE, bc(upto[1].unsqueeze(1), HEADS, P), ALU.mult, ALU.mult).then_inc(chain_dve, 1)
                dve.wait_ge(chain_dve, links.next())
                tt(ef, ef, eb, ALU.add).then_inc(chain_dve, 1)
                dve.wait_ge(chain_dve, links.next())
                tt(qx, qx, bc(retqk[:, 0:2, P:TOK].unsqueeze(1), 2, 2, P), ALU.mult)
                dve.wait_ge(sem["ret_mm"], rise(l, "ret_mm", 1))
                dve.wait_ge(sem["nat_tr"], rise(l, "nat_tr", 1))
                tt(ret_a.rearrange("p s h c -> p s (h c)"), ps[:, 6:8, :],
                   bc(ef.rearrange("p h c -> p (h c)").unsqueeze(1), 2, 512), ALU.mult).then_inc(sem["ret_a"], 1)
                dve.wait_ge(sem["ret_kt"], rise(l, "ret_kt", 1))
                for d in range(2):
                    last = tt(ret_kd[:, d].rearrange("p (h n) -> p h n", h=HEADS), ps[:, 5, 0:256].rearrange("p (h n) -> p h n", h=HEADS),
                              bc(kdc[:, 4 * d:4 * d + 4].unsqueeze(2), HEADS, HD), ALU.mult)
                last.then_inc(sem["ret_kd"], 1)
                dve.wait_ge(sem["ret_o"], rise(l, "ret_o", 1))
                rog, rsq = ef.rearrange("p h c -> p (h c)"), eb.rearrange("p h c -> p (h c)")
                copy(rog, bank(4)).then_inc(sem["ret_og"], 1)
                dve.wait_ge(sem["ret_sf"], rise(l, "ret_sf", 1))

                def states(out, first):
                    for i in range(2):
                        lo = slice(64 * i, 64 * i + 64)
                        last = copy(out[lo], ps[lo, first:first + 2, :].rearrange("p d (j n) -> p d j n", j=2)[:, :, :, 192 * i:192 * i + HD])
                    return last

                states(state, 0).then_inc(sem["ret_st"], 1)
                dve.wait_ge(sem["ret_mean"], rise(l, "ret_mean", 1))
                stt(rog, bank(2), -1.0 / HD, rog, ALU.mult, ALU.add).then_inc(chain_dve, 1)
                dve.wait_ge(chain_dve, links.next())
                tt(rsq, rog, rog, ALU.mult).then_inc(sem["ret_sq"], 1)
                dve.wait_ge(sem["ret_rs"], rise(l, "ret_rs", 1))
                tt(rog, rog, qx.rearrange("p d j c -> p (d j c)"), ALU.mult).then_inc(chain_dve, 1)
                dve.wait_ge(chain_dve, links.next())
                tt(hT[:, 2:4, :].rearrange("p m t -> p (m t)"), rog, zr, ALU.mult).then_inc(sem["ret_out"], 1)
                dve.wait_ge(kv_out, l * 48 + 48)
                dve.wait_ge(sem["ret_out"], rise(l, "ret_out", 1))
                dve.wait_ge(sem["nat_out"], rise(l, "nat_out", 1))
                copy(qdec.rearrange("p d j (i n) -> p (d j i) n", i=2), bc(gdec[:, 1, :].unsqueeze(2), 8, HD)).then_inc(sem["qd_g"], 1)

                for s in range(NS):
                    dve.wait_ge(sem["gr_mm"], rise(l, "gr_mm", s + 1))
                    for d in range(2):
                        ts(group(d, 0).rearrange("p h c -> p (h c)"), bank(2 + d), 0.0, None, ALU.min).then_inc(sem["gr_min"], 1)
                    for d in range(2):
                        dve.wait_ge(sem["gr_exp"], rise(l, "gr_exp", 2 * s + d + 1))
                        tt(group(d, 0), group(d, 0), bc(upto[d].unsqueeze(1), HEADS, P), ALU.mult).then_inc(chain_dve, 1)
                        dve.wait_ge(chain_dve, links.next())
                        m = group(d, 0).rearrange("p (j i) c -> p j (i c)", j=2)
                        tt(group(d, 1).rearrange("p (j i) c -> p j (i c)", j=2), ps[:, 0:2, 0:256], m, ALU.mult)
                        tt(group(d, 2).rearrange("p (j i) c -> p j (i c)", j=2), ps[:, 0:2, 256:512], m, ALU.mult).then_inc(chain_dve, 1)
                        dve.wait_ge(chain_dve, links.next())
                        lt = group(d, 2).rearrange("p h c -> p (h c)")
                        last = tt(lt, lt, bank(4 + d), ALU.mult)
                        if d == 0:
                            last.then_inc(chain_dve, 1)
                            dve.wait_ge(chain_dve, links.next())
                    last.then_inc(sem["gr_dec"], 1)
                    dve.wait_ge(sem["vt_act"], rise(l, "vt_act", s + 1))
                    dve.wait_ge(sem["gcol_exp"], rise(l, "gcol_exp", s + 1))
                    dve.wait_ge(sem["ks_mm"], rise(l, "ks_mm", s + 1))
                    vh = vtok[:, s, :].rearrange("p (h n) -> p h n", h=HEADS)
                    for d in range(2):
                        zd = z[:, d, :].rearrange("p (h n) -> p h n", h=HEADS)
                        bcol = bc(beta[:, s, 4 * d:4 * d + 4].unsqueeze(2), HEADS, HD)
                        if s == 0:
                            last = tt(zd, vh, bcol, ALU.mult)
                            continue
                        ks = ps[:, 6, 256 * d:256 * d + 256].rearrange("p (h n) -> p h n", h=HEADS)
                        tt(zd, ks, bc(egc[:, 4 * d:4 * d + 4].unsqueeze(2), HEADS, HD), ALU.mult).then_inc(chain_dve, 1)
                        dve.wait_ge(chain_dve, links.next())
                        tt(zd, vh, zd, ALU.subtract).then_inc(chain_dve, 1)
                        dve.wait_ge(chain_dve, links.next())
                        last = tt(zd, zd, bcol, ALU.mult)
                    last.then_inc(sem["z_dve"], 1)
                    if s == 0:
                        for d in range(2):
                            last = tt(kdg[:, d, :].rearrange("p (h n) -> p h n", h=HEADS), ps[:, 7, 256:512].rearrange("p (h n) -> p h n", h=HEADS),
                                      bc(egc[:, 8 + 4 * d:12 + 4 * d].unsqueeze(2), HEADS, HD), ALU.mult)
                        last.then_inc(sem["kd_dve"], 1)
                    else:
                        dve.wait_ge(sem["qd_exp"], rise(l, "qd_exp", 1))
                        tt(qdec, qdec, bc(qkv[:, 0:2, P:TOK].unsqueeze(1), 2, 2, P), ALU.mult).then_inc(sem["qd_dve"], 1)
                    for b in range(LEVELS):
                        for g in range(2):
                            n = (s * LEVELS + b) * 2 + g + 1
                            t, t_t = group(g, 3), group(g, 4)
                            if b == 0:
                                dve.wait_ge(sem["inv_dmm"], rise(l, "inv_dmm", n))
                                tt(t, heads(bank(2 + g)), bc(ident.unsqueeze(1), HEADS, P), ALU.add)
                                tt(t_t, group(g, 6), bc(ident.unsqueeze(1), HEADS, P), ALU.add).then_inc(sem["inv_upd"], 1)
                                continue
                            dve.wait_ge(sem["inv_umm"], rise(l, "inv_umm", (s * (LEVELS - 1) + b - 1) * 2 + g + 1))
                            dve.wait_ge(sem["inv_upd"], rise(l, "inv_upd", n - 2))
                            if b < LEVELS - 1:
                                tt(t, t, heads(bank(4 + g)), ALU.add)
                            tt(t_t, t_t, heads(bank(g)), ALU.add).then_inc(sem["inv_upd"], 1)
                    dve.wait_ge(sem["vnp_zero"], rise(l, "vnp_zero", 1))
                    for g in range(2):
                        dve.wait_ge(sem["vn_mm"], rise(l, "vn_mm", 2 * s + g + 1))
                        vn = ps[:, 2 + g, 0:256].rearrange("p (j i n) -> p j i n", j=2, i=2)
                        pad = group(g, 7).rearrange("p (j i) c -> p j i c", j=2)
                        copy(pad[:, :, 0, 0:HD], vn[:, :, 0, :])
                        copy(pad[:, :, 1, HD:P], vn[:, :, 1, :]).then_inc(sem["vn_dve"], 1)
                    dve.wait_ge(sem["go_mm"], rise(l, "go_mm", s + 1))
                    copy(og[:, :, s, :], ps[:, 6, 0:256].rearrange("p (j c) -> p j c", j=2)).then_inc(sem["go_dve"], 1)
                    if s == 0:
                        dve.wait_ge(sem["gs_mm"], rise(l, "gs_mm", 1))
                        dve.wait_ge(state_out, l * 32 + 16)
                        states(state, 4).then_inc(sem["gs_st"], 1)
                dve.wait_ge(sem["gn_rs"], rise(l, "gn_rs", 1))
                gn = group(0, 3).rearrange("p h c -> p (h c)")
                stt(gn, og.rearrange("p j s c -> p (j s c)"), Q("gdn_norm"), group(0, 4).rearrange("p h c -> p (h c)"), ALU.mult, ALU.mult).then_inc(chain_dve, 1)
                dve.wait_ge(chain_dve, links.next())
                tt(hT[:, 0:2, :].rearrange("p m t -> p (m t)"), gn, zg, ALU.mult).then_inc(sem["gn_out"], 1)

                def residual(gate):
                    for f in range(KT):
                        for s in range(NS):
                            t = xT[:, f, s * P:(s + 1) * P]
                            last = stt(t, ps[:, f // 2, (f % 2) * TOK + s * P:(f % 2) * TOK + (s + 1) * P],
                                       adaT[:, gate + f, s:s + 1], t, ALU.mult, ALU.add)
                    return last

                dve.wait_ge(sem["out_mm"], rise(l, "out_mm", 3))
                residual(16).then_inc(sem["res_dve"], 1)
                dve.wait_ge(sem["res_dve"], rise(l, "res_dve", 1))
                modulate(2)

                dve.wait_ge(sem["route_mm"], rise(l, "route_mm", 1))
                gd, tmp4, oh4 = (rs_[:, a:a + 8].rearrange("p (s n) -> p s n", s=2) for a in (0, 20, 28))
                els, oh1, oh2, tmp8, c8 = (rs_[:, a:a + 16].rearrange("p (s n) -> p s n", s=2) for a in (36, 52, 68, 84, 100))
                gm, gs, e2, m1, m2, tw, gw, pick = (rs_[:, a:a + 2] for a in (8, 10, 12, 14, 16, 18, 116, 118))
                prio4, prio8 = C("prio")[:, 4:8], C("prio")
                dve.wait_ge(state_out, l * 32 + 32)
                tt(rt, ps[:, 0, 0:128].rearrange("p (s n) -> p s n", s=2)[:, :, 0:ROUTER], bc(Q("router_b").unsqueeze(1), 2, ROUTER), ALU.add).then_inc(chain_dve, 1)
                dve.wait_ge(chain_dve, links.next())
                V.tensor_reduce(gm, rt[:, :, 0:4], AX.X, ALU.max).then_inc(chain_dve, 1)
                dve.wait_ge(chain_dve, links.next())
                tt(gd, rt[:, :, 0:4], bc(gm.unsqueeze(2), 2, 4), ALU.subtract).then_inc(chain_dve, 1)
                dve.wait_ge(chain_dve, links.next())
                stt(tmp4, gd, 0.0, bc(prio4.unsqueeze(1), 2, 4), ALU.is_ge, ALU.mult).then_inc(sem["route_d1"], 1)
                dve.wait_ge(sem["route_d1"], rise(l, "route_d1", 1))
                V.tensor_reduce(pick, tmp4, AX.X, ALU.max).then_inc(chain_dve, 1)
                dve.wait_ge(chain_dve, links.next())
                tt(oh4, tmp4, bc(pick.unsqueeze(2), 2, 4), ALU.is_equal).then_inc(chain_dve, 1)
                dve.wait_ge(chain_dve, links.next())
                by_group = comb[:].rearrange("p s (g n) -> p s g n", g=N_GROUPS)
                tt(by_group, rt[:, :, 4:ROUTER].rearrange("p s (g n) -> p s g n", g=N_GROUPS),
                          bc(oh4.unsqueeze(3), 2, N_GROUPS, PER_GROUP), ALU.mult).then_inc(chain_dve, 1)
                dve.wait_ge(chain_dve, links.next())
                V.tensor_reduce(els, by_group.rearrange("p s g n -> p s n g"), AX.X, ALU.add).then_inc(chain_dve, 1)
                dve.wait_ge(chain_dve, links.next())
                for n, (m, oh) in enumerate(((m1, oh1), (m2, oh2))):
                    V.tensor_reduce(m, els, AX.X, ALU.max).then_inc(chain_dve, 1)
                    dve.wait_ge(chain_dve, links.next())
                    for s in range(NS):
                        last = stt(tmp8[:, s], els[:, s], m[:, s:s + 1], prio8, ALU.is_equal, ALU.mult)
                    last.then_inc(chain_dve, 1)
                    dve.wait_ge(chain_dve, links.next())
                    V.tensor_reduce(pick, tmp8, AX.X, ALU.max).then_inc(chain_dve, 1)
                    dve.wait_ge(chain_dve, links.next())
                    tt(oh, tmp8, bc(pick.unsqueeze(2), 2, PER_GROUP), ALU.is_equal).then_inc(chain_dve, 1)
                    dve.wait_ge(chain_dve, links.next())
                    if n == 0:
                        stt(els, oh1, -BIG, els, ALU.mult, ALU.add).then_inc(chain_dve, 1)
                        dve.wait_ge(chain_dve, links.next())
                tt(e2, m2, m1, ALU.subtract).then_inc(sem["route_d2"], 1)
                dve.wait_ge(sem["route_exp1"], rise(l, "route_exp1", 1))
                V.tensor_reduce(gs, gd, AX.X, ALU.add).then_inc(chain_dve, 1)
                dve.wait_ge(chain_dve, links.next())
                V.reciprocal(gw, gs).then_inc(chain_dve, 1)
                dve.wait_ge(chain_dve, links.next())
                dve.wait_ge(sem["route_exp2"], rise(l, "route_exp2", 1))
                ts(tw, e2, 1.0, None, ALU.add).then_inc(chain_dve, 1)
                dve.wait_ge(chain_dve, links.next())
                V.reciprocal(tw, tw).then_inc(chain_dve, 1)
                dve.wait_ge(chain_dve, links.next())
                tt(tw, tw, gw, ALU.mult).then_inc(chain_dve, 1)
                dve.wait_ge(chain_dve, links.next())
                tt(e2, e2, tw, ALU.mult).then_inc(chain_dve, 1)
                dve.wait_ge(chain_dve, links.next())
                tt(oh1, oh1, bc(tw.unsqueeze(2), 2, PER_GROUP), ALU.mult)
                tt(oh2, oh2, bc(e2.unsqueeze(2), 2, PER_GROUP), ALU.mult).then_inc(chain_dve, 1)
                dve.wait_ge(chain_dve, links.next())
                tt(c8, oh1, oh2, ALU.add).then_inc(chain_dve, 1)
                dve.wait_ge(chain_dve, links.next())
                dve.sem_clear(chain_dve)
                links.restart()
                tt(by_group, bc(oh4.unsqueeze(3), 2, N_GROUPS, PER_GROUP), bc(c8.unsqueeze(2), 2, N_GROUPS, PER_GROUP), ALU.mult).then_inc(sem["route_dve"], 1)
                for q in range(1, N_EXPERTS // 2, 2):
                    dve.wait_ge(sem["cb_mm"], rise(l, "cb_mm", q + 1))
                    copy(cb[:, 2 * q:2 * q + 2, :].rearrange("p e t -> p (e t)"), bank(q % 4)).then_inc(sem["cb_dve"], 1)
                dve.wait_ge(const_in, 48)
                dve.wait_ge(sem["cb_act"], rise(l, "cb_act", 8))
                dve.wait_ge(sem["cb_dve"], rise(l, "cb_dve", 8))
                with dve.Fori(0, N_EXPERTS // 2) as turn:
                    e2x = turn * 2
                    for j in range(2):
                        dve.wait_ge(sem["silu"], rise(l, "silu", e2x + (j + 1)))
                        t = sg[:, j].rearrange("p f t -> p (f t)")
                        tt(t, t, bank(5 + 2 * j), ALU.mult).then_inc(sem["prod"], 1)
                        dve.wait_ge(sem["prod"], rise(l, "prod", e2x + (j + 1)))
                        weight = arena[:, bass.ds((e2x + j) * TOK, TOK)]
                        tt(gated[:, j], sg[:, j], bc(weight.unsqueeze(1), 2, TOK), ALU.mult).then_inc(sem["act_dve"], 1)
                dve.wait_ge(sem["down_mm"], rise(l, "down_mm", N_EXPERTS))
                residual(40).then_inc(sem["layer_done"], 1)

        @block.gpsimd
        def _(pool):
            G = nc.gpsimd
            with pool.Fori(0, DEPTH) as l:
                pool.wait_ge(const_in, 48)
                pool.wait_ge(sem["layer_done"], rise(l, "layer_done", 1))
                zeros = C("zeros")
                G.tensor_tensor(raw[:, :, :, 0:130:129].rearrange("p m s t -> p (m s) t"), zeros[:, 0:24].rearrange("p (a b) -> p a b", b=2),
                                zeros[:, 0:24].rearrange("p (a b) -> p a b", b=2), ALU.mult)
                G.memset(A("vp"), 0.0)
                G.memset(ub[:, :, :, 0:130:129].rearrange("p m s t -> p (m s) t"), 0.0)
                G.memset(A("gpad"), 0.0)
                G.memset(arena[:, ARENA["npad"].start:ARENA["rpad"].stop], 0.0).then_inc(sem["zeroed"], 1)
                pool.wait_ge(const_in, 48)
                pool.wait_ge(sem["zeroed"], rise(l, "zeroed", 1))
                pool.wait_ge(const_in, 48)
                pool.wait_ge(sem["qk_dve"], rise(l, "qk_dve", 1))
                G.tensor_copy(gpad[64:P, :, :, 1, :].rearrange("p t s c -> p (t s) c"),
                              qkv[64:P, 0:4, :].rearrange("p m (s c) -> p (m s) c", s=2))
                G.tensor_copy(npad[64:P, :, :, 1, :].rearrange("p j s c -> p (j s) c"),
                              natqk[64:P, 2:4, :].rearrange("p m (s c) -> p (m s) c", s=2)).then_inc(sem["pad_pool"], 1)
                pool.wait_ge(const_in, 48)
                pool.wait_ge(sem["rope_dve"], rise(l, "rope_dve", 1))
                G.tensor_copy(rpad[64:P, :, :, 1, :].rearrange("p j s c -> p (j s) c"),
                              retqk[64:P, 0:2, :].rearrange("p m (s c) -> p (m s) c", s=2)).then_inc(sem["rpad_pool"], 1)
                out = dst["nkT"][bass.ds(l, 1)].rearrange("o p j c -> (o p) j c")
                pool.dma_start(out, natqk[:, 2:4, 0:P]).then_inc(kv_out, 16)
                for i in range(2):
                    out = dst["nv"][bass.ds(l, 1)].rearrange("o p j i d -> (o p) j i d")[:, :, i, :]
                    pool.dma_start(out, vp[:, 0, 1, :, 192 * i:192 * i + HD]).then_inc(kv_out, 16)
                pool.wait_ge(const_in, 48)
                pool.wait_ge(sem["ret_st"], rise(l, "ret_st", 1))
                pool.dma_start(dst["s_ret"][bass.ds(l, 1)].rearrange("o p n -> (o p) n"),
                               state[:].rearrange("p d j n -> p (d j n)")).then_inc(state_out, 16)
                pool.wait_ge(const_in, 48)
                pool.wait_ge(sem["ret_out"], rise(l, "ret_out", 1))
                pool.wait_ge(kv_out, l * 48 + 48)
                pool.wait_ge(const_in, 48)
                pool.wait_ge(sem["nat_out"], rise(l, "nat_out", 1))
                G.tensor_tensor(group(0, 7), bc(zeros.unsqueeze(1), HEADS, P), bc(zeros.unsqueeze(1), HEADS, P), ALU.mult)
                G.memset(group(1, 7).rearrange("p h c -> p (h c)"), 0.0).then_inc(sem["vnp_zero"], 1)
                for s in range(NS):
                    pool.wait_ge(const_in, 48)
                    pool.wait_ge(sem["gr_dec"], rise(l, "gr_dec", s + 1))
                    for b in range(LEVELS):
                        for g in range(2):
                            n = (s * LEVELS + b) * 2 + g + 1
                            if n > 2:
                                pool.wait_ge(const_in, 48)
                                pool.wait_ge(sem["inv_upd"], rise(l, "inv_upd", n - 2))
                            G.tensor_tensor(group(g, 6), group(g, 2), bc(levels[:, g, b, :].unsqueeze(1), HEADS, P), ALU.mult)\
                             .then_inc(sem["inv_c"], 1)
                    if s == 0:
                        pool.wait_ge(const_in, 48)
                        pool.wait_ge(sem["gs_st"], rise(l, "gs_st", 1))
                        pool.dma_start(dst["s_gdn"][bass.ds(l, 1)].rearrange("o p n -> (o p) n"),
                                       state[:].rearrange("p d j n -> p (d j n)")).then_inc(state_out, 16)
                pool.wait_ge(state_out, l * 32 + 32)


def constants():
    c = np.zeros((P, CONST_W), np.float32)
    t = np.arange(P)
    k, m = t[:, None], t[None, :]

    def put(name, a):
        c[:, CONST[name]] = a

    put("ident", k == m)
    put("ones", 1.0)
    put("blockones", k // HD == m // HD)
    put("upto_f", k <= m)
    put("upto_b", k >= m)
    put("negupto_f", -1.0 * (k <= m))
    put("negupto_b", -1.0 * (k >= m))
    put("after_f", k > m)
    put("after_b", k < m)
    half = HD // 4
    put("rot", np.where(m % (2 * half) < half, -1.0 * (k == m + half), 1.0 * (k == m - half)))
    freq = np.float32(10000.0) ** (-np.arange(half, dtype=np.float32) / np.float32(half))
    pos = np.where((t % HD)[:, None] < HD // 2, (t // GRID_W)[None, :], (t % GRID_W)[None, :]).astype(np.float32)
    angle = pos * freq[t % half][:, None]
    put("cos", np.cos(angle))
    put("sin", np.sin(angle))
    put("lag_f", np.maximum(m - k, 0))
    put("lag_b", np.maximum(k - m, 0))
    put("cross_f", np.broadcast_to(m + 1.0, (P, P)))
    put("cross_b", np.broadcast_to(P - 1.0 * m, (P, P)))
    col = t[:GRID_W]
    c0 = np.clip(col - WIN_COLS // 2, 0, GRID_W - WIN_COLS)
    inside = (col[None, :] >= c0[:, None]) & (col[None, :] < c0[:, None] + WIN_COLS)
    put("colmask", np.tile(np.where(inside, 0.0, -BIG), (P // GRID_W, 1)))
    put("idx", np.stack([P - 1 - t, t], 1))
    put("prio", np.arange(PER_GROUP, 0, -1))
    lv = np.zeros((P, 2, LEVELS, P), np.float32)
    for b in range(LEVELS):
        size = 2 ** b
        same = k // (2 * size) == m // (2 * size)
        lv[:, 0, b] = -1.0 * (same & (k // size % 2 == 0) & (m // size % 2 == 1))
        lv[:, 1, b] = -1.0 * (same & (k // size % 2 == 1) & (m // size % 2 == 0))
    put("levels", lv.reshape(P, -1))
    return c


def kernel(x_prompt, x_sample, state_gdn, state_ret, cache_nat_k, cache_nat_v, c, c_ctx,
           ada_w, ada_b, norm_mix_w, norm_ffn_w, w_in, gdn_conv_w, gdn_a_log, gdn_dt_bias, gdn_norm_w,
           ret_gamma_logit, nat_q_norm_w, nat_k_norm_w, nat_rpb, sc_conv_w, w_out,
           router_group_w, router_group_b, router_expert_w, router_expert_b,
           moe_w_gate, moe_w_up, moe_w_down):
    import concourse.bacc as _bacc
    from concourse.bass_utils import run_bass_kernel_spmd as _run

    A = np.asarray

    def feat(a):
        a = A(a)
        return np.swapaxes(a.reshape(*a.shape[:-1], -1, P), -1, -2)

    def rows(a):
        a = A(a)
        return np.moveaxis(a.reshape(*a.shape[:-2], -1, P, a.shape[-1]), -3, -2)

    x = np.stack([A(x_prompt)[0], A(x_sample)[0]])
    xT = np.ascontiguousarray(x.reshape(NS, P, KT, P).transpose(3, 2, 0, 1)).reshape(P, KT, TOK)
    condT = np.ascontiguousarray(feat(np.stack([A(c_ctx), A(c)[0]])).transpose(1, 2, 0))

    ada = np.ascontiguousarray(rows(ada_w).reshape(DEPTH, P, KT, ADA_SLOTS, 768).transpose(0, 3, 1, 2, 4)).reshape(DEPTH, ADA_SLOTS, P, SLOT)
    wi = rows(w_in)
    sizes = (768, 256, 8, 8, 768, 256, 768, 768)
    at = np.concatenate([[0], np.cumsum(sizes)])
    a_qkv, a_z, a_dec, a_beta, r_qkv, r_g, n_qkv, s_bcx = (wi[..., at[i]:at[i + 1]] for i in range(8))
    w_feat = np.stack([
        a_qkv,
        np.concatenate([n_qkv[..., :512], r_g], -1),
        np.concatenate([r_qkv[..., :512], a_z], -1),
        np.concatenate([s_bcx[..., :256], s_bcx[..., 512:], s_bcx[..., 256:512]], -1)], 1).reshape(DEPTH, 4, P, SLOT)
    w_tok = np.concatenate([a_dec, a_beta, r_qkv[..., 512:], n_qkv[..., 512:]], -1).reshape(DEPTH, P, KT * TOKCOLS)
    wo = rows(w_out)
    edge = np.concatenate([[0], np.cumsum(OUT_TILES)]) * P
    w_o = np.concatenate([wo[..., edge[i]:edge[i + 1]].reshape(DEPTH, P, -1) for i in range(OUT_SLOTS)], -1)
    moe = np.concatenate([rows(moe_w_gate).reshape(DEPTH, N_EXPERTS, P, -1), rows(moe_w_up).reshape(DEPTH, N_EXPERTS, P, -1),
                          rows(moe_w_down).reshape(DEPTH, N_EXPERTS, P, -1)], -1)

    par = np.zeros((DEPTH, P, PARAM_W), np.float32)

    def put(name, a):
        par[:, :, PARAM[name]] = a

    def everywhere(a):
        return np.broadcast_to(A(a).reshape(DEPTH, 1, -1), (DEPTH, P, A(a)[0].size))

    def pair(a):
        return np.concatenate([A(a), A(a)], 1)[:, :, None]

    put("norm_mix", feat(norm_mix_w))
    put("norm_ffn", feat(norm_ffn_w))
    put("ada_b", feat(ada_b))
    put("conv_gdn", feat(gdn_conv_w).transpose(0, 2, 3, 1).reshape(DEPTH, P, -1))
    put("conv_sc", feat(sc_conv_w).transpose(0, 2, 3, 1).reshape(DEPTH, P, -1))
    put("gdn_norm", pair(gdn_norm_w))
    put("q_norm", pair(nat_q_norm_w))
    put("k_norm", pair(nat_k_norm_w))
    put("dt_bias", everywhere(gdn_dt_bias))
    put("a_log", everywhere(gdn_a_log))
    put("gamma_cols", everywhere(ret_gamma_logit))
    put("gamma_rows", np.repeat(A(ret_gamma_logit).reshape(DEPTH, 2, 2, 2).transpose(0, 3, 1, 2).reshape(DEPTH, 2, 4), HD, 1))
    put("router_b", np.concatenate([everywhere(router_group_b), everywhere(router_expert_b)], -1))
    put("router_w", np.concatenate([rows(router_group_w), rows(router_expert_w)], -1).reshape(DEPTH, P, -1))
    r = np.arange(P) // GRID_W
    q = np.arange(P) % GRID_W
    i, cc = np.arange(2), np.arange(GRID_W)
    ri = i[None, :, None] - r[:, None, None] + WIN_ROWS - 1
    ci = np.clip(cc[None, None, :] - q[:, None, None], -(WIN_COLS - 1), WIN_COLS - 1) + WIN_COLS - 1
    put("nat_bias", A(nat_rpb)[:, :, ri, ci].transpose(0, 2, 1, 3, 4).reshape(DEPTH, P, -1))
    ck = np.zeros((DEPTH, 2, HD, HEADS, P), np.float32)
    cv = np.zeros((DEPTH, P, HEADS, 2, HD), np.float32)
    states = []
    for h in range(HEADS):
        ck[:, h % 2, :, h] = A(cache_nat_k)[0, :, :, h].transpose(0, 2, 1)
        cv[:, :, h, h % 2] = A(cache_nat_v)[0, :, :, h]
    for st in (state_gdn, state_ret):
        b = np.zeros((DEPTH, 2, HD, 2, 2, 2, HD), np.float32)
        for h in range(HEADS):
            b[:, h % 2, :, :, h // 2, h % 2] = A(st)[0, :, :, h].transpose(0, 2, 1, 3)
        states.append(b.reshape(DEPTH, P, -1))
    put("ck", ck.reshape(DEPTH, P, -1))
    put("cv", cv.reshape(DEPTH, P, -1))
    put("s_gdn", states[0])
    put("s_ret", states[1])

    nc = _bacc.Bacc("TRN2", target_bir_lowering=False, num_devices=1)
    arrays = dict(xT=xT, condT=condT, const=constants(), param=par, ada_w=ada, w_feat=w_feat, w_tok=w_tok, w_out=w_o, moe=moe)
    arrays = {n: np.ascontiguousarray(a) for n, a in arrays.items()}
    src = {n: nc.dram_tensor(f"in_{n}", list(a.shape), F32, kind="ExternalInput").ap() for n, a in arrays.items()}
    outs = dict(yT=(P, KT, TOK), nkT=(DEPTH, P, 2, P), nv=(DEPTH, P, 2, 2, HD), s_ret=(DEPTH, P, 4 * HD), s_gdn=(DEPTH, P, 4 * HD))
    dst = {n: nc.dram_tensor(f"out_{n}", list(shape), F32, kind="ExternalOutput").ap() for n, shape in outs.items()}
    build_trunk(nc, src, dst)
    got = _run(nc, [{f"in_{n}": a for n, a in arrays.items()}], core_ids=[0]).results[0]

    y = np.asarray(got["out_yT"]).reshape(P, KT, NS, P).transpose(2, 3, 1, 0).reshape(NS, P, D_MODEL)

    def state(a):
        return np.asarray(a).reshape(DEPTH, 2, HD, 2, 2, HD).transpose(0, 3, 4, 1, 2, 5).reshape(1, DEPTH, 2, HEADS, HD, HD)

    nk = np.asarray(got["out_nkT"]).reshape(DEPTH, 2, HD, 2, P).transpose(0, 4, 3, 1, 2).reshape(1, DEPTH, P, HEADS, HD)
    nv = np.asarray(got["out_nv"]).reshape(1, DEPTH, P, HEADS, HD)
    return (np.ascontiguousarray(y[0:1]), np.ascontiguousarray(y[1:2]), np.ascontiguousarray(state(got["out_s_gdn"])),
            np.ascontiguousarray(state(got["out_s_ret"])), np.ascontiguousarray(nk), np.ascontiguousarray(nv))
```

```python
import math
from contextlib import ExitStack

import numpy as np

import concourse.bass as bass
from concourse import mybir

F32 = mybir.dt.float32
F32R = mybir.dt.float32r
ACT = mybir.ActivationFunctionType
ALU = mybir.AluOpType
AX = mybir.AxisListType

P = 128
D_MODEL, DEPTH = 1024, 2
KT = D_MODEL // P
NS = 2
TOK = NS * P
HEADS, HD = 4, 64
GRID_W, WIN_ROWS, WIN_COLS = 64, 8, 16
N_GROUPS, PER_GROUP, FF = 4, 8, 256
N_EXPERTS = N_GROUPS * PER_GROUP
ROUTER = N_GROUPS + N_EXPERTS
EPS = 1e-6
BIG = 1e30
QK_SCALE = HD ** -0.5
LEVELS = 7

RING, SLOT = 4, 6144
ADA_SLOTS, IN_SLOTS, OUT_SLOTS = 8, 5, 3
HEAD_SLOTS = ADA_SLOTS + IN_SLOTS + OUT_SLOTS
ADA_TILES = 6
ADA_FIRST = 3


def ada_load(i):
    return i if i < ADA_FIRST else i + IN_SLOTS


def in_load(i):
    return ADA_FIRST + i


def out_load(i):
    return ADA_SLOTS + IN_SLOTS + i


TOKCOLS = 16 + 2 * HEADS * HD
OUT_TILES = (3, 3, 2)
assert HEAD_SLOTS % RING == 0 and N_EXPERTS % RING == 0


def layout(*parts):
    at, out = 0, {}
    for name, width in parts:
        out[name] = slice(at, at + width)
        at += width
    return out, at


CONST, CONST_W = layout(
    ("ident", P), ("zeros", P), ("ones", P), ("blockones", P), ("upto_f", P), ("upto_b", P), ("negupto_f", P), ("negupto_b", P),
    ("after_f", P), ("after_b", P), ("rot", P), ("cos", P), ("sin", P), ("lag_f", P), ("lag_b", P),
    ("cross_f", P), ("cross_b", P), ("colmask", GRID_W), ("idx", 2), ("prio", PER_GROUP),
    ("levels", 2 * LEVELS * P))
PARAM, PARAM_W = layout(
    ("norm_mix", KT), ("norm_ffn", KT), ("ada_b", 48), ("conv_gdn", 18), ("conv_sc", 6), ("gdn_norm", 1),
    ("q_norm", 1), ("k_norm", 1), ("dt_bias", 8), ("a_log", 8), ("gamma_cols", 8), ("gamma_rows", 4),
    ("router_b", ROUTER), ("router_w", KT * ROUTER), ("nat_bias", HEADS * 2 * GRID_W),
    ("ck", HEADS * P), ("cv", HEADS * P), ("s_gdn", 4 * P), ("s_ret", 4 * P))
ARENA, ARENA_W = layout(
    ("raw", 6 * 2 * 130), ("qkv", 6 * TOK), ("zg", 2 * TOK), ("gpad", 8 * 256), ("vtok", 2 * 256), ("zr", 2 * TOK),
    ("natqk", 4 * TOK), ("retqk", 4 * TOK), ("sb", 2 * TOK), ("sx", 2 * TOK), ("ub", 2 * 2 * 130),
    ("vp", 2 * 2 * 512), ("norm", 2048), ("npad", 4 * 256), ("rpad", 4 * 256))
GROUP_W = 8 * 512

PER = dict(
    ada_mm=8, ada_row=8, ada_tr=8, ada_dve=8, norm_sq=2, norm_mm=2, norm_rs=2, h_scaled=2, h_act=2, h_dve=2,
    proj_mm=15, proj_act=10, proj_dve=5, conv_dve=1, silu_act=1, sc_dve=1,
    sp_in=1, sp_act=1, gates_dve=1,
    qk_sq=1, qk_mm=1, qk_rs=1, qk_dve=1, pad_act=1, pad_pool=1, rope_mm=1, rope_dve=1, rpad_act=1, rpad_pool=1,
    zeroed=1, param_dma=16, layer_done=1,
    nat_mm=1, nat_max=1, nat_exp=1, nat_p=1, nat_tr=1, nat_pt=1, nat_o=1, nat_out=1,
    ret_exp=1, ret_mm=1, ret_a=1, ret_kt=1, ret_kd=1, ret_o=1, ret_sf=1, ret_st=1, ret_og=1,
    ret_mean=1, ret_sq=1, ret_var=1, ret_rs=1, ret_out=1,
    vnp_zero=1, gr_mm=2, gr_min=4, gr_exp=4, gr_dec=2, gcol_mm=2, gcol_exp=2, vt_mm=2, vt_act=2,
    ks_mm=2, z_dve=2, inv_c=28, inv_dmm=28, inv_dev=24, inv_umm=24, inv_upd=28,
    vn_mm=4, vn_dve=4, qd_g=1, qd_mm=1, qd_exp=1, qd_dve=1, kd_dve=1, gs_mm=1, gs_st=1, go_mm=2, go_dve=2,
    gn_sq=1, gn_mm=1, gn_rs=1, gn_out=1,
    out_mm=3, res_dve=1, route_mm=1, route_exp1=1, route_d1=1, route_d2=1, route_exp2=1, route_dve=1,
    cb_mm=16, cb_act=8, cb_dve=8, h_hi=1, h_lo=1,
    gate_mm=32, up_mm=32, down_mm=32, silu=32, hi_gate=32, hi_up=32, hi_down=32, act_hi=32,
    lo_gate=32, lo_up=32, lo_down=32, prod=32, act_dve=32, act_lo=32,
)


def build_trunk(nc, src, dst):
    with ExitStack() as ctx:
        def sb(name, *shape):
            return ctx.enter_context(nc.sbuf_tensor(name, list(shape), F32))

        def two_types(name, *shape):
            with nc.sbuf_tensor(name, list(shape), F32) as plain:
                pass
            rounded = ctx.enter_context(nc.sbuf_tensor(name + "_r", list(shape), F32R))
            return plain, rounded

        ring, ring_r = zip(*(two_types(f"ring{j}", P, SLOT) for j in range(RING)))
        xT = sb("xT", P, KT, TOK)
        hT, hT_r = two_types("hT", P, KT, TOK)
        const = sb("const", P, CONST_W)
        param, param_r = two_types("param", P, PARAM_W)
        arena, arena_r = two_types("arena", P, ARENA_W)
        condT = sb("condT", P, KT, NS)
        condp = sb("condp", P, KT, 4 * ADA_TILES - 2)
        adaT = sb("adaT", P, 48, NS)
        scale1 = sb("scale1", P, 2, KT, NS)
        rstd = sb("rstd", P, TOK)
        adarow = rstd[:, 0:P]
        spx = sb("spx", P, 28)
        beta = sb("beta", P, 2, 8)
        nega = sb("nega", P, 8)
        gdec = sb("gdec", P, 2, 8)
        lg = sb("lg", P, 12)
        kdc = sb("kdc", P, 8)
        egc = sb("egc", P, 16)
        natm = sb("natm", P, 12)
        natsum = sb("natsum", P, 12)
        state = sb("state", P, 2, 2, HD)
        state_flat = state[:].rearrange("p d j n -> p (d j n)")
        rt = state_flat[:, 0:2 * ROUTER].rearrange("p (s n) -> p s n", s=2)
        rs_ = state_flat[:, 2 * ROUTER:2 * ROUTER + 120]
        gin = state_flat[:, 0:32].rearrange("p (s n) -> p s n", s=2)
        comb = sb("comb", P, 2, N_EXPERTS)
        comb_flat = comb[:].rearrange("p s n -> p (s n)")
        spa, spe = comb_flat[:, 0:28], comb_flat[:, 28:56]
        ps = ctx.enter_context(nc.psum_tensor("ps", [P, 8, 512], F32))

        sem = {name: ctx.enter_context(nc.semaphore(name)) for name in PER}
        slot_in = [ctx.enter_context(nc.semaphore(f"slot_in{j}")) for j in range(RING)]
        const_in = ctx.enter_context(nc.semaphore("const_in"))
        cond_e = ctx.enter_context(nc.semaphore("cond_silu"))
        state_out = ctx.enter_context(nc.semaphore("state_out"))
        kv_out = ctx.enter_context(nc.semaphore("kv_out"))
        y_out = ctx.enter_context(nc.semaphore("y_out"))
        chain_dve = ctx.enter_context(nc.semaphore("chain_dve"))
        chain_act = ctx.enter_context(nc.semaphore("chain_act"))

        def C(name):
            return const[:, CONST[name]]

        def Q(name):
            return param[:, PARAM[name]]

        def A(name):
            return arena[:, ARENA[name]]

        def bc(ap, *shape):
            return ap.broadcast_to([P, *shape])

        raw = A("raw").rearrange("p (m s t) -> p m s t", m=6, s=2)
        qkv = A("qkv").rearrange("p (m t) -> p m t", m=6)
        zg, zr = A("zg"), A("zr")
        og = A("zr").rearrange("p (j s c) -> p j s c", j=2, s=2)
        gpad = A("gpad").rearrange("p (t s i c) -> p t s i c", t=4, s=2, i=2)
        vtok = A("vtok").rearrange("p (s n) -> p s n", s=2)
        natqk = A("natqk").rearrange("p (m t) -> p m t", m=4)
        retqk = A("retqk").rearrange("p (m t) -> p m t", m=4)
        sbT, sxT = A("sb").rearrange("p (m s t) -> p m s t", m=2, s=2), A("sx").rearrange("p (m s t) -> p m s t", m=2, s=2)
        ub = A("ub").rearrange("p (m s t) -> p m s t", m=2, s=2)
        vp = A("vp").rearrange("p (s r j n) -> p s r j n", s=2, r=2, j=2)
        norm = A("norm")
        npad = A("npad").rearrange("p (j s i c) -> p j s i c", j=2, s=2, i=2)
        rpad = A("rpad").rearrange("p (j s i c) -> p j s i c", j=2, s=2, i=2)
        levels = C("levels").rearrange("p (d b c) -> p d b c", d=2, b=LEVELS)
        ident = C("ident")
        g0 = ARENA["natqk"].start

        def group(g, part):
            at = g0 + g * GROUP_W + part * 512
            return arena[:, at:at + 512].rearrange("p (h c) -> p h c", h=HEADS)

        tail = g0 + 2 * GROUP_W
        z = arena[:, tail:tail + 512].rearrange("p (g n) -> p g n", g=2)
        kdg = arena[:, tail + 512:tail + 1024].rearrange("p (g n) -> p g n", g=2)
        qdec = arena[:, tail + 1024:tail + 1536].rearrange("p (g j c) -> p g j c", g=2, j=2)
        assert tail + 1536 <= ARENA_W
        cb = arena[:, 0:N_EXPERTS * TOK].rearrange("p (e t) -> p e t", e=N_EXPERTS)
        moe0 = N_EXPERTS * TOK
        sg = arena[:, moe0:moe0 + 1024].rearrange("p (b f t) -> p b f t", b=2, f=2)
        sg_lo = arena_r[:, moe0:moe0 + 1024].rearrange("p (b f t) -> p b f t", b=2, f=2)
        gated_hi = arena_r[:, moe0 + 1024:moe0 + 2048].rearrange("p (b f t) -> p b f t", b=2, f=2)
        w_hi = arena_r[:, moe0 + 2048:moe0 + 2048 + SLOT]
        assert moe0 + 2048 + SLOT <= ARENA_W
        h_hi = param_r[:, PARAM["ck"].start:PARAM["ck"].start + KT * TOK].rearrange("p (k t) -> p k t", k=KT)
        assert PARAM["ck"].start + KT * TOK <= PARAM_W
        h_lo = hT_r[:]
        nat_s = norm[:, 0:1536]
        nat_t = A("raw")[:, 0:1536]
        ef = arena[:, ARENA["sb"].start:ARENA["sb"].start + 512].rearrange("p (h c) -> p h c", h=HEADS)
        eb = arena[:, ARENA["sb"].start + 512:ARENA["sb"].start + 1024].rearrange("p (h c) -> p h c", h=HEADS)
        qx = arena[:, ARENA["ub"].start:ARENA["ub"].start + 512].rearrange("p (d j c) -> p d j c", d=2, j=2)
        ret_a = norm[:, 0:1024].rearrange("p (s h c) -> p s h c", s=2, h=HEADS)
        ret_kd = norm[:, 1024:1536].rearrange("p (d n) -> p d n", d=2)
        qx_in = norm[:, 1536:2048].rearrange("p (d j c) -> p d j c", d=2, j=2)
        upto = [C("upto_f"), C("upto_b")]
        negupto = [C("negupto_f"), C("negupto_b")]
        after = [C("after_f"), C("after_b")]
        s_gdn = Q("s_gdn").rearrange("p (d j c) -> p d j c", d=2, j=2)
        s_ret = Q("s_ret").rearrange("p (d j c) -> p d j c", d=2, j=2)
        ck = Q("ck").rearrange("p (h c) -> p h c", h=HEADS)
        cv = Q("cv").rearrange("p (h c) -> p h c", h=HEADS)

        def bank(b, width=512):
            return ps[:, b, 0:width]

        def heads(ap):
            return ap.rearrange("p (h c) -> p h c", h=HEADS)

        def proj_bank(u):
            return (u + 2) % 8

        block = ctx.enter_context(nc.Block())

        def rise(layer, name, n):
            return layer * PER[name] + n

        class Links:

            def __init__(self):
                self.count = 0

            def next(self):
                self.count += 1
                return self.count

            def restart(self):
                self.count = 0

        @block.sync
        def _(sp):
            sp.dma_start(condT[:], src["condT"]).then_inc(const_in, 16)
            sp.dma_start(const[:], src["const"]).then_inc(const_in, 16)
            sp.dma_start(xT[:], src["xT"]).then_inc(const_in, 16)

            def ring_in(n, what):
                rows, width = what
                sp.dma_start(ring[n % RING][:, 0:width], rows).then_inc(slot_in[n % RING], 16)

            loads = [None] * HEAD_SLOTS
            for i in range(ADA_SLOTS):
                loads[ada_load(i)] = ("ada_w", i, SLOT, "ada_mm", i + 1)
            for i in range(IN_SLOTS):
                loads[in_load(i)] = ("w_feat", i - (i > 1), SLOT, "proj_mm", 3 * i + 3)
            loads[in_load(1)] = ("w_tok", None, KT * TOKCOLS, "proj_mm", 6)
            for i in range(OUT_SLOTS):
                loads[out_load(i)] = ("w_out", sum(OUT_TILES[:i]) * KT * P, OUT_TILES[i] * KT * P, "out_mm", i + 1)

            def head_slot(l, i):
                name, part, width, _, _ = loads[i]
                if name == "w_tok":
                    return src[name][l], width
                if name == "w_out":
                    return src[name][l][:, part:part + width], width
                return src[name][l, part], width

            def slot_free(l, i):
                if i < HEAD_SLOTS:
                    _, _, _, name, n = loads[i]
                    sp.wait_ge(sem[name], rise(l, name, n))
                else:
                    sp.wait_ge(sem["down_mm"], rise(l, "down_mm", i - HEAD_SLOTS + 1))

            for l in range(DEPTH):
                for i in range(HEAD_SLOTS):
                    if i >= RING:
                        slot_free(l, i - RING)
                    elif l > 0:
                        slot_free(l - 1, HEAD_SLOTS + N_EXPERTS + i - RING)
                    ring_in(i, head_slot(l, i))
                    if i == RING - 1:
                        if l > 0:
                            sp.wait_ge(sem["layer_done"], l + 1)
                        sp.dma_start(param[:], src["param"][l]).then_inc(sem["param_dma"], 16)
                for e in range(RING):
                    slot_free(l, HEAD_SLOTS - RING + e)
                    ring_in(e, (src["moe"][l, e], SLOT))
                with sp.Fori(1, N_EXPERTS // RING) as turn:
                    e4 = turn * RING
                    for j in range(RING):
                        sp.wait_ge(sem["down_mm"], e4 + (l * PER["down_mm"] + j - RING + 1))
                        rows = src["moe"][l, bass.ds(e4 + j, 1)].rearrange("o p n -> (o p) n")
                        ring_in(j, (rows, SLOT))
            sp.wait_ge(sem["layer_done"], DEPTH + 1)
            sp.dma_start(dst["yT"], xT[:]).then_inc(y_out, 16)
            sp.wait_ge(y_out, 16)

        @block.tensor
        def _(pe):
            mm = nc.tensor.matmul

            def in_slot(l, i):
                pe.wait_ge(slot_in[i % RING], l * (16 * (HEAD_SLOTS + N_EXPERTS) // RING) + 16 * (i // RING + 1))

            with pe.Fori(0, DEPTH) as l:
                pe.wait_ge(cond_e, 1)
                pe.wait_ge(sem["layer_done"], rise(l, "layer_done", 1))

                def ada(i, bank_in, tiles=range(ADA_TILES)):
                    if tiles[0] == 0:
                        in_slot(l, ada_load(i))
                    slot = ring[ada_load(i) % RING][:]
                    for m in tiles:
                        for k in range(KT):
                            lead = 2 * (ADA_TILES - 1 - m)
                            last = mm(ps[0:2 * ADA_TILES, bank_in, 0:P], condp[:, k, lead:lead + 2 * ADA_TILES],
                                      slot[:, k * 768 + m * P:k * 768 + (m + 1) * P],
                                      start=m == 0 and k == 0, stop=m == ADA_TILES - 1 and k == KT - 1)
                    if tiles[-1] == ADA_TILES - 1:
                        last.then_inc(sem["ada_mm"], 1)

                def ada_transpose(i, bank_out):
                    pe.wait_ge(sem["ada_row"], rise(l, "ada_row", i + 1))
                    mm(ps[:, bank_out, 0:2 * ADA_TILES], adarow[0:2 * ADA_TILES, :], ident[0:2 * ADA_TILES, 0:2 * ADA_TILES],
                       start=True, stop=True).then_inc(sem["ada_tr"], 1)

                for i in range(ADA_FIRST):
                    if i >= 2:
                        pe.wait_ge(sem["ada_row"], rise(l, "ada_row", i - 1))
                    ada(i, 6 + i % 2)
                    if i > 0:
                        if i > 1:
                            pe.wait_ge(sem["ada_dve"], rise(l, "ada_dve", i - 1))
                        ada_transpose(i - 1, 5)
                pe.wait_ge(sem["ada_dve"], rise(l, "ada_dve", ADA_FIRST - 1))
                ada_transpose(ADA_FIRST - 1, 5)

                def norm_sum(n):
                    pe.wait_ge(sem["norm_sq"], rise(l, "norm_sq", n))
                    sq = norm.rearrange("p (k t) -> p k t", k=KT)
                    for k in range(KT):
                        last = mm(bank(1, TOK), C("ones"), sq[:, k, :], start=k == 0, stop=k == KT - 1)
                    last.then_inc(sem["norm_mm"], 1)

                norm_sum(1)
                pe.wait_ge(sem["h_act"], rise(l, "h_act", 1))
                pe.wait_ge(sem["h_dve"], rise(l, "h_dve", 1))
                free_of = {8: ("proj_act", 1), 9: ("proj_act", 2), 10: ("proj_act", 3), 11: ("proj_dve", 1),
                           12: ("proj_dve", 2), 13: ("proj_dve", 3), 14: ("proj_act", 4)}
                u = 0
                for i in range(IN_SLOTS):
                    in_slot(l, in_load(i))
                    slot = ring[in_load(i) % RING][:]
                    if i == 1:
                        for s in range(NS):
                            for k in range(KT):
                                last = mm(bank(proj_bank(3 + s)), hT[:, k, s * P:(s + 1) * P],
                                          slot[:, k * TOKCOLS + 16:(k + 1) * TOKCOLS], start=k == 0, stop=k == KT - 1)
                            last.then_inc(sem["proj_mm"], 1)
                        for s in range(NS):
                            for k in range(KT):
                                last = mm(ps[:, proj_bank(5), 16 * s:16 * s + 16], hT[:, k, s * P:(s + 1) * P],
                                          slot[:, k * TOKCOLS:k * TOKCOLS + 16], start=k == 0, stop=k == KT - 1)
                        last.then_inc(sem["proj_mm"], 1)
                        u += 3
                        continue
                    for pair in range(3):
                        if u in free_of:
                            name, n = free_of[u]
                            pe.wait_ge(sem[name], rise(l, name, n))
                        for m in range(2):
                            for k in range(KT):
                                at = k * 768 + (2 * pair + m) * P
                                last = mm(ps[:, proj_bank(u), m * TOK:(m + 1) * TOK], slot[:, at:at + P],
                                          hT[:, k, :], start=k == 0, stop=k == KT - 1)
                        last.then_inc(sem["proj_mm"], 1)
                        u += 1
                pe.wait_ge(sem["proj_act"], rise(l, "proj_act", 10))
                pe.wait_ge(sem["proj_dve"], rise(l, "proj_dve", 5))
                pe.wait_ge(sem["qk_sq"], rise(l, "qk_sq", 1))
                for b in range(4):
                    last = mm(bank(b), C("blockones"), norm[:, b * 512:(b + 1) * 512], start=True, stop=True)
                last.then_inc(sem["qk_mm"], 1)
                mm(bank(4), C("rot"), retqk[:, :, P:TOK], start=True, stop=True).then_inc(sem["rope_mm"], 1)
                ada(ADA_FIRST, 7)
                ada_transpose(ADA_FIRST, 6)

                pe.wait_ge(sem["pad_act"], rise(l, "pad_act", 1))
                pe.wait_ge(sem["pad_pool"], rise(l, "pad_pool", 1))
                pe.wait_ge(sem["qk_dve"], rise(l, "qk_dve", 1))
                for s in range(NS):
                    for j in range(2):
                        last = mm(ps[:, s, j * 256:(j + 1) * 256], natqk[:, j, s * P:(s + 1) * P],
                                  npad[:, j, s].rearrange("p i c -> p (i c)"), start=True, stop=True)
                for j in range(2):
                    last = mm(ps[:, 2, j * 256:(j + 1) * 256], natqk[:, j, P:TOK],
                              Q("ck")[:, j * 256:(j + 1) * 256], start=True, stop=True)
                last.then_inc(sem["nat_mm"], 1)
                pe.wait_ge(sem["rpad_act"], rise(l, "rpad_act", 1))
                pe.wait_ge(sem["rpad_pool"], rise(l, "rpad_pool", 1))
                pe.wait_ge(sem["ada_dve"], rise(l, "ada_dve", ADA_FIRST + 1))
                for s in range(NS):
                    for j in range(2):
                        last = mm(ps[:, 6 + s, j * 256:(j + 1) * 256], retqk[:, 2 + j, s * P:(s + 1) * P],
                                  rpad[:, j, s].rearrange("p i c -> p (i c)"), start=True, stop=True)
                last.then_inc(sem["ret_mm"], 1)
                for j in range(2):
                    last = nc.tensor.transpose(ps[:, 5, j * P:(j + 1) * P], retqk[:, 2 + j, 0:P], ident)
                last.then_inc(sem["ret_kt"], 1)
                pe.wait_ge(sem["nat_p"], rise(l, "nat_p", 1))
                for b in range(3):
                    for h in range(HEADS):
                        last = nc.tensor.transpose(ps[:, b, h * P:(h + 1) * P],
                                                   nat_s[:, (b * HEADS + h) * P:(b * HEADS + h + 1) * P], ident)
                last.then_inc(sem["nat_tr"], 1)
                pe.wait_ge(sem["nat_pt"], rise(l, "nat_pt", 1))
                for j in range(2):
                    for s in range(NS):
                        parts = [(vp[:, s, 1, j, i * P:(i + 1) * P], nat_t[:, (s * HEADS + 2 * j + i) * P:(s * HEADS + 2 * j + i + 1) * P])
                                 for i in range(2)]
                        if s == 1:
                            parts += [(cv[:, 2 * j + i, :], nat_t[:, (2 * HEADS + 2 * j + i) * P:(2 * HEADS + 2 * j + i + 1) * P])
                                      for i in range(2)]
                        for n, (v, p) in enumerate(parts):
                            last = mm(ps[:, 3, j * 256 + s * P:j * 256 + (s + 1) * P], v, p,
                                      start=n == 0, stop=n == len(parts) - 1)
                last.then_inc(sem["nat_o"], 1)
                pe.wait_ge(sem["ret_a"], rise(l, "ret_a", 1))
                for j in range(2):
                    for s in range(NS):
                        parts = [(vp[:, s, 0, j, i * P:(i + 1) * P], ret_a[:, s, 2 * j + i, :]) for i in range(2)]
                        if s == 1:
                            parts += [(s_ret[:, d, j, :], qx[:, d, j, :]) for d in range(2)]
                        for n, (v, p) in enumerate(parts):
                            last = mm(ps[:, 4, j * 256 + s * P:j * 256 + (s + 1) * P], v, p,
                                      start=n == 0, stop=n == len(parts) - 1)
                last.then_inc(sem["ret_o"], 1)
                pe.wait_ge(sem["ret_kd"], rise(l, "ret_kd", 1))
                for d in range(2):
                    for j in range(2):
                        last = mm(ps[:, d, j * 256:(j + 1) * 256], ret_kd[:, d, j * P:(j + 1) * P],
                                  vp[:, 0, 0, j, :], start=True, stop=True)
                last.then_inc(sem["ret_sf"], 1)
                pe.wait_ge(sem["ret_og"], rise(l, "ret_og", 1))
                mm(bank(2), C("blockones"), ef.rearrange("p h c -> p (h c)"), start=True, stop=True).then_inc(sem["ret_mean"], 1)
                pe.wait_ge(sem["ret_sq"], rise(l, "ret_sq", 1))
                pe.wait_ge(sem["nat_out"], rise(l, "nat_out", 1))
                mm(bank(3), C("blockones"), eb.rearrange("p h c -> p (h c)"), start=True, stop=True).then_inc(sem["ret_var"], 1)
                pe.wait_ge(sem["ret_out"], rise(l, "ret_out", 1))
                pe.wait_ge(sem["ret_st"], rise(l, "ret_st", 1))

                for s in range(NS):
                    tk = slice(s * P, (s + 1) * P)
                    if s == 1:
                        pe.wait_ge(sem["go_dve"], rise(l, "go_dve", 1))
                        pe.wait_ge(sem["gs_st"], rise(l, "gs_st", 1))
                    for d in range(2):
                        for h in range(HEADS):
                            gcol = gdec[:, s, d * 4 + h:d * 4 + h + 1]
                            mm(ps[:, 2 + d, h * P:(h + 1) * P], bc(gcol, P), upto[d], start=True, stop=False)
                            mm(ps[:, 2 + d, h * P:(h + 1) * P], negupto[d], bc(gcol, P), start=False, stop=True)
                        for h in range(HEADS):
                            bcol = beta[:, s, d * 4 + h:d * 4 + h + 1]
                            last = mm(ps[:, 4 + d, h * P:(h + 1) * P], bc(bcol, P), ident, start=True, stop=True)
                    for j in range(2):
                        last = mm(bank(j), qkv[:, 2 + j, tk], gpad[:, j::2, s, :, :].rearrange("p t i c -> p t (i c)"),
                                  start=True, stop=True)
                    last.then_inc(sem["gr_mm"], 1)
                    for d in range(2):
                        mm(ps[:, 6, d * 4:d * 4 + 4], upto[d], gdec[:, s, d * 4:d * 4 + 4], start=True, stop=True)
                        last = mm(ps[:, 6, 8 + d * 4:12 + d * 4], after[d], gdec[:, s, d * 4:d * 4 + 4], start=True, stop=True)
                    last.then_inc(sem["gcol_mm"], 1)
                    for j in range(2):
                        last = nc.tensor.transpose(ps[:, 7, j * P:(j + 1) * P], qkv[:, 4 + j, tk], ident)
                    last.then_inc(sem["vt_mm"], 1)
                    pe.wait_ge(sem["gcol_exp"], rise(l, "gcol_exp", s + 1))
                    if s == 0:
                        for j in range(2):
                            last = nc.tensor.transpose(ps[:, 7, (2 + j) * P:(3 + j) * P], qkv[:, 2 + j, tk], ident)
                        last.then_inc(sem["ks_mm"], 1)
                    else:
                        for d in range(2):
                            for j in range(2):
                                last = mm(ps[:, 6, d * 256 + j * P:d * 256 + (j + 1) * P], qkv[:, 2 + j, tk],
                                          s_gdn[:, d, j, :], start=True, stop=True)
                        last.then_inc(sem["ks_mm"], 1)
                        pe.wait_ge(sem["vt_act"], rise(l, "vt_act", 2))
                        pe.wait_ge(sem["qd_g"], rise(l, "qd_g", 1))
                        for d in range(2):
                            for j in range(2):
                                last = mm(ps[:, 7, (2 * d + j) * P:(2 * d + j + 1) * P], qdec[:, d, j, :], upto[d], start=True, stop=True)
                        last.then_inc(sem["qd_mm"], 1)
                    for b in range(LEVELS):
                        for g in range(2):
                            n = (s * LEVELS + b) * 2 + g + 1
                            m = (s * (LEVELS - 1) + b - 1) * 2 + g + 1
                            pe.wait_ge(sem["inv_c"], rise(l, "inv_c", n))
                            name = "inv_upd" if b else "gr_dec"
                            pe.wait_ge(sem[name], rise(l, name, n - 2 if b else s + 1))
                            for h in range(HEADS):
                                last = mm(ps[:, 2 + g, h * P:(h + 1) * P], group(g, 6)[:, h, :],
                                          group(g, 3)[:, h, :] if b else ident, start=True, stop=True)
                            last.then_inc(sem["inv_dmm"], 1)
                        if b == 0:
                            continue
                        piece = s * (LEVELS - 1) + b - 1
                        third = piece % 3
                        if third == 0:
                            pe.wait_ge(sem["kd_dve"], rise(l, "kd_dve", 1))
                            if s == 1:
                                pe.wait_ge(sem["qd_exp"], rise(l, "qd_exp", 1))
                        ada(ADA_FIRST + 1 + piece // 3, 7, range(2 * third, 2 * third + 2))
                        for g in range(2):
                            m = (s * (LEVELS - 1) + b - 1) * 2 + g + 1
                            pe.wait_ge(sem["inv_dev"], rise(l, "inv_dev", m))
                            for h in range(HEADS):
                                if b < LEVELS - 1:
                                    mm(ps[:, 4 + g, h * P:(h + 1) * P], group(g, 4)[:, h, :], group(g, 5)[:, h, :],
                                       start=True, stop=True)
                            for h in range(HEADS):
                                last = mm(ps[:, g, h * P:(h + 1) * P], group(g, 5)[:, h, :], group(g, 4)[:, h, :],
                                          start=True, stop=True)
                            last.then_inc(sem["inv_umm"], 1)
                        if third == 2:
                            pe.wait_ge(sem["z_dve"], rise(l, "z_dve", s + 1))
                            pe.wait_ge(sem["gcol_exp"], rise(l, "gcol_exp", s + 1))
                            if piece > 2:
                                pe.wait_ge(sem["ada_dve"], rise(l, "ada_dve", ADA_FIRST + 1 + piece // 3))
                            ada_transpose(ADA_FIRST + 1 + piece // 3, 6)
                    pe.wait_ge(sem["z_dve"], rise(l, "z_dve", s + 1))
                    for g in range(2):
                        pe.wait_ge(sem["inv_upd"], rise(l, "inv_upd", (s * LEVELS + LEVELS - 1) * 2 + g + 1))
                        for h in range(HEADS):
                            last = mm(ps[:, 2 + g, h * HD:(h + 1) * HD], group(g, 4)[:, h, :],
                                      z[:, g, h * HD:(h + 1) * HD], start=True, stop=True)
                        last.then_inc(sem["vn_mm"], 1)
                    pe.wait_ge(sem["vn_dve"], rise(l, "vn_dve", 2 * s + 2))
                    pe.wait_ge(sem["ada_dve"], rise(l, "ada_dve", ADA_FIRST + 3 + 2 * s))
                    if s == 1:
                        pe.wait_ge(sem["qd_dve"], rise(l, "qd_dve", 1))
                    for j in range(2):
                        parts = [(group(g, 7)[:, 2 * j + i, :], group(g, 1)[:, 2 * j + i, :]) for g in range(2) for i in range(2)]
                        if s == 1:
                            parts += [(s_gdn[:, d, j, :], qdec[:, d, j, :]) for d in range(2)]
                        for n, (v, p) in enumerate(parts):
                            last = mm(ps[:, 6, j * P:(j + 1) * P], v, p, start=n == 0, stop=n == len(parts) - 1)
                    last.then_inc(sem["go_mm"], 1)
                    if s == 0:
                        pe.wait_ge(sem["kd_dve"], rise(l, "kd_dve", 1))
                        for g in range(2):
                            for j in range(2):
                                last = mm(ps[:, 4 + g, j * 256:(j + 1) * 256], kdg[:, g, j * P:(j + 1) * P],
                                          group(g, 7)[:, 2 * j:2 * j + 2, :].rearrange("p i c -> p (i c)"),
                                          start=True, stop=True)
                        last.then_inc(sem["gs_mm"], 1)
                pe.wait_ge(sem["gn_sq"], rise(l, "gn_sq", 1))
                mm(bank(7), C("blockones"), group(0, 3).rearrange("p h c -> p (h c)"), start=True, stop=True).then_inc(sem["gn_mm"], 1)

                pe.wait_ge(sem["gn_out"], rise(l, "gn_out", 1))
                pe.wait_ge(sem["nat_out"], rise(l, "nat_out", 1))
                pe.wait_ge(sem["sc_dve"], rise(l, "sc_dve", 1))
                f = 0
                for i, tiles in enumerate(OUT_TILES):
                    in_slot(l, out_load(i))
                    slot = ring[out_load(i) % RING][:]
                    for m in range(tiles):
                        for k in range(KT):
                            at = (k * tiles + m) * P
                            last = mm(ps[:, f // 2, (f % 2) * TOK:(f % 2 + 1) * TOK], slot[:, at:at + P],
                                      hT[:, k, :], start=k == 0, stop=k == KT - 1)
                        f += 1
                    last.then_inc(sem["out_mm"], 1)
                pe.wait_ge(sem["res_dve"], rise(l, "res_dve", 1))
                norm_sum(2)
                pe.wait_ge(sem["h_act"], rise(l, "h_act", 2))
                pe.wait_ge(sem["h_dve"], rise(l, "h_dve", 2))
                rw = Q("router_w").rearrange("p (k n) -> p k n", k=KT)
                for s in range(NS):
                    for k in range(KT):
                        last = mm(ps[:, 0, 64 * s:64 * s + ROUTER], hT[:, k, s * P:(s + 1) * P], rw[:, k, :],
                                  start=k == 0, stop=k == KT - 1)
                last.then_inc(sem["route_mm"], 1)
                pe.wait_ge(sem["route_dve"], rise(l, "route_dve", 1))
                for q in range(N_EXPERTS // 2):
                    b = q % 4
                    if q >= 4:
                        name = "cb_dve" if q % 2 else "cb_act"
                        pe.wait_ge(sem[name], rise(l, name, (q - 4) // 2 + 1))
                    for n in range(4):
                        last = mm(ps[:, b, n * P:(n + 1) * P], bc(comb[:, n % 2, 2 * q + n // 2:2 * q + n // 2 + 1], P), ident,
                                  start=True, stop=True)
                    last.then_inc(sem["cb_mm"], 1)
                pe.wait_ge(sem["cb_act"], rise(l, "cb_act", 8))
                pe.wait_ge(sem["cb_dve"], rise(l, "cb_dve", 8))
                for b in range(4):
                    mm(bank(b), C("zeros"), const[:, 0:512], start=True, stop=False, skip_group_check=True)

                def split_products(out, slot_lo, at, x_hi, x_lo, start, stop):
                    hi, lo = w_hi[:, at:at + P], slot_lo[:, at:at + P]
                    mm(out, hi, x_hi, start=start, stop=False, skip_group_check=True)
                    mm(out, hi, x_lo, start=False, stop=False, skip_group_check=True)
                    return mm(out, lo, x_hi, start=False, stop=stop, skip_group_check=True)

                def first_products(e, j, which, name):
                    slot_lo = ring_r[j][:]
                    for fblk in range(2):
                        for k in range(KT):
                            last = split_products(ps[:, 4 + 2 * (j % 2) + which, fblk * TOK:(fblk + 1) * TOK], slot_lo,
                                                  which * 2048 + k * FF + fblk * P, h_hi[:, k, :], h_lo[:, k, :],
                                                  k == 0, k == KT - 1)
                    last.then_inc(sem[name], 1)

                def down(e, j, final):
                    slot_lo = ring_r[j][:]
                    for f8 in range(KT):
                        for kk in range(2):
                            last = split_products(ps[:, f8 // 2, (f8 % 2) * TOK:(f8 % 2 + 1) * TOK], slot_lo,
                                                  4096 + kk * D_MODEL + f8 * P, gated_hi[:, j % 2, kk, :], sg_lo[:, j % 2, kk, :],
                                                  False, final and f8 % 2 == 1 and kk == 1)
                    last.then_inc(sem["down_mm"], 1)

                def step(e, j, first=1, last=False):
                    nxt = (j + 1) % RING
                    if not last:
                        pe.wait_ge(sem["lo_gate"], rise(l, "lo_gate", e + 2))
                        if first > 0:
                            pe.wait_ge(sem["silu"], rise(l, "silu", e))
                        first_products(e + 1, nxt, 0, "gate_mm")
                        pe.wait_ge(sem["lo_up"], rise(l, "lo_up", e + 2))
                        if first > 0:
                            pe.wait_ge(sem["prod"], rise(l, "prod", e))
                        first_products(e + 1, nxt, 1, "up_mm")
                    if first >= 0:
                        pe.wait_ge(sem["lo_down"], rise(l, "lo_down", e + 1))
                        pe.wait_ge(sem["act_lo"], rise(l, "act_lo", e + 1))
                        down(e, j, last)

                pe.wait_ge(sem["h_hi"], rise(l, "h_hi", 1))
                pe.wait_ge(sem["h_lo"], rise(l, "h_lo", 1))
                step(-1, RING - 1, first=-1)
                step(0, 0, first=0)
                for e in range(1, RING):
                    step(e, e)
                with pe.Fori(1, N_EXPERTS // RING - 1) as turn:
                    for j in range(RING):
                        step(turn * RING + j, j)
                for e in range(N_EXPERTS - RING, N_EXPERTS):
                    step(e, e % RING, last=e == N_EXPERTS - 1)

        @block.scalar
        def _(act):
            go = nc.scalar.activation
            act.wait_ge(const_in, 48)
            go(condp[:, :, 0:2 * (ADA_TILES - 1)], C("zeros")[:, 0:2 * (ADA_TILES - 1) * KT].rearrange("p (k n) -> p k n", k=KT), ACT.Copy)
            go(condp[:, :, 2 * ADA_TILES:], C("zeros")[:, 0:2 * (ADA_TILES - 1) * KT].rearrange("p (k n) -> p k n", k=KT), ACT.Copy)
            go(condp[:, :, 2 * (ADA_TILES - 1):2 * ADA_TILES], condT[:], ACT.Silu).then_inc(cond_e, 1)
            with act.Fori(0, DEPTH) as l:
                links = Links()

                def norm_stats(n):
                    name = "layer_done" if n == 1 else "res_dve"
                    act.wait_ge(sem[name], rise(l, name, 1))
                    go(norm, xT[:].rearrange("p k t -> p (k t)"), ACT.Square).then_inc(sem["norm_sq"], 1)
                    act.wait_ge(sem["norm_mm"], rise(l, "norm_mm", n))
                    go(rstd[:], bank(1, TOK), ACT.Ln, bias=EPS, scale=1.0 / D_MODEL).then_inc(chain_act, 1)
                    act.wait_ge(chain_act, links.next())
                    go(rstd[:], rstd[:], ACT.Exp, scale=-0.5).then_inc(sem["norm_rs"], 1)
                    act.wait_ge(sem["h_scaled"], rise(l, "h_scaled", n))
                    which, sh = (0, 0) if n == 1 else (1, 24)
                    for k in range(4, KT):
                        for s in range(NS):
                            t = hT[:, k, s * P:(s + 1) * P]
                            last = go(t, t, ACT.Identity, bias=adaT[:, sh + k, s:s + 1], scale=scale1[:, which, k, s:s + 1])
                    last.then_inc(sem["h_act"], 1)

                def ada_rows(i, bank_in):
                    act.wait_ge(sem["ada_mm"], rise(l, "ada_mm", i + 1))
                    if i > 0:
                        act.wait_ge(sem["ada_tr"], rise(l, "ada_tr", i))
                    go(adarow[0:2 * ADA_TILES, :], ps[0:2 * ADA_TILES, bank_in, 0:P], ACT.Copy).then_inc(sem["ada_row"], 1)

                for i in range(ADA_FIRST):
                    ada_rows(i, 6 + i % 2)
                norm_stats(1)
                act.wait_ge(sem["zeroed"], rise(l, "zeroed", 1))
                for u in range(3):
                    act.wait_ge(sem["proj_mm"], rise(l, "proj_mm", u + 1))
                    go(raw[:, 2 * u:2 * u + 2, :, 1:129].rearrange("p m s t -> p (m s) t"),
                       bank(proj_bank(u)).rearrange("p (m t) -> p m t", m=4), ACT.Copy).then_inc(sem["proj_act"], 1)
                act.wait_ge(sem["sp_in"], rise(l, "sp_in", 1))
                go(spe, spa, ACT.Exp, scale=-1.0).then_inc(chain_act, 1)
                act.wait_ge(chain_act, links.next())
                go(spe, spe, ACT.Ln, bias=1.0).then_inc(chain_act, 1)
                act.wait_ge(chain_act, links.next())
                go(beta[:], gin[:, :, 8:16], ACT.Exp, scale=-1.0).then_inc(chain_act, 1)
                act.wait_ge(chain_act, links.next())
                go(nega[:], Q("a_log"), ACT.Exp).then_inc(sem["sp_act"], 1)

                def copy_unit(u, out):
                    act.wait_ge(sem["proj_mm"], rise(l, "proj_mm", u + 1))
                    go(out, bank(proj_bank(u)), ACT.Copy).then_inc(sem["proj_act"], 1)

                copy_unit(6, A("natqk")[:, 0:512])
                copy_unit(7, A("natqk")[:, 512:1024])
                act.wait_ge(sem["proj_mm"], rise(l, "proj_mm", 9))
                go(zr, bank(proj_bank(8)), ACT.Silu).then_inc(sem["proj_act"], 1)
                copy_unit(9, A("retqk")[:, 0:512])
                copy_unit(10, A("retqk")[:, 512:1024])
                act.wait_ge(sem["proj_mm"], rise(l, "proj_mm", 12))
                go(zg, bank(proj_bank(11)), ACT.Silu).then_inc(sem["proj_act"], 1)
                act.wait_ge(sem["conv_dve"], rise(l, "conv_dve", 1))
                go(A("qkv"), A("qkv"), ACT.Silu).then_inc(sem["silu_act"], 1)
                copy_unit(13, A("sx"))
                act.wait_ge(sem["qk_mm"], rise(l, "qk_mm", 1))
                go(norm[:, 0:1024], ps[:, 0:2, :].rearrange("p b n -> p (b n)"), ACT.Ln, bias=EPS).then_inc(chain_act, 1)
                act.wait_ge(chain_act, links.next())
                go(norm[:, 1024:2048], ps[:, 2:4, :].rearrange("p b n -> p (b n)"), ACT.Ln, bias=EPS, scale=1.0 / HD).then_inc(chain_act, 1)
                act.wait_ge(chain_act, links.next())
                go(norm[:, 0:512], norm[:, 0:512], ACT.Exp, scale=-0.5, bias=math.log(QK_SCALE))
                go(norm[:, 512:2048], norm[:, 512:2048], ACT.Exp, scale=-0.5).then_inc(sem["qk_rs"], 1)
                ada_rows(ADA_FIRST, 7)
                act.wait_ge(sem["qk_dve"], rise(l, "qk_dve", 1))
                go(gpad[0:64, :, :, 0, :].rearrange("p t s c -> p (t s) c"),
                   qkv[0:64, 0:4, :].rearrange("p m (s c) -> p (m s) c", s=2), ACT.Copy)
                go(npad[0:64, :, :, 0, :].rearrange("p j s c -> p (j s) c"),
                   natqk[0:64, 2:4, :].rearrange("p m (s c) -> p (m s) c", s=2), ACT.Copy).then_inc(sem["pad_act"], 1)
                act.wait_ge(sem["rope_dve"], rise(l, "rope_dve", 1))
                go(rpad[0:64, :, :, 0, :].rearrange("p j s c -> p (j s) c"),
                   retqk[0:64, 0:2, :].rearrange("p m (s c) -> p (m s) c", s=2), ACT.Copy).then_inc(sem["rpad_act"], 1)
                act.wait_ge(sem["gates_dve"], rise(l, "gates_dve", 1))
                act.wait_ge(sem["sc_dve"], rise(l, "sc_dve", 1))
                for h in range(HEADS):
                    go(ef[:, h, :], C("lag_f"), ACT.Exp, scale=lg[:, h:h + 1])
                    go(eb[:, h, :], C("lag_b"), ACT.Exp, scale=lg[:, 4 + h:5 + h])
                go(kdc[:], kdc[:], ACT.Exp, bias=math.log(QK_SCALE))
                for d, x in enumerate(("cross_f", "cross_b")):
                    for j in range(2):
                        last = go(qx[:, d, j, :], C(x), ACT.Exp, scale=lg[:, 8 + 2 * d + j:9 + 2 * d + j])
                last.then_inc(sem["ret_exp"], 1)
                act.wait_ge(sem["nat_max"], rise(l, "nat_max", 1))
                for n in range(HEADS):
                    t = nat_s[:, n * P:(n + 1) * P]
                    go(t, t, ACT.Exp, bias=natm[:, n:n + 1], accum_out=natsum[:, n:n + 1])
                for h in range(HEADS):
                    for part in range(2):
                        n = HEADS * (1 + part) + h
                        t = nat_s[:, n * P:(n + 1) * P]
                        last = go(t, t, ACT.Exp, bias=natm[:, 4 + h:5 + h], accum_out=natsum[:, n:n + 1])
                last.then_inc(sem["nat_exp"], 1)
                act.wait_ge(sem["nat_tr"], rise(l, "nat_tr", 1))
                go(nat_t, ps[:, 0:3, :].rearrange("p b n -> p (b n)"), ACT.Copy).then_inc(sem["nat_pt"], 1)
                act.wait_ge(sem["nat_o"], rise(l, "nat_o", 1))
                act.wait_ge(sem["proj_mm"], rise(l, "proj_mm", 15))
                go(hT[:, 4:6, :].rearrange("p m t -> p (m t)"), bank(3), ACT.Copy).then_inc(sem["nat_out"], 1)
                act.wait_ge(sem["ret_var"], rise(l, "ret_var", 1))
                go(qx[:].rearrange("p d j c -> p (d j c)"), bank(3), ACT.Ln, bias=EPS, scale=1.0 / HD).then_inc(chain_act, 1)
                act.wait_ge(chain_act, links.next())
                go(qx[:].rearrange("p d j c -> p (d j c)"), qx[:].rearrange("p d j c -> p (d j c)"), ACT.Exp, scale=-0.5).then_inc(sem["ret_rs"], 1)

                for s in range(NS):
                    act.wait_ge(sem["gcol_mm"], rise(l, "gcol_mm", s + 1))
                    go(egc[:], ps[:, 6, 0:16], ACT.Exp).then_inc(sem["gcol_exp"], 1)
                    for d in range(2):
                        act.wait_ge(sem["gr_min"], rise(l, "gr_min", 2 * s + d + 1))
                        m = group(d, 0).rearrange("p h c -> p (h c)")
                        go(m, m, ACT.Exp).then_inc(sem["gr_exp"], 1)
                    act.wait_ge(sem["vt_mm"], rise(l, "vt_mm", s + 1))
                    if s == 0:
                        act.wait_ge(sem["ks_mm"], rise(l, "ks_mm", 1))
                    go(vtok[:, s, :], ps[:, 7, 0:256], ACT.Copy).then_inc(sem["vt_act"], 1)
                    if s == 1:
                        act.wait_ge(sem["qd_mm"], rise(l, "qd_mm", 1))
                        go(qdec.rearrange("p g j c -> p (g j c)"), bank(7), ACT.Exp).then_inc(sem["qd_exp"], 1)
                    for b in range(1, LEVELS):
                        for g in range(2):
                            act.wait_ge(sem["inv_dmm"], rise(l, "inv_dmm", (s * LEVELS + b) * 2 + g + 1))
                            go(group(g, 5).rearrange("p h c -> p (h c)"), bank(2 + g), ACT.Copy).then_inc(sem["inv_dev"], 1)
                        piece = s * (LEVELS - 1) + b - 1
                        if piece % 3 == 2:
                            ada_rows(ADA_FIRST + 1 + piece // 3, 7)
                act.wait_ge(sem["go_dve"], rise(l, "go_dve", 2))
                go(group(0, 3).rearrange("p h c -> p (h c)"), og.rearrange("p j s c -> p (j s c)"), ACT.Square).then_inc(sem["gn_sq"], 1)
                act.wait_ge(sem["gn_mm"], rise(l, "gn_mm", 1))
                t = group(0, 4).rearrange("p h c -> p (h c)")
                go(t, bank(7), ACT.Ln, bias=EPS, scale=1.0 / HD).then_inc(chain_act, 1)
                act.wait_ge(chain_act, links.next())
                go(t, t, ACT.Exp, scale=-0.5).then_inc(sem["gn_rs"], 1)

                norm_stats(2)
                act.wait_ge(sem["route_d1"], rise(l, "route_d1", 1))
                go(rs_[:, 0:8], rs_[:, 0:8], ACT.Exp).then_inc(sem["route_exp1"], 1)
                act.wait_ge(sem["route_d2"], rise(l, "route_d2", 1))
                go(rs_[:, 12:14], rs_[:, 12:14], ACT.Exp).then_inc(sem["route_exp2"], 1)
                for q in range(0, N_EXPERTS // 2, 2):
                    act.wait_ge(sem["cb_mm"], rise(l, "cb_mm", q + 1))
                    go(cb[:, 2 * q:2 * q + 2, :].rearrange("p e t -> p (e t)"), bank(q % 4), ACT.Copy).then_inc(sem["cb_act"], 1)
                act.sem_clear(chain_act)
                links.restart()

                def high(e, j, part, name, freed=None):
                    if part == 0:
                        act.wait_ge(slot_in[j], (l * ((HEAD_SLOTS + N_EXPERTS) // RING) + HEAD_SLOTS // RING + 1) * 16 + (e - j) * (16 // RING))
                    if freed:
                        act.wait_ge(sem[freed], rise(l, freed, e))
                    at = part * 2048
                    go(w_hi[:, at:at + 2048], ring[j][:, at:at + 2048], ACT.Copy).then_inc(sem[name], 1)

                def step(e, j, first=1, ahead=2):
                    if ahead > 0:
                        act.wait_ge(sem["gate_mm"], rise(l, "gate_mm", e + 2))
                        if first > 0:
                            act.wait_ge(sem["down_mm"], rise(l, "down_mm", e))
                        go(sg[:, (j + 1) % 2].rearrange("p f t -> p (f t)"), bank(4 + 2 * ((j + 1) % 2)), ACT.Silu).then_inc(sem["silu"], 1)
                    if ahead > 1:
                        high(e + 2, (j + 2) % RING, 0, "hi_gate", "gate_mm")
                        high(e + 2, (j + 2) % RING, 1, "hi_up", "up_mm")
                    if ahead > 0:
                        act.wait_ge(sem["act_dve"], rise(l, "act_dve", e + 2))
                        go(gated_hi[:, (j + 1) % 2].rearrange("p f t -> p (f t)"), sg[:, (j + 1) % 2].rearrange("p f t -> p (f t)"),
                           ACT.Copy).then_inc(sem["act_hi"], 1)
                        high(e + 1, (j + 1) % RING, 2, "hi_down", "down_mm" if first >= 0 else None)

                act.wait_ge(sem["route_mm"], rise(l, "route_mm", 1))
                go(h_hi, hT[:], ACT.Copy).then_inc(sem["h_hi"], 1)
                high(0, 0, 0, "hi_gate")
                high(0, 0, 1, "hi_up")
                step(-1, RING - 1, first=-1)
                step(0, 0, first=0)
                for e in range(1, RING):
                    step(e, e)
                with act.Fori(1, N_EXPERTS // RING - 1) as turn:
                    for j in range(RING):
                        step(turn * RING + j, j)
                for e in range(N_EXPERTS - RING, N_EXPERTS - 1):
                    step(e, e % RING, ahead=N_EXPERTS - 1 - e)

        @block.vector
        def _(dve):
            V = nc.vector
            tt, ts, stt, copy = V.tensor_tensor, V.tensor_scalar, V.scalar_tensor_tensor, V.tensor_copy
            dve.wait_ge(const_in, 48)
            V.memset(natm[:], 0.0).then_inc(sem["layer_done"], 1)
            with dve.Fori(0, DEPTH) as l:
                links = Links()
                dve.wait_ge(sem["layer_done"], rise(l, "layer_done", 1))
                dve.wait_ge(sem["param_dma"], rise(l, "param_dma", 16))
                tt(Q("nat_bias").rearrange("p (a c) -> p a c", c=GRID_W), Q("nat_bias").rearrange("p (a c) -> p a c", c=GRID_W),
                          bc(C("colmask").unsqueeze(1), 2 * HEADS, GRID_W), ALU.add).then_inc(chain_dve, 1)
                dve.wait_ge(chain_dve, links.next())

                def ada_columns(i, bank_out):
                    dve.wait_ge(sem["ada_tr"], rise(l, "ada_tr", i + 1))
                    m = slice(ADA_TILES * i, ADA_TILES * (i + 1))
                    tt(adaT[:, m, :], ps[:, bank_out, 0:2 * ADA_TILES].rearrange("p (m s) -> p m s", s=NS),
                       bc(Q("ada_b")[:, m].unsqueeze(2), ADA_TILES, NS), ALU.add).then_inc(sem["ada_dve"], 1)

                def norm_scale(n, at, name):
                    stt(scale1[:, n], adaT[:, at:at + KT, :], 1.0, bc(Q(name).unsqueeze(2), KT, NS), ALU.add, ALU.mult).then_inc(chain_dve, 1)
                    dve.wait_ge(chain_dve, links.next())

                for i in range(ADA_FIRST):
                    ada_columns(i, 5)
                dve.wait_ge(sem["ada_dve"], rise(l, "ada_dve", ADA_FIRST))
                norm_scale(0, 8, "norm_mix")

                def modulate(n):
                    dve.wait_ge(sem["norm_rs"], rise(l, "norm_rs", n))
                    tt(hT[:], xT[:], bc(rstd[:].unsqueeze(1), KT, TOK), ALU.mult).then_inc(sem["h_scaled"], 1)
                    dve.wait_ge(sem["h_scaled"], rise(l, "h_scaled", n))
                    which, sh = (0, 0) if n == 1 else (1, 24)
                    for k in range(4):
                        for s in range(NS):
                            t = hT[:, k, s * P:(s + 1) * P]
                            last = ts(t, t, scale1[:, which, k, s:s + 1], adaT[:, sh + k, s:s + 1], ALU.mult, ALU.add)
                    last.then_inc(sem["h_dve"], 1)

                modulate(1)
                dve.wait_ge(sem["zeroed"], rise(l, "zeroed", 1))
                for s in range(NS):
                    dve.wait_ge(sem["proj_mm"], rise(l, "proj_mm", 4 + s))
                    v_in = bank(proj_bank(3 + s)).rearrange("p (a i d) -> p a i d", i=2, d=HD)
                    v_out = vp[:, s].rearrange("p r j n -> p (r j) n")
                    copy(v_out[:, :, 0:HD], v_in[:, :, 0, :])
                    copy(v_out[:, :, P + HD:256], v_in[:, :, 1, :]).then_inc(sem["proj_dve"], 1)
                dve.wait_ge(sem["proj_mm"], rise(l, "proj_mm", 6))
                copy(gin, ps[:, proj_bank(5), 0:32].rearrange("p (s n) -> p s n", s=2)).then_inc(sem["proj_dve"], 1)
                dve.wait_ge(sem["proj_dve"], rise(l, "proj_dve", 3))
                tt(spx[:, 0:16].rearrange("p (s n) -> p s n", s=2), gin[:, :, 0:8], bc(Q("dt_bias").unsqueeze(1), 2, 8), ALU.add)
                gam = param[:, PARAM["gamma_cols"].start:PARAM["gamma_rows"].stop]
                ts(spx[:, 16:28], gam, -1.0, None, ALU.mult).then_inc(chain_dve, 1)
                dve.wait_ge(chain_dve, links.next())
                stt(spa, spx[:], -1.0, spx[:], ALU.mult, ALU.max).then_inc(sem["sp_in"], 1)

                def conv(out, inp, taps, tiles, at=0):
                    for tap in range(3):
                        for m in range(tiles):
                            k = taps[:, 3 * m + tap:3 * m + tap + 1]
                            t = inp[:, m, :, tap:tap + P]
                            o = out(m)
                            last = ts(o, t, k, None, ALU.mult) if tap == 0 else stt(o, t, k, o, ALU.mult, ALU.add)
                        if tap < 2:
                            last.then_inc(chain_dve, 1)
                            dve.wait_ge(chain_dve, links.next())
                    return last

                dve.wait_ge(sem["proj_act"], rise(l, "proj_act", 3))
                conv(lambda m: qkv[:, m, :].rearrange("p (s t) -> p s t", s=2), raw, Q("conv_gdn"), 6).then_inc(sem["conv_dve"], 1)
                dve.wait_ge(sem["sp_act"], rise(l, "sp_act", 1))
                stt(spx[:], spx[:], 0.0, spe, ALU.max, ALU.add).then_inc(chain_dve, 1)
                dve.wait_ge(chain_dve, links.next())
                stt(gdec[:], spx[:, 0:16].rearrange("p (s n) -> p s n", s=2), -1.0, bc(nega[:].unsqueeze(1), 2, 8), ALU.mult, ALU.mult)
                ts(lg[:], spx[:, 16:28], -1.0, None, ALU.mult)
                ts(beta[:], beta[:], 1.0, None, ALU.add).then_inc(chain_dve, 1)
                dve.wait_ge(chain_dve, links.next())
                V.reciprocal(beta[:], beta[:]).then_inc(chain_dve, 1)
                dve.wait_ge(chain_dve, links.next())
                for d in range(2):
                    last = ts(kdc[:, 4 * d:4 * d + 4], lg[:, 4 * d:4 * d + 4], C("idx")[:, d:d + 1], None, ALU.mult)
                last.then_inc(sem["gates_dve"], 1)
                dve.wait_ge(sem["proj_mm"], rise(l, "proj_mm", 13))
                copy(A("sb"), bank(proj_bank(12))).then_inc(sem["proj_dve"], 1)
                dve.wait_ge(sem["silu_act"], rise(l, "silu_act", 1))
                tt(norm[:, 0:1024], A("qkv")[:, 0:1024], A("qkv")[:, 0:1024], ALU.mult)
                dve.wait_ge(sem["proj_act"], rise(l, "proj_act", 5))
                tt(norm[:, 1024:2048], A("natqk"), A("natqk"), ALU.mult).then_inc(sem["qk_sq"], 1)
                dve.wait_ge(sem["proj_mm"], rise(l, "proj_mm", 15))
                dve.wait_ge(sem["proj_act"], rise(l, "proj_act", 10))
                tt(ub[:, :, :, 1:129].rearrange("p m s t -> p (m s) t"), bank(proj_bank(14)).rearrange("p (m t) -> p m t", m=4),
                   sxT.rearrange("p m s t -> p (m s) t"), ALU.mult).then_inc(sem["proj_dve"], 1)
                dve.wait_ge(sem["proj_dve"], rise(l, "proj_dve", 5))
                conv(lambda m: hT[:, 6 + m, :].rearrange("p (s t) -> p s t", s=2), ub, Q("conv_sc"), 2).then_inc(chain_dve, 1)
                dve.wait_ge(chain_dve, links.next())
                mix_sc = hT[:, 6:8, :].rearrange("p m t -> p (m t)")
                tt(mix_sc, mix_sc, A("sb"), ALU.mult).then_inc(sem["sc_dve"], 1)
                dve.wait_ge(sem["qk_rs"], rise(l, "qk_rs", 1))
                dve.wait_ge(sem["sc_dve"], rise(l, "sc_dve", 1))
                tt(A("qkv")[:, 0:1024], A("qkv")[:, 0:1024], norm[:, 0:1024], ALU.mult)
                stt(A("natqk")[:, 0:512], A("natqk")[:, 0:512], Q("q_norm"), norm[:, 1024:1536], ALU.mult, ALU.mult)
                stt(A("natqk")[:, 512:1024], A("natqk")[:, 512:1024], Q("k_norm"), norm[:, 1536:2048], ALU.mult, ALU.mult).then_inc(sem["qk_dve"], 1)
                ada_columns(ADA_FIRST, 6)
                dve.wait_ge(sem["rope_mm"], rise(l, "rope_mm", 1))
                dve.wait_ge(sem["qk_dve"], rise(l, "qk_dve", 1))
                rsin = norm[:, 0:512].rearrange("p (m t) -> p m t", m=4)
                tt(rsin, bank(4).rearrange("p (m t) -> p m t", m=4), bc(C("sin").unsqueeze(1), 4, P), ALU.mult)
                tt(retqk[:, :, P:TOK], retqk[:, :, P:TOK], bc(C("cos").unsqueeze(1), 4, P), ALU.mult).then_inc(chain_dve, 1)
                dve.wait_ge(chain_dve, links.next())
                tt(retqk[:, :, P:TOK], retqk[:, :, P:TOK], rsin, ALU.add).then_inc(sem["rope_dve"], 1)

                dve.wait_ge(sem["rope_dve"], rise(l, "rope_dve", 1))
                dve.wait_ge(sem["nat_mm"], rise(l, "nat_mm", 1))
                ts(nat_s[:, 0:512], bank(0), QK_SCALE, None, ALU.mult)
                stt(nat_s[:, 512:1024], bank(1), QK_SCALE, Q("nat_bias"), ALU.mult, ALU.add)
                ts(nat_s[:, 1024:1536], bank(2), QK_SCALE, None, ALU.mult).then_inc(chain_dve, 1)
                dve.wait_ge(chain_dve, links.next())
                V.tensor_reduce(natm[:], nat_s.rearrange("p (n k) -> p n k", k=P), AX.X, ALU.max).then_inc(chain_dve, 1)
                dve.wait_ge(chain_dve, links.next())
                tt(natm[:, 4:8], natm[:, 4:8], natm[:, 8:12], ALU.max).then_inc(chain_dve, 1)
                dve.wait_ge(chain_dve, links.next())
                ts(natm[:, 0:8], natm[:, 0:8], -1.0, None, ALU.mult).then_inc(sem["nat_max"], 1)
                dve.wait_ge(sem["nat_exp"], rise(l, "nat_exp", 1))
                tt(natsum[:, 4:8], natsum[:, 4:8], natsum[:, 8:12], ALU.add).then_inc(chain_dve, 1)
                dve.wait_ge(chain_dve, links.next())
                V.reciprocal(natsum[:, 0:8], natsum[:, 0:8]).then_inc(chain_dve, 1)
                dve.wait_ge(chain_dve, links.next())
                for n, r in enumerate((0, 4, 4)):
                    t = heads(nat_s[:, n * 512:(n + 1) * 512])
                    last = tt(t, t, bc(natsum[:, r:r + 4].unsqueeze(2), 4, P), ALU.mult)
                last.then_inc(sem["nat_p"], 1)

                dve.wait_ge(sem["ret_exp"], rise(l, "ret_exp", 1))
                stt(ef, ef, QK_SCALE, bc(upto[0].unsqueeze(1), HEADS, P), ALU.mult, ALU.mult)
                stt(eb, eb, QK_SCALE, bc(upto[1].unsqueeze(1), HEADS, P), ALU.mult, ALU.mult).then_inc(chain_dve, 1)
                dve.wait_ge(chain_dve, links.next())
                tt(ef, ef, eb, ALU.add).then_inc(chain_dve, 1)
                dve.wait_ge(chain_dve, links.next())
                tt(qx, qx, bc(retqk[:, 0:2, P:TOK].unsqueeze(1), 2, 2, P), ALU.mult)
                dve.wait_ge(sem["ret_mm"], rise(l, "ret_mm", 1))
                dve.wait_ge(sem["nat_tr"], rise(l, "nat_tr", 1))
                tt(ret_a.rearrange("p s h c -> p s (h c)"), ps[:, 6:8, :],
                   bc(ef.rearrange("p h c -> p (h c)").unsqueeze(1), 2, 512), ALU.mult).then_inc(sem["ret_a"], 1)
                dve.wait_ge(sem["ret_kt"], rise(l, "ret_kt", 1))
                for d in range(2):
                    last = tt(ret_kd[:, d].rearrange("p (h n) -> p h n", h=HEADS), ps[:, 5, 0:256].rearrange("p (h n) -> p h n", h=HEADS),
                              bc(kdc[:, 4 * d:4 * d + 4].unsqueeze(2), HEADS, HD), ALU.mult)
                last.then_inc(sem["ret_kd"], 1)
                dve.wait_ge(sem["ret_o"], rise(l, "ret_o", 1))
                rog, rsq = ef.rearrange("p h c -> p (h c)"), eb.rearrange("p h c -> p (h c)")
                copy(rog, bank(4)).then_inc(sem["ret_og"], 1)
                dve.wait_ge(sem["ret_sf"], rise(l, "ret_sf", 1))

                def states(out, first):
                    for i in range(2):
                        lo = slice(64 * i, 64 * i + 64)
                        last = copy(out[lo], ps[lo, first:first + 2, :].rearrange("p d (j n) -> p d j n", j=2)[:, :, :, 192 * i:192 * i + HD])
                    return last

                states(state, 0).then_inc(sem["ret_st"], 1)
                dve.wait_ge(sem["ret_mean"], rise(l, "ret_mean", 1))
                stt(rog, bank(2), -1.0 / HD, rog, ALU.mult, ALU.add).then_inc(chain_dve, 1)
                dve.wait_ge(chain_dve, links.next())
                tt(rsq, rog, rog, ALU.mult).then_inc(sem["ret_sq"], 1)
                dve.wait_ge(sem["ret_rs"], rise(l, "ret_rs", 1))
                tt(rog, rog, qx.rearrange("p d j c -> p (d j c)"), ALU.mult).then_inc(chain_dve, 1)
                dve.wait_ge(chain_dve, links.next())
                tt(hT[:, 2:4, :].rearrange("p m t -> p (m t)"), rog, zr, ALU.mult).then_inc(sem["ret_out"], 1)
                dve.wait_ge(kv_out, l * 48 + 48)
                dve.wait_ge(sem["ret_out"], rise(l, "ret_out", 1))
                dve.wait_ge(sem["nat_out"], rise(l, "nat_out", 1))
                copy(qdec.rearrange("p d j (i n) -> p (d j i) n", i=2), bc(gdec[:, 1, :].unsqueeze(2), 8, HD)).then_inc(sem["qd_g"], 1)

                for s in range(NS):
                    dve.wait_ge(sem["gr_mm"], rise(l, "gr_mm", s + 1))
                    for d in range(2):
                        ts(group(d, 0).rearrange("p h c -> p (h c)"), bank(2 + d), 0.0, None, ALU.min).then_inc(sem["gr_min"], 1)
                    for d in range(2):
                        dve.wait_ge(sem["gr_exp"], rise(l, "gr_exp", 2 * s + d + 1))
                        tt(group(d, 0), group(d, 0), bc(upto[d].unsqueeze(1), HEADS, P), ALU.mult).then_inc(chain_dve, 1)
                        dve.wait_ge(chain_dve, links.next())
                        m = group(d, 0).rearrange("p (j i) c -> p j (i c)", j=2)
                        tt(group(d, 1).rearrange("p (j i) c -> p j (i c)", j=2), ps[:, 0:2, 0:256], m, ALU.mult)
                        tt(group(d, 2).rearrange("p (j i) c -> p j (i c)", j=2), ps[:, 0:2, 256:512], m, ALU.mult).then_inc(chain_dve, 1)
                        dve.wait_ge(chain_dve, links.next())
                        lt = group(d, 2).rearrange("p h c -> p (h c)")
                        last = tt(lt, lt, bank(4 + d), ALU.mult)
                        if d == 0:
                            last.then_inc(chain_dve, 1)
                            dve.wait_ge(chain_dve, links.next())
                    last.then_inc(sem["gr_dec"], 1)
                    dve.wait_ge(sem["vt_act"], rise(l, "vt_act", s + 1))
                    dve.wait_ge(sem["gcol_exp"], rise(l, "gcol_exp", s + 1))
                    dve.wait_ge(sem["ks_mm"], rise(l, "ks_mm", s + 1))
                    vh = vtok[:, s, :].rearrange("p (h n) -> p h n", h=HEADS)
                    for d in range(2):
                        zd = z[:, d, :].rearrange("p (h n) -> p h n", h=HEADS)
                        bcol = bc(beta[:, s, 4 * d:4 * d + 4].unsqueeze(2), HEADS, HD)
                        if s == 0:
                            last = tt(zd, vh, bcol, ALU.mult)
                            continue
                        ks = ps[:, 6, 256 * d:256 * d + 256].rearrange("p (h n) -> p h n", h=HEADS)
                        tt(zd, ks, bc(egc[:, 4 * d:4 * d + 4].unsqueeze(2), HEADS, HD), ALU.mult).then_inc(chain_dve, 1)
                        dve.wait_ge(chain_dve, links.next())
                        tt(zd, vh, zd, ALU.subtract).then_inc(chain_dve, 1)
                        dve.wait_ge(chain_dve, links.next())
                        last = tt(zd, zd, bcol, ALU.mult)
                    last.then_inc(sem["z_dve"], 1)
                    if s == 0:
                        for d in range(2):
                            last = tt(kdg[:, d, :].rearrange("p (h n) -> p h n", h=HEADS), ps[:, 7, 256:512].rearrange("p (h n) -> p h n", h=HEADS),
                                      bc(egc[:, 8 + 4 * d:12 + 4 * d].unsqueeze(2), HEADS, HD), ALU.mult)
                        last.then_inc(sem["kd_dve"], 1)
                    else:
                        dve.wait_ge(sem["qd_exp"], rise(l, "qd_exp", 1))
                        tt(qdec, qdec, bc(qkv[:, 0:2, P:TOK].unsqueeze(1), 2, 2, P), ALU.mult).then_inc(sem["qd_dve"], 1)
                    for b in range(LEVELS):
                        for g in range(2):
                            n = (s * LEVELS + b) * 2 + g + 1
                            t, t_t = group(g, 3), group(g, 4)
                            if b == 0:
                                dve.wait_ge(sem["inv_dmm"], rise(l, "inv_dmm", n))
                                tt(t, heads(bank(2 + g)), bc(ident.unsqueeze(1), HEADS, P), ALU.add)
                                tt(t_t, group(g, 6), bc(ident.unsqueeze(1), HEADS, P), ALU.add).then_inc(sem["inv_upd"], 1)
                                continue
                            dve.wait_ge(sem["inv_umm"], rise(l, "inv_umm", (s * (LEVELS - 1) + b - 1) * 2 + g + 1))
                            dve.wait_ge(sem["inv_upd"], rise(l, "inv_upd", n - 2))
                            if b < LEVELS - 1:
                                tt(t, t, heads(bank(4 + g)), ALU.add)
                            tt(t_t, t_t, heads(bank(g)), ALU.add).then_inc(sem["inv_upd"], 1)
                        piece = s * (LEVELS - 1) + b - 1
                        if b > 0 and piece % 3 == 2:
                            ada_columns(ADA_FIRST + 1 + piece // 3, 6)
                    dve.wait_ge(sem["vnp_zero"], rise(l, "vnp_zero", 1))
                    for g in range(2):
                        dve.wait_ge(sem["vn_mm"], rise(l, "vn_mm", 2 * s + g + 1))
                        vn = ps[:, 2 + g, 0:256].rearrange("p (j i n) -> p j i n", j=2, i=2)
                        pad = group(g, 7).rearrange("p (j i) c -> p j i c", j=2)
                        copy(pad[:, :, 0, 0:HD], vn[:, :, 0, :])
                        copy(pad[:, :, 1, HD:P], vn[:, :, 1, :]).then_inc(sem["vn_dve"], 1)
                    dve.wait_ge(sem["go_mm"], rise(l, "go_mm", s + 1))
                    copy(og[:, :, s, :], ps[:, 6, 0:256].rearrange("p (j c) -> p j c", j=2)).then_inc(sem["go_dve"], 1)
                    if s == 0:
                        dve.wait_ge(sem["gs_mm"], rise(l, "gs_mm", 1))
                        dve.wait_ge(state_out, l * 32 + 16)
                        states(state, 4).then_inc(sem["gs_st"], 1)
                dve.wait_ge(sem["gn_rs"], rise(l, "gn_rs", 1))
                gn = group(0, 3).rearrange("p h c -> p (h c)")
                stt(gn, og.rearrange("p j s c -> p (j s c)"), Q("gdn_norm"), group(0, 4).rearrange("p h c -> p (h c)"), ALU.mult, ALU.mult).then_inc(chain_dve, 1)
                dve.wait_ge(chain_dve, links.next())
                tt(hT[:, 0:2, :].rearrange("p m t -> p (m t)"), gn, zg, ALU.mult).then_inc(sem["gn_out"], 1)

                def residual(gate):
                    for f in range(KT):
                        for s in range(NS):
                            t = xT[:, f, s * P:(s + 1) * P]
                            last = stt(t, ps[:, f // 2, (f % 2) * TOK + s * P:(f % 2) * TOK + (s + 1) * P],
                                       adaT[:, gate + f, s:s + 1], t, ALU.mult, ALU.add)
                    return last

                dve.wait_ge(sem["out_mm"], rise(l, "out_mm", 3))
                residual(16).then_inc(sem["res_dve"], 1)
                dve.wait_ge(sem["ada_dve"], rise(l, "ada_dve", ADA_SLOTS))
                norm_scale(1, 32, "norm_ffn")
                dve.wait_ge(sem["res_dve"], rise(l, "res_dve", 1))
                modulate(2)

                dve.wait_ge(sem["route_mm"], rise(l, "route_mm", 1))
                gd, tmp4, oh4 = (rs_[:, a:a + 8].rearrange("p (s n) -> p s n", s=2) for a in (0, 20, 28))
                els, oh1, oh2, tmp8, c8 = (rs_[:, a:a + 16].rearrange("p (s n) -> p s n", s=2) for a in (36, 52, 68, 84, 100))
                gm, gs, e2, m1, m2, tw, gw, pick = (rs_[:, a:a + 2] for a in (8, 10, 12, 14, 16, 18, 116, 118))
                prio4, prio8 = C("prio")[:, 4:8], C("prio")
                dve.wait_ge(state_out, l * 32 + 32)
                tt(rt, ps[:, 0, 0:128].rearrange("p (s n) -> p s n", s=2)[:, :, 0:ROUTER], bc(Q("router_b").unsqueeze(1), 2, ROUTER), ALU.add).then_inc(chain_dve, 1)
                dve.wait_ge(chain_dve, links.next())
                V.tensor_reduce(gm, rt[:, :, 0:4], AX.X, ALU.max).then_inc(chain_dve, 1)
                dve.wait_ge(chain_dve, links.next())
                tt(gd, rt[:, :, 0:4], bc(gm.unsqueeze(2), 2, 4), ALU.subtract).then_inc(chain_dve, 1)
                dve.wait_ge(chain_dve, links.next())
                stt(tmp4, gd, 0.0, bc(prio4.unsqueeze(1), 2, 4), ALU.is_ge, ALU.mult).then_inc(sem["route_d1"], 1)
                dve.wait_ge(sem["route_d1"], rise(l, "route_d1", 1))
                V.tensor_reduce(pick, tmp4, AX.X, ALU.max).then_inc(chain_dve, 1)
                dve.wait_ge(chain_dve, links.next())
                tt(oh4, tmp4, bc(pick.unsqueeze(2), 2, 4), ALU.is_equal).then_inc(chain_dve, 1)
                dve.wait_ge(chain_dve, links.next())
                by_group = comb[:].rearrange("p s (g n) -> p s g n", g=N_GROUPS)
                tt(by_group, rt[:, :, 4:ROUTER].rearrange("p s (g n) -> p s g n", g=N_GROUPS),
                          bc(oh4.unsqueeze(3), 2, N_GROUPS, PER_GROUP), ALU.mult).then_inc(chain_dve, 1)
                dve.wait_ge(chain_dve, links.next())
                V.tensor_reduce(els, by_group.rearrange("p s g n -> p s n g"), AX.X, ALU.add).then_inc(chain_dve, 1)
                dve.wait_ge(chain_dve, links.next())
                for n, (m, oh) in enumerate(((m1, oh1), (m2, oh2))):
                    V.tensor_reduce(m, els, AX.X, ALU.max).then_inc(chain_dve, 1)
                    dve.wait_ge(chain_dve, links.next())
                    for s in range(NS):
                        last = stt(tmp8[:, s], els[:, s], m[:, s:s + 1], prio8, ALU.is_equal, ALU.mult)
                    last.then_inc(chain_dve, 1)
                    dve.wait_ge(chain_dve, links.next())
                    V.tensor_reduce(pick, tmp8, AX.X, ALU.max).then_inc(chain_dve, 1)
                    dve.wait_ge(chain_dve, links.next())
                    tt(oh, tmp8, bc(pick.unsqueeze(2), 2, PER_GROUP), ALU.is_equal).then_inc(chain_dve, 1)
                    dve.wait_ge(chain_dve, links.next())
                    if n == 0:
                        stt(els, oh1, -BIG, els, ALU.mult, ALU.add).then_inc(chain_dve, 1)
                        dve.wait_ge(chain_dve, links.next())
                tt(e2, m2, m1, ALU.subtract).then_inc(sem["route_d2"], 1)
                dve.wait_ge(sem["route_exp1"], rise(l, "route_exp1", 1))
                V.tensor_reduce(gs, gd, AX.X, ALU.add).then_inc(chain_dve, 1)
                dve.wait_ge(chain_dve, links.next())
                V.reciprocal(gw, gs).then_inc(chain_dve, 1)
                dve.wait_ge(chain_dve, links.next())
                dve.wait_ge(sem["route_exp2"], rise(l, "route_exp2", 1))
                ts(tw, e2, 1.0, None, ALU.add).then_inc(chain_dve, 1)
                dve.wait_ge(chain_dve, links.next())
                V.reciprocal(tw, tw).then_inc(chain_dve, 1)
                dve.wait_ge(chain_dve, links.next())
                tt(tw, tw, gw, ALU.mult).then_inc(chain_dve, 1)
                dve.wait_ge(chain_dve, links.next())
                tt(e2, e2, tw, ALU.mult).then_inc(chain_dve, 1)
                dve.wait_ge(chain_dve, links.next())
                tt(oh1, oh1, bc(tw.unsqueeze(2), 2, PER_GROUP), ALU.mult)
                tt(oh2, oh2, bc(e2.unsqueeze(2), 2, PER_GROUP), ALU.mult).then_inc(chain_dve, 1)
                dve.wait_ge(chain_dve, links.next())
                tt(c8, oh1, oh2, ALU.add).then_inc(chain_dve, 1)
                dve.wait_ge(chain_dve, links.next())
                dve.sem_clear(chain_dve)
                links.restart()
                tt(by_group, bc(oh4.unsqueeze(3), 2, N_GROUPS, PER_GROUP), bc(c8.unsqueeze(2), 2, N_GROUPS, PER_GROUP), ALU.mult).then_inc(sem["route_dve"], 1)
                for q in range(1, N_EXPERTS // 2, 2):
                    dve.wait_ge(sem["cb_mm"], rise(l, "cb_mm", q + 1))
                    copy(cb[:, 2 * q:2 * q + 2, :].rearrange("p e t -> p (e t)"), bank(q % 4)).then_inc(sem["cb_dve"], 1)
                dve.wait_ge(sem["h_hi"], rise(l, "h_hi", 1))
                tt(h_lo, hT[:], h_hi, ALU.subtract).then_inc(sem["h_lo"], 1)

                def low(e, j, part, name, made):
                    dve.wait_ge(sem[made], rise(l, made, e + 1))
                    at = part * 2048
                    tt(ring_r[j][:, at:at + 2048], ring[j][:, at:at + 2048], w_hi[:, at:at + 2048], ALU.subtract).then_inc(sem[name], 1)

                def step(e, j, ahead=2):
                    if ahead > 1:
                        low(e + 2, (j + 2) % RING, 0, "lo_gate", "hi_gate")
                    if ahead > 0:
                        dve.wait_ge(sem["silu"], rise(l, "silu", e + 2))
                        dve.wait_ge(sem["up_mm"], rise(l, "up_mm", e + 2))
                        b = (j + 1) % 2
                        t = sg[:, b].rearrange("p f t -> p (f t)")
                        tt(t, t, bank(5 + 2 * b), ALU.mult).then_inc(sem["prod"], 1)
                        dve.wait_ge(sem["prod"], rise(l, "prod", e + 2))
                        weight = arena[:, bass.ds((e + 1) * TOK, TOK)]
                        tt(sg[:, b], sg[:, b], bc(weight.unsqueeze(1), 2, TOK), ALU.mult).then_inc(sem["act_dve"], 1)
                    if ahead > 1:
                        low(e + 2, (j + 2) % RING, 1, "lo_up", "hi_up")
                    if ahead > 0:
                        dve.wait_ge(sem["act_hi"], rise(l, "act_hi", e + 2))
                        tt(sg_lo[:, b], sg[:, b], gated_hi[:, b], ALU.subtract).then_inc(sem["act_lo"], 1)
                        low(e + 1, (j + 1) % RING, 2, "lo_down", "hi_down")

                low(0, 0, 0, "lo_gate", "hi_gate")
                low(0, 0, 1, "lo_up", "hi_up")
                dve.wait_ge(const_in, 48)
                dve.wait_ge(sem["cb_act"], rise(l, "cb_act", 8))
                dve.wait_ge(sem["cb_dve"], rise(l, "cb_dve", 8))
                for e in range(-1, RING):
                    step(e, e % RING)
                with dve.Fori(1, N_EXPERTS // RING - 1) as turn:
                    for j in range(RING):
                        step(turn * RING + j, j)
                for e in range(N_EXPERTS - RING, N_EXPERTS - 1):
                    step(e, e % RING, ahead=N_EXPERTS - 1 - e)
                dve.wait_ge(sem["down_mm"], rise(l, "down_mm", N_EXPERTS))
                residual(40).then_inc(sem["layer_done"], 1)

        @block.gpsimd
        def _(pool):
            G = nc.gpsimd
            with pool.Fori(0, DEPTH) as l:
                pool.wait_ge(const_in, 48)
                pool.wait_ge(sem["layer_done"], rise(l, "layer_done", 1))
                zeros = C("zeros")
                G.tensor_tensor(raw[:, :, :, 0:130:129].rearrange("p m s t -> p (m s) t"), zeros[:, 0:24].rearrange("p (a b) -> p a b", b=2),
                                zeros[:, 0:24].rearrange("p (a b) -> p a b", b=2), ALU.mult)
                G.memset(A("vp"), 0.0)
                G.memset(ub[:, :, :, 0:130:129].rearrange("p m s t -> p (m s) t"), 0.0)
                G.memset(A("gpad"), 0.0)
                G.memset(arena[:, ARENA["npad"].start:ARENA["rpad"].stop], 0.0).then_inc(sem["zeroed"], 1)
                pool.wait_ge(const_in, 48)
                pool.wait_ge(sem["zeroed"], rise(l, "zeroed", 1))
                pool.wait_ge(const_in, 48)
                pool.wait_ge(sem["qk_dve"], rise(l, "qk_dve", 1))
                G.tensor_copy(gpad[64:P, :, :, 1, :].rearrange("p t s c -> p (t s) c"),
                              qkv[64:P, 0:4, :].rearrange("p m (s c) -> p (m s) c", s=2))
                G.tensor_copy(npad[64:P, :, :, 1, :].rearrange("p j s c -> p (j s) c"),
                              natqk[64:P, 2:4, :].rearrange("p m (s c) -> p (m s) c", s=2)).then_inc(sem["pad_pool"], 1)
                pool.wait_ge(const_in, 48)
                pool.wait_ge(sem["rope_dve"], rise(l, "rope_dve", 1))
                G.tensor_copy(rpad[64:P, :, :, 1, :].rearrange("p j s c -> p (j s) c"),
                              retqk[64:P, 0:2, :].rearrange("p m (s c) -> p (m s) c", s=2)).then_inc(sem["rpad_pool"], 1)
                out = dst["nkT"][bass.ds(l, 1)].rearrange("o p j c -> (o p) j c")
                pool.dma_start(out, natqk[:, 2:4, 0:P]).then_inc(kv_out, 16)
                for i in range(2):
                    out = dst["nv"][bass.ds(l, 1)].rearrange("o p j i d -> (o p) j i d")[:, :, i, :]
                    pool.dma_start(out, vp[:, 0, 1, :, 192 * i:192 * i + HD]).then_inc(kv_out, 16)
                pool.wait_ge(const_in, 48)
                pool.wait_ge(sem["ret_st"], rise(l, "ret_st", 1))
                pool.dma_start(dst["s_ret"][bass.ds(l, 1)].rearrange("o p n -> (o p) n"),
                               state[:].rearrange("p d j n -> p (d j n)")).then_inc(state_out, 16)
                pool.wait_ge(const_in, 48)
                pool.wait_ge(sem["ret_out"], rise(l, "ret_out", 1))
                pool.wait_ge(kv_out, l * 48 + 48)
                pool.wait_ge(const_in, 48)
                pool.wait_ge(sem["nat_out"], rise(l, "nat_out", 1))
                G.tensor_tensor(group(0, 7), bc(zeros.unsqueeze(1), HEADS, P), bc(zeros.unsqueeze(1), HEADS, P), ALU.mult)
                G.memset(group(1, 7).rearrange("p h c -> p (h c)"), 0.0).then_inc(sem["vnp_zero"], 1)
                for s in range(NS):
                    pool.wait_ge(const_in, 48)
                    pool.wait_ge(sem["gr_dec"], rise(l, "gr_dec", s + 1))
                    for b in range(LEVELS):
                        for g in range(2):
                            n = (s * LEVELS + b) * 2 + g + 1
                            if n > 2:
                                pool.wait_ge(const_in, 48)
                                pool.wait_ge(sem["inv_upd"], rise(l, "inv_upd", n - 2))
                            G.tensor_tensor(group(g, 6), group(g, 2), bc(levels[:, g, b, :].unsqueeze(1), HEADS, P), ALU.mult)\
                             .then_inc(sem["inv_c"], 1)
                    if s == 0:
                        pool.wait_ge(const_in, 48)
                        pool.wait_ge(sem["gs_st"], rise(l, "gs_st", 1))
                        pool.dma_start(dst["s_gdn"][bass.ds(l, 1)].rearrange("o p n -> (o p) n"),
                                       state[:].rearrange("p d j n -> p (d j n)")).then_inc(state_out, 16)
                pool.wait_ge(state_out, l * 32 + 32)


def constants():
    c = np.zeros((P, CONST_W), np.float32)
    t = np.arange(P)
    k, m = t[:, None], t[None, :]

    def put(name, a):
        c[:, CONST[name]] = a

    put("ident", k == m)
    put("ones", 1.0)
    put("blockones", k // HD == m // HD)
    put("upto_f", k <= m)
    put("upto_b", k >= m)
    put("negupto_f", -1.0 * (k <= m))
    put("negupto_b", -1.0 * (k >= m))
    put("after_f", k > m)
    put("after_b", k < m)
    half = HD // 4
    put("rot", np.where(m % (2 * half) < half, -1.0 * (k == m + half), 1.0 * (k == m - half)))
    freq = np.float32(10000.0) ** (-np.arange(half, dtype=np.float32) / np.float32(half))
    pos = np.where((t % HD)[:, None] < HD // 2, (t // GRID_W)[None, :], (t % GRID_W)[None, :]).astype(np.float32)
    angle = pos * freq[t % half][:, None]
    put("cos", np.cos(angle))
    put("sin", np.sin(angle))
    put("lag_f", np.maximum(m - k, 0))
    put("lag_b", np.maximum(k - m, 0))
    put("cross_f", np.broadcast_to(m + 1.0, (P, P)))
    put("cross_b", np.broadcast_to(P - 1.0 * m, (P, P)))
    col = t[:GRID_W]
    c0 = np.clip(col - WIN_COLS // 2, 0, GRID_W - WIN_COLS)
    inside = (col[None, :] >= c0[:, None]) & (col[None, :] < c0[:, None] + WIN_COLS)
    put("colmask", np.tile(np.where(inside, 0.0, -BIG), (P // GRID_W, 1)))
    put("idx", np.stack([P - 1 - t, t], 1))
    put("prio", np.arange(PER_GROUP, 0, -1))
    lv = np.zeros((P, 2, LEVELS, P), np.float32)
    for b in range(LEVELS):
        size = 2 ** b
        same = k // (2 * size) == m // (2 * size)
        lv[:, 0, b] = -1.0 * (same & (k // size % 2 == 0) & (m // size % 2 == 1))
        lv[:, 1, b] = -1.0 * (same & (k // size % 2 == 1) & (m // size % 2 == 0))
    put("levels", lv.reshape(P, -1))
    return c


def kernel(x_prompt, x_sample, state_gdn, state_ret, cache_nat_k, cache_nat_v, c, c_ctx,
           ada_w, ada_b, norm_mix_w, norm_ffn_w, w_in, gdn_conv_w, gdn_a_log, gdn_dt_bias, gdn_norm_w,
           ret_gamma_logit, nat_q_norm_w, nat_k_norm_w, nat_rpb, sc_conv_w, w_out,
           router_group_w, router_group_b, router_expert_w, router_expert_b,
           moe_w_gate, moe_w_up, moe_w_down):
    import concourse.bacc as _bacc
    from concourse.bass_utils import run_bass_kernel_spmd as _run

    A = np.asarray

    def feat(a):
        a = A(a)
        return np.swapaxes(a.reshape(*a.shape[:-1], -1, P), -1, -2)

    def rows(a):
        a = A(a)
        return np.moveaxis(a.reshape(*a.shape[:-2], -1, P, a.shape[-1]), -3, -2)

    x = np.stack([A(x_prompt)[0], A(x_sample)[0]])
    xT = np.ascontiguousarray(x.reshape(NS, P, KT, P).transpose(3, 2, 0, 1)).reshape(P, KT, TOK)
    condT = np.ascontiguousarray(feat(np.stack([A(c_ctx), A(c)[0]])).transpose(1, 2, 0))

    ada = np.ascontiguousarray(rows(ada_w).reshape(DEPTH, P, KT, ADA_SLOTS, 768).transpose(0, 3, 1, 2, 4)).reshape(DEPTH, ADA_SLOTS, P, SLOT)
    wi = rows(w_in)
    sizes = (768, 256, 8, 8, 768, 256, 768, 768)
    at = np.concatenate([[0], np.cumsum(sizes)])
    a_qkv, a_z, a_dec, a_beta, r_qkv, r_g, n_qkv, s_bcx = (wi[..., at[i]:at[i + 1]] for i in range(8))
    w_feat = np.stack([
        a_qkv,
        np.concatenate([n_qkv[..., :512], r_g], -1),
        np.concatenate([r_qkv[..., :512], a_z], -1),
        np.concatenate([s_bcx[..., :256], s_bcx[..., 512:], s_bcx[..., 256:512]], -1)], 1).reshape(DEPTH, 4, P, SLOT)
    w_tok = np.concatenate([a_dec, a_beta, r_qkv[..., 512:], n_qkv[..., 512:]], -1).reshape(DEPTH, P, KT * TOKCOLS)
    wo = rows(w_out)
    edge = np.concatenate([[0], np.cumsum(OUT_TILES)]) * P
    w_o = np.concatenate([wo[..., edge[i]:edge[i + 1]].reshape(DEPTH, P, -1) for i in range(OUT_SLOTS)], -1)
    moe = np.concatenate([rows(moe_w_gate).reshape(DEPTH, N_EXPERTS, P, -1), rows(moe_w_up).reshape(DEPTH, N_EXPERTS, P, -1),
                          rows(moe_w_down).reshape(DEPTH, N_EXPERTS, P, -1)], -1)

    par = np.zeros((DEPTH, P, PARAM_W), np.float32)

    def put(name, a):
        par[:, :, PARAM[name]] = a

    def everywhere(a):
        return np.broadcast_to(A(a).reshape(DEPTH, 1, -1), (DEPTH, P, A(a)[0].size))

    def pair(a):
        return np.concatenate([A(a), A(a)], 1)[:, :, None]

    put("norm_mix", feat(norm_mix_w))
    put("norm_ffn", feat(norm_ffn_w))
    put("ada_b", feat(ada_b))
    put("conv_gdn", feat(gdn_conv_w).transpose(0, 2, 3, 1).reshape(DEPTH, P, -1))
    put("conv_sc", feat(sc_conv_w).transpose(0, 2, 3, 1).reshape(DEPTH, P, -1))
    put("gdn_norm", pair(gdn_norm_w))
    put("q_norm", pair(nat_q_norm_w))
    put("k_norm", pair(nat_k_norm_w))
    put("dt_bias", everywhere(gdn_dt_bias))
    put("a_log", everywhere(gdn_a_log))
    put("gamma_cols", everywhere(ret_gamma_logit))
    put("gamma_rows", np.repeat(A(ret_gamma_logit).reshape(DEPTH, 2, 2, 2).transpose(0, 3, 1, 2).reshape(DEPTH, 2, 4), HD, 1))
    put("router_b", np.concatenate([everywhere(router_group_b), everywhere(router_expert_b)], -1))
    put("router_w", np.concatenate([rows(router_group_w), rows(router_expert_w)], -1).reshape(DEPTH, P, -1))
    r = np.arange(P) // GRID_W
    q = np.arange(P) % GRID_W
    i, cc = np.arange(2), np.arange(GRID_W)
    ri = i[None, :, None] - r[:, None, None] + WIN_ROWS - 1
    ci = np.clip(cc[None, None, :] - q[:, None, None], -(WIN_COLS - 1), WIN_COLS - 1) + WIN_COLS - 1
    put("nat_bias", A(nat_rpb)[:, :, ri, ci].transpose(0, 2, 1, 3, 4).reshape(DEPTH, P, -1))
    ck = np.zeros((DEPTH, 2, HD, HEADS, P), np.float32)
    cv = np.zeros((DEPTH, P, HEADS, 2, HD), np.float32)
    states = []
    for h in range(HEADS):
        ck[:, h % 2, :, h] = A(cache_nat_k)[0, :, :, h].transpose(0, 2, 1)
        cv[:, :, h, h % 2] = A(cache_nat_v)[0, :, :, h]
    for st in (state_gdn, state_ret):
        b = np.zeros((DEPTH, 2, HD, 2, 2, 2, HD), np.float32)
        for h in range(HEADS):
            b[:, h % 2, :, :, h // 2, h % 2] = A(st)[0, :, :, h].transpose(0, 2, 1, 3)
        states.append(b.reshape(DEPTH, P, -1))
    put("ck", ck.reshape(DEPTH, P, -1))
    put("cv", cv.reshape(DEPTH, P, -1))
    put("s_gdn", states[0])
    put("s_ret", states[1])

    nc = _bacc.Bacc("TRN2", target_bir_lowering=False, num_devices=1)
    arrays = dict(xT=xT, condT=condT, const=constants(), param=par, ada_w=ada, w_feat=w_feat, w_tok=w_tok, w_out=w_o, moe=moe)
    arrays = {n: np.ascontiguousarray(a) for n, a in arrays.items()}
    src = {n: nc.dram_tensor(f"in_{n}", list(a.shape), F32, kind="ExternalInput").ap() for n, a in arrays.items()}
    outs = dict(yT=(P, KT, TOK), nkT=(DEPTH, P, 2, P), nv=(DEPTH, P, 2, 2, HD), s_ret=(DEPTH, P, 4 * HD), s_gdn=(DEPTH, P, 4 * HD))
    dst = {n: nc.dram_tensor(f"out_{n}", list(shape), F32, kind="ExternalOutput").ap() for n, shape in outs.items()}
    build_trunk(nc, src, dst)
    got = _run(nc, [{f"in_{n}": a for n, a in arrays.items()}], core_ids=[0]).results[0]

    y = np.asarray(got["out_yT"]).reshape(P, KT, NS, P).transpose(2, 3, 1, 0).reshape(NS, P, D_MODEL)

    def state(a):
        return np.asarray(a).reshape(DEPTH, 2, HD, 2, 2, HD).transpose(0, 3, 4, 1, 2, 5).reshape(1, DEPTH, 2, HEADS, HD, HD)

    nk = np.asarray(got["out_nkT"]).reshape(DEPTH, 2, HD, 2, P).transpose(0, 4, 3, 1, 2).reshape(1, DEPTH, P, HEADS, HD)
    nv = np.asarray(got["out_nv"]).reshape(1, DEPTH, P, HEADS, HD)
    return (np.ascontiguousarray(y[0:1]), np.ascontiguousarray(y[1:2]), np.ascontiguousarray(state(got["out_s_gdn"])),
            np.ascontiguousarray(state(got["out_s_ret"])), np.ascontiguousarray(nk), np.ascontiguousarray(nv))
```

```python
import math
from contextlib import ExitStack

import numpy as np

import concourse.bass as bass
from concourse import mybir

F32 = mybir.dt.float32
I32 = mybir.dt.int32
F32R = mybir.dt.float32r
ACT = mybir.ActivationFunctionType
ALU = mybir.AluOpType
AX = mybir.AxisListType

P = 128
D_MODEL, DEPTH = 1024, 2
KT = D_MODEL // P
NS = 2
TOK = NS * P
HEADS, HD = 4, 64
GRID_W, WIN_ROWS, WIN_COLS = 64, 8, 16
N_GROUPS, PER_GROUP, FF = 4, 8, 256
N_EXPERTS = N_GROUPS * PER_GROUP
ROUTER = N_GROUPS + N_EXPERTS
EPS = 1e-6
BIG = 1e30
QK_SCALE = HD ** -0.5
LEVELS = 7

RING, SLOT = 4, 6144
ADA_SLOTS, IN_SLOTS, OUT_SLOTS = 8, 5, 3
HEAD_SLOTS = ADA_SLOTS + IN_SLOTS + OUT_SLOTS
ADA_TILES = 6
ADA_FIRST = 3


ADA_UNITS = ADA_TILES * KT


def ada_piece(s, level):
    own = ADA_FIRST + (2 if s == 0 else 4)
    if level < 0:
        return own, 0, 2 * ADA_UNITS // 3
    if level == 0:
        return own, 2 * ADA_UNITS // 3, ADA_UNITS // 3
    if s == 0:
        return ADA_FIRST + 3, (level - 1) * (ADA_UNITS // 6), ADA_UNITS // 6
    return None, 0, 0


def ada_load(i):
    return i if i < ADA_FIRST else i + IN_SLOTS


def in_load(i):
    return ADA_FIRST + i


def out_load(i):
    return ADA_SLOTS + IN_SLOTS + i


TOKCOLS = 16 + 2 * HEADS * HD
OUT_TILES = (4, 2, 2)
assert HEAD_SLOTS % RING == 0 and N_EXPERTS % RING == 0


def layout(*parts):
    at, out = 0, {}
    for name, width in parts:
        out[name] = slice(at, at + width)
        at += width
    return out, at


CONST, CONST_W = layout(
    ("ident", P), ("zeros", P), ("ones", P), ("blockones", P), ("upto_f", P), ("upto_b", P), 
    ("after_f", P), ("after_b", P), ("rot", P), ("cos", P), ("sin", P), ("lag_f", P), ("lag_b", P),
    ("cross_f", P), ("cross_b", P), ("colmask", GRID_W), ("fold", 2 * ADA_TILES), ("idx", 2), ("prio", PER_GROUP),
    ("levels", 2 * LEVELS * P))
PARAM, PARAM_W = layout(
    ("norm_mix", KT), ("norm_ffn", KT), ("ada_b", 48), ("conv_gdn", 18), ("conv_sc", 6), ("gdn_norm", 1),
    ("q_norm", 1), ("k_norm", 1), ("dt_bias", 8), ("a_log", 8), ("gamma_cols", 8), ("gamma_rows", 4),
    ("router_b", ROUTER), ("router_w", KT * ROUTER), ("nat_bias", HEADS * 2 * GRID_W),
    ("ck", HEADS * P), ("cv", HEADS * P), ("s_gdn", 4 * P), ("s_ret", 4 * P))
ARENA, ARENA_W = layout(
    ("raw", 6 * 2 * 130), ("qkv", 6 * TOK), ("zg", 2 * TOK), ("gpad", 8 * 256), ("vtok", 2 * 256), ("zr", 2 * TOK),
    ("natqk", 4 * TOK), ("retqk", 4 * TOK), ("sb", 2 * TOK), ("sx", 2 * TOK), ("ub", 2 * 2 * 130),
    ("vp", 2 * 2 * 512), ("norm", 2048), ("npad", 4 * 256), ("rpad", 4 * 256))
GROUP_W = 8 * 512

PER = dict(
    ada_mm=8, ada_row=8, ada_tr=8, ada_dve=8, norm_sq=4, norm_mm=2, norm_rs=2, h_scaled=4, h_act=2, h_dve=2,
    proj_mm=15, proj_act=10, proj_dve=5, conv_dve=1, silu_act=1, sc_dve=1,
    sp_in=1, sp_act=1, gates_dve=1,
    qk_sq=1, qk_mm=1, qk_rs=1, qk_dve=1, pad_act=1, pad_pool=1, rope_mm=1, rope_dve=1, rpad_act=1, rpad_pool=1,
    zeroed=1, param_dma=16, layer_done=1,
    nat_mm=1, nat_max=1, nat_exp=1, nat_p=1, nat_tr=1, nat_pt=1, nat_o=1, nat_out=1,
    ret_exp=1, ret_mm=1, ret_a=1, ret_kt=1, ret_kd=1, ret_o=1, ret_sf=1, ret_st=1, ret_og=1,
    ret_mean=1, ret_sq=1, ret_var=1, ret_rs=1, ret_out=1,
    vnp_zero=1, gr_mm=2, gr_min=4, gr_exp=4, gr_dec=2, gcol_mm=2, gcol_exp=2, vt_mm=2, vt_act=2,
    ks_mm=2, z_dve=2, inv_c=28, inv_dmm=28, inv_dev=24, inv_umm=24, inv_upd=28,
    vn_mm=4, vn_dve=4, qd_g=1, qd_mm=1, qd_exp=1, qd_dve=1, kd_dve=1, gs_mm=1, gs_st=1, go_mm=2, go_dve=2,
    gn_sq=1, gn_mm=1, gn_rs=1, gn_out=1,
    out_mm=3, res_dve=3, route_mm=1, route_exp1=1, route_d1=1, route_d2=1, route_exp2=1, route_dve=1,
    cb_mm=16, cb_act=8, cb_dve=8, h_hi=1, h_lo=1,
    gate_mm=32, up_mm=32, down_mm=32, silu=32, hi_gate=32, hi_up=32, hi_down=32, act_hi=32,
    lo_gate=32, lo_up=32, lo_down=32, prod=32, act_dve=32, act_lo=32,
    route_oh=1, ht_mm=4, rank_mm=1, flag=1,
    ht_hi=4, ht_lo=4, sel=1, ga_mm=8, ga_hi=8, ga_lo=8, cg_mm=1, cg_dve=1, st_mm=2, st_act=2,
    half_mm=32, gu_mm=32, tr_mm=32, hi_a=31, hi_b=31, lo_a=31, lo_b=31, g_silu=32, g_act=32, act_t=32, yg_hi=4, yg_lo=5,
    scatter_mm=4,
)


def build_trunk(nc, src, dst):
    with ExitStack() as ctx:
        def sb(name, *shape):
            return ctx.enter_context(nc.sbuf_tensor(name, list(shape), F32))

        def two_types(name, *shape):
            with nc.sbuf_tensor(name, list(shape), F32) as plain:
                pass
            rounded = ctx.enter_context(nc.sbuf_tensor(name + "_r", list(shape), F32R))
            return plain, rounded

        ring, ring_r = zip(*(two_types(f"ring{j}", P, SLOT) for j in range(RING)))
        xT = sb("xT", P, KT, TOK)
        hT, hT_r = two_types("hT", P, KT, TOK)
        const = sb("const", P, CONST_W)
        param, param_r = two_types("param", P, PARAM_W)
        arena, arena_r = two_types("arena", P, ARENA_W)
        condT = sb("condT", P, KT, NS)
        condp = sb("condp", P, KT, 2 * (ADA_TILES - 1) + 32)
        adaT = sb("adaT", P, 48, NS)
        scale1 = sb("scale1", P, 2, KT, NS)
        rstd = sb("rstd", P, TOK)
        adarow = rstd[:, 0:P]
        spx = sb("spx", P, 28)
        beta = sb("beta", P, 2, 8)
        nega = sb("nega", P, 8)
        gdec = sb("gdec", P, 2, 8)
        gneg = sb("gneg", P, 2, 8)
        lg = sb("lg", P, 12)
        kdc = sb("kdc", P, 8)
        egc = sb("egc", P, 16)
        natm = sb("natm", P, 12)
        natsum = sb("natsum", P, 12)
        state = sb("state", P, 2, 2, HD)
        state_flat = state[:].rearrange("p d j n -> p (d j n)")
        rt = state_flat[:, 0:2 * ROUTER].rearrange("p (s n) -> p s n", s=2)
        rs_ = state_flat[:, 2 * ROUTER:2 * ROUTER + 120]
        gin = state_flat[:, 0:32].rearrange("p (s n) -> p s n", s=2)
        comb = sb("comb", P, 2, N_EXPERTS)
        comb_flat = comb[:].rearrange("p s n -> p (s n)")
        spa, spe = comb_flat[:, 0:28], comb_flat[:, 28:56]
        most = ctx.enter_context(nc.sbuf_tensor("most", [P, 1], I32))
        ps = ctx.enter_context(nc.psum_tensor("ps", [P, 8, 512], F32))

        sem = {name: ctx.enter_context(nc.semaphore(name)) for name in PER}
        slot_in = [ctx.enter_context(nc.semaphore(f"slot_in{j}")) for j in range(RING)]
        const_in = ctx.enter_context(nc.semaphore("const_in"))
        cond_in = ctx.enter_context(nc.semaphore("cond_in"))
        cond_zero = ctx.enter_context(nc.semaphore("cond_zero"))
        cond_e = ctx.enter_context(nc.semaphore("cond_silu"))
        state_out = ctx.enter_context(nc.semaphore("state_out"))
        kv_out = ctx.enter_context(nc.semaphore("kv_out"))
        y_out = ctx.enter_context(nc.semaphore("y_out"))
        chain_dve = ctx.enter_context(nc.semaphore("chain_dve"))
        chain_act = ctx.enter_context(nc.semaphore("chain_act"))

        def C(name):
            return const[:, CONST[name]]

        def Q(name):
            return param[:, PARAM[name]]

        def A(name):
            return arena[:, ARENA[name]]

        def bc(ap, *shape):
            return ap.broadcast_to([P, *shape])

        raw = A("raw").rearrange("p (m s t) -> p m s t", m=6, s=2)
        qkv = A("qkv").rearrange("p (m t) -> p m t", m=6)
        zg, zr = A("zg"), A("zr")
        og = A("zr").rearrange("p (j s c) -> p j s c", j=2, s=2)
        gpad = A("gpad").rearrange("p (t s i c) -> p t s i c", t=4, s=2, i=2)
        vtok = A("vtok").rearrange("p (s n) -> p s n", s=2)
        natqk = A("natqk").rearrange("p (m t) -> p m t", m=4)
        retqk = A("retqk").rearrange("p (m t) -> p m t", m=4)
        sbT, sxT = A("sb").rearrange("p (m s t) -> p m s t", m=2, s=2), A("sx").rearrange("p (m s t) -> p m s t", m=2, s=2)
        ub = A("ub").rearrange("p (m s t) -> p m s t", m=2, s=2)
        vp = A("vp").rearrange("p (s r j n) -> p s r j n", s=2, r=2, j=2)
        norm = A("norm")
        npad = A("npad").rearrange("p (j s i c) -> p j s i c", j=2, s=2, i=2)
        rpad = A("rpad").rearrange("p (j s i c) -> p j s i c", j=2, s=2, i=2)
        levels = C("levels").rearrange("p (d b c) -> p d b c", d=2, b=LEVELS)
        ident = C("ident")
        g0 = ARENA["natqk"].start

        def group(g, part):
            at = g0 + g * GROUP_W + part * 512
            return arena[:, at:at + 512].rearrange("p (h c) -> p h c", h=HEADS)

        tail = g0 + 2 * GROUP_W
        z = arena[:, tail:tail + 512].rearrange("p (g n) -> p g n", g=2)
        kdg = arena[:, tail + 512:tail + 1024].rearrange("p (g n) -> p g n", g=2)
        qdec = arena[:, tail + 1024:tail + 1536].rearrange("p (g j c) -> p g j c", g=2, j=2)
        assert tail + 1536 <= ARENA_W
        cb = arena[:, 0:N_EXPERTS * TOK].rearrange("p (e t) -> p e t", e=N_EXPERTS)
        moe0 = N_EXPERTS * TOK
        sg = arena[:, moe0:moe0 + 1024].rearrange("p (b f t) -> p b f t", b=2, f=2)
        sg_lo = arena_r[:, moe0:moe0 + 1024].rearrange("p (b f t) -> p b f t", b=2, f=2)
        gated_hi = arena_r[:, moe0 + 1024:moe0 + 2048].rearrange("p (b f t) -> p b f t", b=2, f=2)
        w_hi = arena_r[:, moe0 + 2048:moe0 + 2048 + SLOT]
        assert moe0 + 2048 + SLOT <= ARENA_W
        h_hi = param_r[:, PARAM["ck"].start:PARAM["ck"].start + KT * TOK].rearrange("p (k t) -> p k t", k=KT)
        assert PARAM["ck"].start + KT * TOK <= PARAM_W
        h_lo = hT_r[:]
        def three(ap):
            return ap.rearrange("p (k c) -> p k c", k=KT)

        def halves(ap):
            return ap.rearrange("p (b n) -> p b n", b=2)

        hg_hi, hg_lo = three(arena_r[:, 0:4096]), three(arena_r[:, 4096:8192])
        sel_r, sel = (a[:, 8192:9216].rearrange("p (s g c) -> p s g c", s=2, g=N_GROUPS) for a in (arena_r, arena))
        sel_t = arena_r[:, 9216:10240].rearrange("p (g t) -> p g t", g=N_GROUPS)
        after_w = moe0 + 2048 + 4096
        g_silu, gat, act_t = (halves(arena[:, after_w + n * 512:after_w + (n + 1) * 512]) for n in range(3))
        cg = arena[:, after_w + 1536:after_w + 1536 + N_EXPERTS]
        c8_hi, c8_lo = (arena_r[:, after_w + 1568 + 16 * n:after_w + 1584 + 16 * n].rearrange("p (s n) -> p s n", s=2) for n in range(2))
        assert after_w + 1600 <= ARENA_W
        ht_hi = param_r[:, PARAM["ck"].start:PARAM["ck"].start + 2048].rearrange("p (s n) -> p s n", s=2)
        ht_lo = h_lo.rearrange("p k t -> p (k t)").rearrange("p (s n) -> p s n", s=2)
        norm2 = arena[:, 0:2048]
        nat_s = norm[:, 0:1536]
        nat_t = A("raw")[:, 0:1536]
        ef = arena[:, ARENA["sb"].start:ARENA["sb"].start + 512].rearrange("p (h c) -> p h c", h=HEADS)
        eb = arena[:, ARENA["sb"].start + 512:ARENA["sb"].start + 1024].rearrange("p (h c) -> p h c", h=HEADS)
        qx = arena[:, ARENA["ub"].start:ARENA["ub"].start + 512].rearrange("p (d j c) -> p d j c", d=2, j=2)
        ret_a = norm[:, 0:1024].rearrange("p (s h c) -> p s h c", s=2, h=HEADS)
        ret_kd = norm[:, 1024:1536].rearrange("p (d n) -> p d n", d=2)
        qx_in = norm[:, 1536:2048].rearrange("p (d j c) -> p d j c", d=2, j=2)
        upto = [C("upto_f"), C("upto_b")]
        after = [C("after_f"), C("after_b")]
        s_gdn = Q("s_gdn").rearrange("p (d j c) -> p d j c", d=2, j=2)
        s_ret = Q("s_ret").rearrange("p (d j c) -> p d j c", d=2, j=2)
        ck = Q("ck").rearrange("p (h c) -> p h c", h=HEADS)
        cv = Q("cv").rearrange("p (h c) -> p h c", h=HEADS)

        def bank(b, width=512):
            return ps[:, b, 0:width]

        def heads(ap):
            return ap.rearrange("p (h c) -> p h c", h=HEADS)

        def proj_bank(u):
            return (u + 2) % 8

        block = ctx.enter_context(nc.Block())

        def rise(layer, name, n):
            return layer * PER[name] + n

        class Links:

            def __init__(self):
                self.count = 0

            def next(self):
                self.count += 1
                return self.count

            def restart(self):
                self.count = 0

        @block.sync
        def _(sp):
            sp.dma_start(condT[:], src["condT"]).then_inc(cond_in, 16)

            def ring_in(n, what):
                rows, width = what
                sp.dma_start(ring[n % RING][:, 0:width], rows).then_inc(slot_in[n % RING], 16)

            loads = [None] * HEAD_SLOTS
            for i in range(ADA_SLOTS):
                loads[ada_load(i)] = ("ada_w", i, SLOT, "ada_mm", i + 1)
            for i in range(IN_SLOTS):
                loads[in_load(i)] = ("w_feat", i - (i > 1), SLOT, "proj_mm", 3 * i + 3)
            loads[in_load(1)] = ("w_tok", None, KT * TOKCOLS, "proj_mm", 6)
            for i in range(OUT_SLOTS):
                loads[out_load(i)] = ("w_out", sum(OUT_TILES[:i]) * KT * P, OUT_TILES[i] * KT * P, "out_mm", i + 1)

            def head_slot(l, i):
                name, part, width, _, _ = loads[i]
                if name == "w_tok":
                    return src[name][l], width
                if name == "w_out":
                    return src[name][l][:, part:part + width], width
                return src[name][l, part], width

            def slot_free(l, i):
                if i < HEAD_SLOTS:
                    _, _, _, name, n = loads[i]
                    sp.wait_ge(sem[name], rise(l, name, n))
                else:
                    sp.wait_ge(sem["down_mm"], rise(l, "down_mm", i - HEAD_SLOTS + 1))

            for l in range(DEPTH):
                for i in range(HEAD_SLOTS):
                    if i >= RING:
                        slot_free(l, i - RING)
                    elif l > 0:
                        slot_free(l - 1, HEAD_SLOTS + N_EXPERTS + i - RING)
                    ring_in(i, head_slot(l, i))
                    if l == 0 and i == 1:
                        sp.dma_start(const[:], src["const"]).then_inc(const_in, 16)
                    if l == 0 and i == 2:
                        sp.dma_start(xT[:], src["xT"]).then_inc(const_in, 16)
                    if i == RING - 1:
                        if l > 0:
                            sp.wait_ge(sem["layer_done"], l + 1)
                        sp.dma_start(param[:], src["param"][l]).then_inc(sem["param_dma"], 16)
                for e in range(RING):
                    slot_free(l, HEAD_SLOTS - RING + e)
                    ring_in(e, (src["moe"][l, e], SLOT))
                with sp.Fori(1, N_EXPERTS // RING) as turn:
                    e4 = turn * RING
                    for j in range(RING):
                        sp.wait_ge(sem["down_mm"], e4 + (l * PER["down_mm"] + j - RING + 1))
                        rows = src["moe"][l, bass.ds(e4 + j, 1)].rearrange("o p n -> (o p) n")
                        ring_in(j, (rows, SLOT))
            sp.wait_ge(sem["layer_done"], DEPTH + 1)
            sp.dma_start(dst["yT"], xT[:]).then_inc(y_out, 16)
            sp.wait_ge(y_out, 16)

        @block.tensor
        def _(pe):
            mm = nc.tensor.matmul

            def in_slot(l, i):
                pe.wait_ge(slot_in[i % RING], l * (16 * (HEAD_SLOTS + N_EXPERTS) // RING) + 16 * (i // RING + 1))

            with pe.Fori(0, DEPTH) as l:
                pe.wait_ge(cond_e, 1)
                pe.wait_ge(sem["layer_done"], rise(l, "layer_done", 1))

                def ada(i, bank_in, units=range(ADA_UNITS)):
                    if units[0] == 0:
                        in_slot(l, ada_load(i))
                    slot = ring[ada_load(i) % RING][:]
                    for u in units:
                        m, k = divmod(u, KT)
                        lead = 2 * (ADA_TILES - 1 - m)
                        j = 32 * (k % 4)
                        last = mm(ps[j:j + 32, bank_in, 0:P], condp[:, k, lead:lead + 32], slot[:, k * 768 + m * P:k * 768 + (m + 1) * P],
                                  start=u < 4, stop=u >= ADA_UNITS - 4, tile_position=(0, j), skip_group_check=True)
                    if units[-1] == ADA_UNITS - 1:
                        last.then_inc(sem["ada_mm"], 1)

                def ada_transpose(i, bank_out):
                    pe.wait_ge(const_in, 32)
                    pe.wait_ge(sem["ada_row"], rise(l, "ada_row", i + 1))
                    mm(ps[:, bank_out, 0:2 * ADA_TILES], adarow, C("fold"),
                       start=True, stop=True).then_inc(sem["ada_tr"], 1)

                for i in range(ADA_FIRST):
                    if i >= 2:
                        pe.wait_ge(sem["ada_row"], rise(l, "ada_row", i - 1))
                    ada(i, 6 + i % 2)
                    if i > 0:
                        if i > 1:
                            pe.wait_ge(sem["ada_dve"], rise(l, "ada_dve", i - 1))
                        ada_transpose(i - 1, 5)
                pe.wait_ge(sem["ada_dve"], rise(l, "ada_dve", ADA_FIRST - 1))
                ada_transpose(ADA_FIRST - 1, 5)

                def norm_sum(squares, part, bank_in, tiles):
                    pe.wait_ge(sem["norm_sq"], rise(l, "norm_sq", part))
                    for k in tiles:
                        last = mm(bank(bank_in, TOK), C("ones"), squares[:, k * TOK:(k + 1) * TOK], start=k == 0, stop=k == KT - 1)
                    if tiles[-1] == KT - 1:
                        last.then_inc(sem["norm_mm"], 1)

                norm_sum(norm, 1, 1, range(KT))
                pe.wait_ge(sem["h_act"], rise(l, "h_act", 1))
                pe.wait_ge(sem["h_dve"], rise(l, "h_dve", 1))
                free_of = {8: ("proj_act", 1), 9: ("proj_act", 2), 10: ("proj_act", 3), 11: ("proj_dve", 1),
                           12: ("proj_dve", 2), 13: ("proj_dve", 3), 14: ("proj_act", 4)}
                u = 0
                for i in range(IN_SLOTS):
                    in_slot(l, in_load(i))
                    slot = ring[in_load(i) % RING][:]
                    if i == 1:
                        for s in range(NS):
                            for k in range(KT):
                                last = mm(bank(proj_bank(3 + s)), hT[:, k, s * P:(s + 1) * P],
                                          slot[:, k * TOKCOLS + 16:(k + 1) * TOKCOLS], start=k == 0, stop=k == KT - 1)
                            last.then_inc(sem["proj_mm"], 1)
                        for s in range(NS):
                            for k in range(KT):
                                last = mm(ps[:, proj_bank(5), 16 * s:16 * s + 16], hT[:, k, s * P:(s + 1) * P],
                                          slot[:, k * TOKCOLS:k * TOKCOLS + 16], start=k == 0, stop=k == KT - 1)
                        last.then_inc(sem["proj_mm"], 1)
                        u += 3
                        continue
                    for pair in range(3):
                        if u in free_of:
                            name, n = free_of[u]
                            pe.wait_ge(sem[name], rise(l, name, n))
                        for m in range(2):
                            for k in range(KT):
                                at = k * 768 + (2 * pair + m) * P
                                last = mm(ps[:, proj_bank(u), m * TOK:(m + 1) * TOK], slot[:, at:at + P],
                                          hT[:, k, :], start=k == 0, stop=k == KT - 1)
                        last.then_inc(sem["proj_mm"], 1)
                        u += 1
                pe.wait_ge(sem["proj_act"], rise(l, "proj_act", 10))
                pe.wait_ge(sem["proj_dve"], rise(l, "proj_dve", 5))
                pe.wait_ge(sem["qk_sq"], rise(l, "qk_sq", 1))
                for b in range(4):
                    last = mm(bank(b), C("blockones"), norm[:, b * 512:(b + 1) * 512], start=True, stop=True)
                last.then_inc(sem["qk_mm"], 1)
                mm(bank(4), C("rot"), retqk[:, :, P:TOK], start=True, stop=True).then_inc(sem["rope_mm"], 1)
                ada(ADA_FIRST, 7)
                ada_transpose(ADA_FIRST, 6)

                pe.wait_ge(sem["pad_act"], rise(l, "pad_act", 1))
                pe.wait_ge(sem["pad_pool"], rise(l, "pad_pool", 1))
                pe.wait_ge(sem["qk_dve"], rise(l, "qk_dve", 1))
                for s in range(NS):
                    for j in range(2):
                        last = mm(ps[:, s, j * 256:(j + 1) * 256], natqk[:, j, s * P:(s + 1) * P],
                                  npad[:, j, s].rearrange("p i c -> p (i c)"), start=True, stop=True)
                for j in range(2):
                    last = mm(ps[:, 2, j * 256:(j + 1) * 256], natqk[:, j, P:TOK],
                              Q("ck")[:, j * 256:(j + 1) * 256], start=True, stop=True)
                last.then_inc(sem["nat_mm"], 1)
                pe.wait_ge(sem["rpad_act"], rise(l, "rpad_act", 1))
                pe.wait_ge(sem["rpad_pool"], rise(l, "rpad_pool", 1))
                pe.wait_ge(sem["ada_dve"], rise(l, "ada_dve", ADA_FIRST + 1))
                for s in range(NS):
                    for j in range(2):
                        last = mm(ps[:, 6 + s, j * 256:(j + 1) * 256], retqk[:, 2 + j, s * P:(s + 1) * P],
                                  rpad[:, j, s].rearrange("p i c -> p (i c)"), start=True, stop=True)
                last.then_inc(sem["ret_mm"], 1)
                for j in range(2):
                    last = nc.tensor.transpose(ps[:, 5, j * P:(j + 1) * P], retqk[:, 2 + j, 0:P], ident)
                last.then_inc(sem["ret_kt"], 1)
                ada(ADA_FIRST + 1, 3)
                pe.wait_ge(sem["nat_p"], rise(l, "nat_p", 1))
                for b in range(3):
                    for h in range(HEADS):
                        last = nc.tensor.transpose(ps[:, b, h * P:(h + 1) * P],
                                                   nat_s[:, (b * HEADS + h) * P:(b * HEADS + h + 1) * P], ident)
                last.then_inc(sem["nat_tr"], 1)
                ada_transpose(ADA_FIRST + 1, 4)
                pe.wait_ge(sem["nat_pt"], rise(l, "nat_pt", 1))
                for j in range(2):
                    for s in range(NS):
                        parts = [(vp[:, s, 1, j, i * P:(i + 1) * P], nat_t[:, (s * HEADS + 2 * j + i) * P:(s * HEADS + 2 * j + i + 1) * P])
                                 for i in range(2)]
                        if s == 1:
                            parts += [(cv[:, 2 * j + i, :], nat_t[:, (2 * HEADS + 2 * j + i) * P:(2 * HEADS + 2 * j + i + 1) * P])
                                      for i in range(2)]
                        for n, (v, p) in enumerate(parts):
                            last = mm(ps[:, 3, j * 256 + s * P:j * 256 + (s + 1) * P], v, p,
                                      start=n == 0, stop=n == len(parts) - 1)
                last.then_inc(sem["nat_o"], 1)
                pe.wait_ge(sem["ret_a"], rise(l, "ret_a", 1))
                pe.wait_ge(sem["ada_dve"], rise(l, "ada_dve", ADA_FIRST + 2))
                for j in range(2):
                    for s in range(NS):
                        parts = [(vp[:, s, 0, j, i * P:(i + 1) * P], ret_a[:, s, 2 * j + i, :]) for i in range(2)]
                        if s == 1:
                            parts += [(s_ret[:, d, j, :], qx[:, d, j, :]) for d in range(2)]
                        for n, (v, p) in enumerate(parts):
                            last = mm(ps[:, 4, j * 256 + s * P:j * 256 + (s + 1) * P], v, p,
                                      start=n == 0, stop=n == len(parts) - 1)
                last.then_inc(sem["ret_o"], 1)
                pe.wait_ge(sem["ret_kd"], rise(l, "ret_kd", 1))
                for d in range(2):
                    for j in range(2):
                        last = mm(ps[:, d, j * 256:(j + 1) * 256], ret_kd[:, d, j * P:(j + 1) * P],
                                  vp[:, 0, 0, j, :], start=True, stop=True)
                last.then_inc(sem["ret_sf"], 1)
                pe.wait_ge(sem["ret_og"], rise(l, "ret_og", 1))
                mm(bank(2), C("blockones"), ef.rearrange("p h c -> p (h c)"), start=True, stop=True).then_inc(sem["ret_mean"], 1)
                pe.wait_ge(sem["ret_sq"], rise(l, "ret_sq", 1))
                pe.wait_ge(sem["nat_out"], rise(l, "nat_out", 1))
                mm(bank(3), C("blockones"), eb.rearrange("p h c -> p (h c)"), start=True, stop=True).then_inc(sem["ret_var"], 1)
                pe.wait_ge(sem["ret_out"], rise(l, "ret_out", 1))
                pe.wait_ge(sem["ret_st"], rise(l, "ret_st", 1))

                for s in range(NS):
                    tk = slice(s * P, (s + 1) * P)
                    if s == 1:
                        pe.wait_ge(sem["ada_dve"], rise(l, "ada_dve", ADA_FIRST + 4))
                        pe.wait_ge(sem["go_dve"], rise(l, "go_dve", 1))
                        pe.wait_ge(sem["gs_st"], rise(l, "gs_st", 1))
                    for d in range(2):
                        for h in range(HEADS):
                            gcol = gdec[:, s, d * 4 + h:d * 4 + h + 1]
                            mm(ps[:, 2 + d, h * P:(h + 1) * P], bc(gcol, P), upto[d], start=True, stop=False)
                            mm(ps[:, 2 + d, h * P:(h + 1) * P], upto[d], bc(gneg[:, s, d * 4 + h:d * 4 + h + 1], P), start=False, stop=True)
                        for h in range(HEADS):
                            bcol = beta[:, s, d * 4 + h:d * 4 + h + 1]
                            last = mm(ps[:, 4 + d, h * P:(h + 1) * P], bc(bcol, P), ident, start=True, stop=True)
                    for j in range(2):
                        last = mm(bank(j), qkv[:, 2 + j, tk], gpad[:, j::2, s, :, :].rearrange("p t i c -> p t (i c)"),
                                  start=True, stop=True)
                    last.then_inc(sem["gr_mm"], 1)
                    for d in range(2):
                        mm(ps[:, 6, d * 4:d * 4 + 4], upto[d], gdec[:, s, d * 4:d * 4 + 4], start=True, stop=True)
                        last = mm(ps[:, 6, 8 + d * 4:12 + d * 4], after[d], gdec[:, s, d * 4:d * 4 + 4], start=True, stop=True)
                    last.then_inc(sem["gcol_mm"], 1)
                    for j in range(2):
                        last = nc.tensor.transpose(ps[:, 7, j * P:(j + 1) * P], qkv[:, 4 + j, tk], ident)
                    last.then_inc(sem["vt_mm"], 1)
                    pe.wait_ge(sem["gcol_exp"], rise(l, "gcol_exp", s + 1))
                    if s == 0:
                        for j in range(2):
                            last = nc.tensor.transpose(ps[:, 7, (2 + j) * P:(3 + j) * P], qkv[:, 2 + j, tk], ident)
                        last.then_inc(sem["ks_mm"], 1)
                    else:
                        for d in range(2):
                            for j in range(2):
                                last = mm(ps[:, 6, d * 256 + j * P:d * 256 + (j + 1) * P], qkv[:, 2 + j, tk],
                                          s_gdn[:, d, j, :], start=True, stop=True)
                        last.then_inc(sem["ks_mm"], 1)
                        pe.wait_ge(sem["vt_act"], rise(l, "vt_act", 2))
                        pe.wait_ge(sem["qd_g"], rise(l, "qd_g", 1))
                        for d in range(2):
                            for j in range(2):
                                last = mm(ps[:, 7, (2 * d + j) * P:(2 * d + j + 1) * P], qdec[:, d, j, :], upto[d], start=True, stop=True)
                        last.then_inc(sem["qd_mm"], 1)
                    i, first, count = ada_piece(s, -1)
                    if s == 1:
                        pe.wait_ge(sem["qd_exp"], rise(l, "qd_exp", 1))
                    ada(i, 6 + s, range(first, first + count))
                    for b in range(LEVELS):
                        for g in range(2):
                            n = (s * LEVELS + b) * 2 + g + 1
                            m = (s * (LEVELS - 1) + b - 1) * 2 + g + 1
                            pe.wait_ge(sem["inv_c"], rise(l, "inv_c", n))
                            name = "inv_upd" if b else "gr_dec"
                            pe.wait_ge(sem[name], rise(l, name, n - 2 if b else s + 1))
                            for h in range(HEADS):
                                last = mm(ps[:, 2 + g, h * P:(h + 1) * P], group(g, 6)[:, h, :],
                                          group(g, 3)[:, h, :] if b else ident, start=True, stop=True)
                            last.then_inc(sem["inv_dmm"], 1)
                        i, first, count = ada_piece(s, b)
                        if b == 0:
                            ada(i, 6 + s, range(first, first + count))
                            continue
                        if b == 1:
                            pe.wait_ge(sem["z_dve"], rise(l, "z_dve", s + 1))
                            pe.wait_ge(sem["kd_dve"], rise(l, "kd_dve", 1))
                            ada_transpose(ADA_FIRST + 2 + 2 * s, 7 - s)
                        now = count if b == LEVELS - 1 else count // 2
                        if now:
                            ada(i, 6, range(first, first + now))
                        for g in range(2):
                            m = (s * (LEVELS - 1) + b - 1) * 2 + g + 1
                            pe.wait_ge(sem["inv_dev"], rise(l, "inv_dev", m))
                            for h in range(HEADS):
                                if b < LEVELS - 1:
                                    mm(ps[:, 4 + g, h * P:(h + 1) * P], group(g, 4)[:, h, :], group(g, 5)[:, h, :],
                                       start=True, stop=True)
                            for h in range(HEADS):
                                last = mm(ps[:, g, h * P:(h + 1) * P], group(g, 5)[:, h, :], group(g, 4)[:, h, :],
                                          start=True, stop=True)
                            last.then_inc(sem["inv_umm"], 1)
                        if now < count:
                            ada(i, 6, range(first + now, first + count))
                        elif count:
                            pe.wait_ge(sem["ada_dve"], rise(l, "ada_dve", i))
                            ada_transpose(i, 7)
                    pe.wait_ge(sem["z_dve"], rise(l, "z_dve", s + 1))
                    for g in range(2):
                        pe.wait_ge(sem["inv_upd"], rise(l, "inv_upd", (s * LEVELS + LEVELS - 1) * 2 + g + 1))
                        for h in range(HEADS):
                            last = mm(ps[:, 2 + g, h * HD:(h + 1) * HD], group(g, 4)[:, h, :],
                                      z[:, g, h * HD:(h + 1) * HD], start=True, stop=True)
                        last.then_inc(sem["vn_mm"], 1)
                    pe.wait_ge(sem["vn_dve"], rise(l, "vn_dve", 2 * s + 2))
                    pe.wait_ge(sem["ada_dve"], rise(l, "ada_dve", ADA_FIRST + 4 + s))
                    if s == 1:
                        pe.wait_ge(sem["qd_dve"], rise(l, "qd_dve", 1))
                    for j in range(2):
                        parts = [(group(g, 7)[:, 2 * j + i, :], group(g, 1)[:, 2 * j + i, :]) for g in range(2) for i in range(2)]
                        if s == 1:
                            parts += [(s_gdn[:, d, j, :], qdec[:, d, j, :]) for d in range(2)]
                        for n, (v, p) in enumerate(parts):
                            last = mm(ps[:, 6, j * P:(j + 1) * P], v, p, start=n == 0, stop=n == len(parts) - 1)
                    last.then_inc(sem["go_mm"], 1)
                    if s == 0:
                        pe.wait_ge(sem["kd_dve"], rise(l, "kd_dve", 1))
                        for g in range(2):
                            for j in range(2):
                                last = mm(ps[:, 4 + g, j * 256:(j + 1) * 256], kdg[:, g, j * P:(j + 1) * P],
                                          group(g, 7)[:, 2 * j:2 * j + 2, :].rearrange("p i c -> p (i c)"),
                                          start=True, stop=True)
                        last.then_inc(sem["gs_mm"], 1)
                pe.wait_ge(sem["gn_sq"], rise(l, "gn_sq", 1))
                mm(bank(7), C("blockones"), group(0, 3).rearrange("p h c -> p (h c)"), start=True, stop=True).then_inc(sem["gn_mm"], 1)

                pe.wait_ge(sem["gn_out"], rise(l, "gn_out", 1))
                pe.wait_ge(sem["nat_out"], rise(l, "nat_out", 1))
                pe.wait_ge(sem["sc_dve"], rise(l, "sc_dve", 1))
                first = [sum(OUT_TILES[:i]) for i in range(OUT_SLOTS + 1)]
                for i, tiles in enumerate(OUT_TILES):
                    in_slot(l, out_load(i))
                    slot = ring[out_load(i) % RING][:]
                    for m in range(tiles):
                        f = first[i] + m
                        for k in range(KT):
                            at = (k * tiles + m) * P
                            last = mm(ps[:, f // 2, (f % 2) * TOK:(f % 2 + 1) * TOK], slot[:, at:at + P],
                                      hT[:, k, :], start=k == 0, stop=k == KT - 1)
                    last.then_inc(sem["out_mm"], 1)
                    if i > 0:
                        norm_sum(norm2, 1 + i, 5, range(first[i - 1], first[i]))
                norm_sum(norm2, 1 + OUT_SLOTS, 5, range(first[-2], KT))
                pe.wait_ge(sem["h_act"], rise(l, "h_act", 2))
                pe.wait_ge(sem["h_dve"], rise(l, "h_dve", 2))
                rw = Q("router_w").rearrange("p (k n) -> p k n", k=KT)
                for s in range(NS):
                    for k in range(KT):
                        last = mm(ps[:, 0, 64 * s:64 * s + ROUTER], hT[:, k, s * P:(s + 1) * P], rw[:, k, :],
                                  start=k == 0, stop=k == KT - 1)
                last.then_inc(sem["route_mm"], 1)
                for s in range(NS):
                    for half in range(2):
                        for k in range(4):
                            last = nc.tensor.transpose(ps[:, 2 + 2 * s + half, k * P:(k + 1) * P], hT[:, 4 * half + k, s * P:(s + 1) * P], ident)
                        last.then_inc(sem["ht_mm"], 1)
                oh4 = rs_[:, 28:36].rearrange("p (s n) -> p s n", s=2)
                pe.wait_ge(sem["route_oh"], rise(l, "route_oh", 1))
                mm(ps[:, 1, 0:4], upto[0], oh4[:, 0], start=True, stop=True)
                mm(ps[:, 1, 4:8], upto[0], oh4[:, 1], start=True, stop=False)
                mm(ps[:, 1, 4:8], C("ones"), oh4[:, 0], start=False, stop=True)
                mm(ps[:, 1, 8:12], C("ones"), oh4[:, 0], start=True, stop=False)
                mm(ps[:, 1, 8:12], C("ones"), oh4[:, 1], start=False, stop=True).then_inc(sem["rank_mm"], 1)
                pe.wait_ge(const_in, 32)
                pe.wait_ge(sem["flag"], rise(l, "flag", 1))
                def split_products(out, slot_lo, at, x_hi, x_lo, start, stop):
                    hi, lo = w_hi[:, at:at + P], slot_lo[:, at:at + P]
                    mm(out, hi, x_hi, start=start, stop=False, skip_group_check=True)
                    mm(out, hi, x_lo, start=False, stop=False, skip_group_check=True)
                    return mm(out, lo, x_hi, start=False, stop=stop, skip_group_check=True)

                def first_products(e, j, which, name):
                    slot_lo = ring_r[j][:]
                    for fblk in range(2):
                        for k in range(KT):
                            last = split_products(ps[:, 4 + 2 * (j % 2) + which, fblk * TOK:(fblk + 1) * TOK], slot_lo,
                                                  which * 2048 + k * FF + fblk * P, h_hi[:, k, :], h_lo[:, k, :],
                                                  k == 0, k == KT - 1)
                    last.then_inc(sem[name], 1)

                def down(e, j, final):
                    slot_lo = ring_r[j][:]
                    for f8 in range(KT):
                        for kk in range(2):
                            last = split_products(ps[:, f8 // 2, (f8 % 2) * TOK:(f8 % 2 + 1) * TOK], slot_lo,
                                                  4096 + kk * D_MODEL + f8 * P, gated_hi[:, j % 2, kk, :], sg_lo[:, j % 2, kk, :],
                                                  False, final and f8 % 2 == 1 and kk == 1)
                    last.then_inc(sem["down_mm"], 1)

                def step(e, j, first=1, last=False):
                    nxt = (j + 1) % RING
                    if not last:
                        pe.wait_ge(sem["lo_gate"], rise(l, "lo_gate", e + 2))
                        if first > 0:
                            pe.wait_ge(sem["silu"], rise(l, "silu", e))
                        first_products(e + 1, nxt, 0, "gate_mm")
                        pe.wait_ge(sem["lo_up"], rise(l, "lo_up", e + 2))
                        if first > 0:
                            pe.wait_ge(sem["prod"], rise(l, "prod", e))
                        first_products(e + 1, nxt, 1, "up_mm")
                    if first >= 0:
                        pe.wait_ge(sem["lo_down"], rise(l, "lo_down", e + 1))
                        pe.wait_ge(sem["act_lo"], rise(l, "act_lo", e + 1))
                        down(e, j, last)

                def gate_up(e, j, group, first_half):
                    hi = w_hi[:, 0:4096].rearrange("p (w k n) -> p k w n", w=2, k=KT)
                    lo = ring_r[j][:, 0:4096].rearrange("p (w k n) -> p k w n", w=2, k=KT)
                    out = bank((j % 2)).rearrange("p (w n) -> p w n", w=2)
                    for k in range(0, 4) if first_half else range(4, KT):
                        x_hi, x_lo = hg_hi[:, k, group:group + P], hg_lo[:, k, group:group + P]
                        mm(out, x_hi, hi[:, k], start=k == 0, stop=False)
                        mm(out, x_lo, hi[:, k], start=False, stop=False)
                        last = mm(out, x_hi, lo[:, k], start=False, stop=k == KT - 1)
                    last.then_inc(sem["half_mm" if first_half else "gu_mm"], 1)

                def gathered_step(e, i, turn, last=False):
                    nxt = (i + 1) % RING
                    group = (turn + (i + 1) // PER_GROUP) * P
                    if not last:
                        if i >= 0:
                            pe.wait_ge(sem["lo_a"], rise(l, "lo_a", e + 1))
                        gate_up(e + 1, nxt, group, True)
                    if i >= 0:
                        pe.wait_ge(sem["g_act"], rise(l, "g_act", e + 1))
                        for kk in range(2):
                            done = nc.tensor.transpose(ps[:, 2 + i % 2, kk * P:(kk + 1) * P], gat[:, i % 2, kk * P:(kk + 1) * P], ident)
                        done.then_inc(sem["tr_mm"], 1)
                    if not last:
                        if i >= 0:
                            pe.wait_ge(sem["lo_b"], rise(l, "lo_b", e + 1))
                        gate_up(e + 1, nxt, group, False)
                    if i >= 0:
                        pe.wait_ge(sem["act_t"], rise(l, "act_t", e + 1))
                        if i == 0:
                            pe.wait_ge(sem["yg_lo"], rise(l, "yg_lo", turn + 1))
                        for half in range(2):
                            for kk in range(2):
                                at = 4096 + kk * D_MODEL + half * 512
                                done = mm(bank(4 + half), act_t[:, i % 2, kk * P:(kk + 1) * P], ring[i % RING][:, at:at + 512],
                                          start=i == 0 and kk == 0, stop=i == PER_GROUP - 1 and kk == 1, skip_group_check=True)
                        done.then_inc(sem["down_mm"], 1)

                fullest = pe.value_load(most[0:1, 0:1], min_val=0, max_val=TOK)
                with pe.If(fullest < P + 1):
                    pe.wait_ge(sem["sel"], rise(l, "sel", 1))
                    pe.wait_ge(sem["ht_hi"], rise(l, "ht_hi", 4))
                    pe.wait_ge(sem["ht_lo"], rise(l, "ht_lo", 4))
                    for k in range(KT):
                        if k >= 4:
                            pe.wait_ge(sem["ga_lo"], rise(l, "ga_lo", k - 3))
                        for n, (x, s) in enumerate((x, s) for s in range(NS) for x in (ht_hi, ht_lo)):
                            last = mm(bank((6, 7, 0, 1)[k % 4]), x[:, s, k * P:(k + 1) * P], sel_r[:, s].rearrange("p g c -> p (g c)"),
                                      start=n == 0, stop=n == 3)
                        last.then_inc(sem["ga_mm"], 1)
                    for g in range(N_GROUPS):
                        for n, (x, s) in enumerate((x, s) for s in range(NS) for x in (c8_hi, c8_lo)):
                            last = mm(ps[:, 4, g * PER_GROUP:(g + 1) * PER_GROUP], sel_r[:, s, g, :], x[:, s, :], start=n == 0, stop=n == 3)
                    last.then_inc(sem["cg_mm"], 1)
                    for g in range(N_GROUPS):
                        for s in range(NS):
                            last = nc.tensor.transpose(ps[:, 2 + g // 2, (g % 2) * TOK + s * P:(g % 2) * TOK + (s + 1) * P], sel[:, s, g, :], ident)
                        if g % 2:
                            last.then_inc(sem["st_mm"], 1)
                    pe.wait_ge(sem["ga_lo"], rise(l, "ga_lo", KT))
                    pe.wait_ge(sem["st_act"], rise(l, "st_act", 2))
                    pe.wait_ge(sem["lo_up"], rise(l, "lo_up", 1))
                    gathered_step(-1, -1, 0)
                    for e in range(N_EXPERTS):
                        gathered_step(e, e % PER_GROUP, e // PER_GROUP, last=e == N_EXPERTS - 1)
                    pe.wait_ge(sem["yg_lo"], rise(l, "yg_lo", N_GROUPS + 1))
                    for f in range(KT):
                        for n, (y, g) in enumerate((y, g) for g in range(N_GROUPS) for y in (hg_hi, hg_lo)):
                            last = mm(ps[:, f // 2, (f % 2) * TOK:(f % 2 + 1) * TOK], y[:, f, g * P:(g + 1) * P], sel_t[:, g, :],
                                      start=n == 0, stop=n == 2 * N_GROUPS - 1)
                        if f % 2:
                            last.then_inc(sem["scatter_mm"], 1)
                    for name, n in (("cb_mm", 16), ("gate_mm", 32), ("up_mm", 32)):
                        pe.sem_inc(sem[name], n)
                with pe.Else():
                    pe.wait_ge(sem["route_dve"], rise(l, "route_dve", 1))
                    for q in range(N_EXPERTS // 2):
                        b = q % 4
                        if q >= 4:
                            name = "cb_dve" if q % 2 else "cb_act"
                            pe.wait_ge(sem[name], rise(l, name, (q - 4) // 2 + 1))
                        for n in range(4):
                            last = mm(ps[:, b, n * P:(n + 1) * P], bc(comb[:, n % 2, 2 * q + n // 2:2 * q + n // 2 + 1], P), ident,
                                      start=True, stop=True)
                        last.then_inc(sem["cb_mm"], 1)
                    pe.wait_ge(sem["cb_act"], rise(l, "cb_act", 8))
                    pe.wait_ge(sem["cb_dve"], rise(l, "cb_dve", 8))
                    for b in range(4):
                        mm(bank(b), C("zeros"), const[:, 0:512], start=True, stop=False, skip_group_check=True)

                    pe.wait_ge(sem["h_hi"], rise(l, "h_hi", 1))
                    pe.wait_ge(sem["h_lo"], rise(l, "h_lo", 1))
                    step(-1, RING - 1, first=-1)
                    step(0, 0, first=0)
                    for e in range(1, RING):
                        step(e, e)
                    with pe.Fori(1, N_EXPERTS // RING - 1) as turn:
                        for j in range(RING):
                            step(turn * RING + j, j)
                    for e in range(N_EXPERTS - RING, N_EXPERTS):
                        step(e, e % RING, last=e == N_EXPERTS - 1)
                    for name in ("ga_mm", "cg_mm", "st_mm", "half_mm", "gu_mm", "tr_mm", "scatter_mm"):
                        pe.sem_inc(sem[name], PER[name])

        @block.scalar
        def _(act):
            go = nc.scalar.activation
            act.wait_ge(cond_in, 16)
            act.wait_ge(cond_zero, 1)
            go(condp[:, :, 2 * (ADA_TILES - 1):2 * ADA_TILES], condT[:], ACT.Silu).then_inc(cond_e, 1)
            act.wait_ge(const_in, 32)
            with act.Fori(0, DEPTH) as l:
                links = Links()

                def norm_stats(n):
                    if n == 1:
                        act.wait_ge(sem["layer_done"], rise(l, "layer_done", 1))
                        go(norm, xT[:].rearrange("p k t -> p (k t)"), ACT.Square).then_inc(sem["norm_sq"], 1)
                    else:
                        at = 0
                        for i, tiles in enumerate(OUT_TILES):
                            act.wait_ge(sem["res_dve"], rise(l, "res_dve", i + 1))
                            go(norm2[:, at * TOK:(at + tiles) * TOK], xT[:, at:at + tiles, :].rearrange("p k t -> p (k t)"),
                               ACT.Square).then_inc(sem["norm_sq"], 1)
                            at += tiles
                    act.wait_ge(sem["norm_mm"], rise(l, "norm_mm", n))
                    go(rstd[:], bank(1 if n == 1 else 5, TOK), ACT.Ln, bias=EPS, scale=1.0 / D_MODEL).then_inc(chain_act, 1)
                    act.wait_ge(chain_act, links.next())
                    go(rstd[:], rstd[:], ACT.Exp, scale=-0.5).then_inc(sem["norm_rs"], 1)
                    act.wait_ge(sem["h_scaled"], rise(l, "h_scaled", 2 * n - 1))
                    which, sh = (0, 0) if n == 1 else (1, 24)
                    for k in range(4):
                        for s in range(NS):
                            t = hT[:, k, s * P:(s + 1) * P]
                            last = go(t, t, ACT.Identity, bias=adaT[:, sh + k, s:s + 1], scale=scale1[:, which, k, s:s + 1])
                    last.then_inc(sem["h_act"], 1)

                def ada_rows(i, bank_in):
                    act.wait_ge(sem["ada_mm"], rise(l, "ada_mm", i + 1))
                    if i > 0:
                        act.wait_ge(sem["ada_tr"], rise(l, "ada_tr", i))
                    go(adarow, ps[:, bank_in, 0:P], ACT.Copy).then_inc(sem["ada_row"], 1)

                for i in range(ADA_FIRST):
                    ada_rows(i, 6 + i % 2)
                norm_stats(1)
                act.wait_ge(sem["zeroed"], rise(l, "zeroed", 1))
                for u in range(3):
                    act.wait_ge(sem["proj_mm"], rise(l, "proj_mm", u + 1))
                    go(raw[:, 2 * u:2 * u + 2, :, 1:129].rearrange("p m s t -> p (m s) t"),
                       bank(proj_bank(u)).rearrange("p (m t) -> p m t", m=4), ACT.Copy).then_inc(sem["proj_act"], 1)
                act.wait_ge(sem["sp_in"], rise(l, "sp_in", 1))
                go(spe, spa, ACT.Exp, scale=-1.0).then_inc(chain_act, 1)
                act.wait_ge(chain_act, links.next())
                go(spe, spe, ACT.Ln, bias=1.0).then_inc(chain_act, 1)
                act.wait_ge(chain_act, links.next())
                go(beta[:], gin[:, :, 8:16], ACT.Exp, scale=-1.0).then_inc(chain_act, 1)
                act.wait_ge(chain_act, links.next())
                go(nega[:], Q("a_log"), ACT.Exp).then_inc(sem["sp_act"], 1)

                def copy_unit(u, out):
                    act.wait_ge(sem["proj_mm"], rise(l, "proj_mm", u + 1))
                    go(out, bank(proj_bank(u)), ACT.Copy).then_inc(sem["proj_act"], 1)

                copy_unit(6, A("natqk")[:, 0:512])
                copy_unit(7, A("natqk")[:, 512:1024])
                act.wait_ge(sem["proj_mm"], rise(l, "proj_mm", 9))
                go(zr, bank(proj_bank(8)), ACT.Silu).then_inc(sem["proj_act"], 1)
                copy_unit(9, A("retqk")[:, 0:512])
                copy_unit(10, A("retqk")[:, 512:1024])
                act.wait_ge(sem["proj_mm"], rise(l, "proj_mm", 12))
                go(zg, bank(proj_bank(11)), ACT.Silu).then_inc(sem["proj_act"], 1)
                act.wait_ge(sem["conv_dve"], rise(l, "conv_dve", 1))
                go(A("qkv"), A("qkv"), ACT.Silu).then_inc(sem["silu_act"], 1)
                copy_unit(13, A("sx"))
                act.wait_ge(sem["qk_mm"], rise(l, "qk_mm", 1))
                go(norm[:, 0:1024], ps[:, 0:2, :].rearrange("p b n -> p (b n)"), ACT.Ln, bias=EPS).then_inc(chain_act, 1)
                act.wait_ge(chain_act, links.next())
                go(norm[:, 1024:2048], ps[:, 2:4, :].rearrange("p b n -> p (b n)"), ACT.Ln, bias=EPS, scale=1.0 / HD).then_inc(chain_act, 1)
                act.wait_ge(chain_act, links.next())
                go(norm[:, 0:512], norm[:, 0:512], ACT.Exp, scale=-0.5, bias=math.log(QK_SCALE))
                go(norm[:, 512:2048], norm[:, 512:2048], ACT.Exp, scale=-0.5).then_inc(sem["qk_rs"], 1)
                ada_rows(ADA_FIRST, 7)
                act.wait_ge(sem["qk_dve"], rise(l, "qk_dve", 1))
                go(gpad[0:64, :, :, 0, :].rearrange("p t s c -> p (t s) c"),
                   qkv[0:64, 0:4, :].rearrange("p m (s c) -> p (m s) c", s=2), ACT.Copy)
                go(npad[0:64, :, :, 0, :].rearrange("p j s c -> p (j s) c"),
                   natqk[0:64, 2:4, :].rearrange("p m (s c) -> p (m s) c", s=2), ACT.Copy).then_inc(sem["pad_act"], 1)
                act.wait_ge(sem["rope_dve"], rise(l, "rope_dve", 1))
                go(rpad[0:64, :, :, 0, :].rearrange("p j s c -> p (j s) c"),
                   retqk[0:64, 0:2, :].rearrange("p m (s c) -> p (m s) c", s=2), ACT.Copy).then_inc(sem["rpad_act"], 1)
                act.wait_ge(sem["gates_dve"], rise(l, "gates_dve", 1))
                act.wait_ge(sem["sc_dve"], rise(l, "sc_dve", 1))
                for h in range(HEADS):
                    go(ef[:, h, :], C("lag_f"), ACT.Exp, scale=lg[:, h:h + 1])
                    go(eb[:, h, :], C("lag_b"), ACT.Exp, scale=lg[:, 4 + h:5 + h])
                go(kdc[:], kdc[:], ACT.Exp, bias=math.log(QK_SCALE))
                for d, x in enumerate(("cross_f", "cross_b")):
                    for j in range(2):
                        last = go(qx[:, d, j, :], C(x), ACT.Exp, scale=lg[:, 8 + 2 * d + j:9 + 2 * d + j])
                last.then_inc(sem["ret_exp"], 1)
                act.wait_ge(sem["nat_max"], rise(l, "nat_max", 1))
                for n in range(HEADS):
                    t = nat_s[:, n * P:(n + 1) * P]
                    go(t, t, ACT.Exp, bias=natm[:, n:n + 1], accum_out=natsum[:, n:n + 1])
                for h in range(HEADS):
                    for part in range(2):
                        n = HEADS * (1 + part) + h
                        t = nat_s[:, n * P:(n + 1) * P]
                        last = go(t, t, ACT.Exp, bias=natm[:, 4 + h:5 + h], accum_out=natsum[:, n:n + 1])
                last.then_inc(sem["nat_exp"], 1)
                ada_rows(ADA_FIRST + 1, 3)
                act.wait_ge(sem["nat_tr"], rise(l, "nat_tr", 1))
                go(nat_t, ps[:, 0:3, :].rearrange("p b n -> p (b n)"), ACT.Copy).then_inc(sem["nat_pt"], 1)
                act.wait_ge(sem["nat_o"], rise(l, "nat_o", 1))
                act.wait_ge(sem["proj_mm"], rise(l, "proj_mm", 15))
                go(hT[:, 4:6, :].rearrange("p m t -> p (m t)"), bank(3), ACT.Copy).then_inc(sem["nat_out"], 1)
                act.wait_ge(sem["ret_var"], rise(l, "ret_var", 1))
                go(qx[:].rearrange("p d j c -> p (d j c)"), bank(3), ACT.Ln, bias=EPS, scale=1.0 / HD).then_inc(chain_act, 1)
                act.wait_ge(chain_act, links.next())
                go(qx[:].rearrange("p d j c -> p (d j c)"), qx[:].rearrange("p d j c -> p (d j c)"), ACT.Exp, scale=-0.5).then_inc(sem["ret_rs"], 1)

                for s in range(NS):
                    act.wait_ge(sem["gcol_mm"], rise(l, "gcol_mm", s + 1))
                    go(egc[:], ps[:, 6, 0:16], ACT.Exp).then_inc(sem["gcol_exp"], 1)
                    for d in range(2):
                        act.wait_ge(sem["gr_min"], rise(l, "gr_min", 2 * s + d + 1))
                        m = group(d, 0).rearrange("p h c -> p (h c)")
                        go(m, m, ACT.Exp).then_inc(sem["gr_exp"], 1)
                    act.wait_ge(sem["vt_mm"], rise(l, "vt_mm", s + 1))
                    if s == 0:
                        act.wait_ge(sem["ks_mm"], rise(l, "ks_mm", 1))
                    go(vtok[:, s, :], ps[:, 7, 0:256], ACT.Copy).then_inc(sem["vt_act"], 1)
                    if s == 1:
                        act.wait_ge(sem["qd_mm"], rise(l, "qd_mm", 1))
                        go(qdec.rearrange("p g j c -> p (g j c)"), bank(7), ACT.Exp).then_inc(sem["qd_exp"], 1)
                    ada_rows(ADA_FIRST + 2 + 2 * s, 6 + s)
                    for b in range(1, LEVELS):
                        for g in range(2):
                            act.wait_ge(sem["inv_dmm"], rise(l, "inv_dmm", (s * LEVELS + b) * 2 + g + 1))
                            go(group(g, 5).rearrange("p h c -> p (h c)"), bank(2 + g), ACT.Copy).then_inc(sem["inv_dev"], 1)
                        if s == 0 and b == LEVELS - 1:
                            ada_rows(ADA_FIRST + 3, 6)
                act.wait_ge(sem["go_dve"], rise(l, "go_dve", 2))
                go(group(0, 3).rearrange("p h c -> p (h c)"), og.rearrange("p j s c -> p (j s c)"), ACT.Square).then_inc(sem["gn_sq"], 1)
                act.wait_ge(sem["gn_mm"], rise(l, "gn_mm", 1))
                t = group(0, 4).rearrange("p h c -> p (h c)")
                go(t, bank(7), ACT.Ln, bias=EPS, scale=1.0 / HD).then_inc(chain_act, 1)
                act.wait_ge(chain_act, links.next())
                go(t, t, ACT.Exp, scale=-0.5).then_inc(sem["gn_rs"], 1)

                def high(e, j, part, name, freed=None):
                    if part == 0:
                        act.wait_ge(slot_in[j], (l * ((HEAD_SLOTS + N_EXPERTS) // RING) + HEAD_SLOTS // RING + 1) * 16 + (e - j) * (16 // RING))
                    if freed:
                        act.wait_ge(sem[freed], rise(l, freed, e))
                    at = part * 2048
                    go(w_hi[:, at:at + 2048], ring[j][:, at:at + 2048], ACT.Copy).then_inc(sem[name], 1)

                act.wait_ge(sem["gn_out"], rise(l, "gn_out", 1))
                high(0, 0, 0, "hi_gate")
                high(0, 0, 1, "hi_up")
                norm_stats(2)
                act.wait_ge(sem["route_d1"], rise(l, "route_d1", 1))
                go(rs_[:, 0:8], rs_[:, 0:8], ACT.Exp).then_inc(sem["route_exp1"], 1)
                act.wait_ge(sem["route_d2"], rise(l, "route_d2", 1))
                go(rs_[:, 12:14], rs_[:, 12:14], ACT.Exp).then_inc(sem["route_exp2"], 1)
                act.sem_clear(chain_act)
                links.restart()

                def step(e, j, first=1, ahead=2):
                    if ahead > 0:
                        act.wait_ge(sem["gate_mm"], rise(l, "gate_mm", e + 2))
                        if first > 0:
                            act.wait_ge(sem["down_mm"], rise(l, "down_mm", e))
                        go(sg[:, (j + 1) % 2].rearrange("p f t -> p (f t)"), bank(4 + 2 * ((j + 1) % 2)), ACT.Silu).then_inc(sem["silu"], 1)
                    if ahead > 1:
                        high(e + 2, (j + 2) % RING, 0, "hi_gate", "gate_mm")
                        high(e + 2, (j + 2) % RING, 1, "hi_up", "up_mm")
                    if ahead > 0:
                        act.wait_ge(sem["act_dve"], rise(l, "act_dve", e + 2))
                        go(gated_hi[:, (j + 1) % 2].rearrange("p f t -> p (f t)"), sg[:, (j + 1) % 2].rearrange("p f t -> p (f t)"),
                           ACT.Copy).then_inc(sem["act_hi"], 1)
                        high(e + 1, (j + 1) % RING, 2, "hi_down", "down_mm" if first >= 0 else None)

                def high_half(e, j, name, freed, part):
                    if part == 0:
                        act.wait_ge(slot_in[j], (l * ((HEAD_SLOTS + N_EXPERTS) // RING) + HEAD_SLOTS // RING + 1) * 16 + (e - j) * (16 // RING))
                    act.wait_ge(sem[freed], rise(l, freed, e))
                    cols = slice(part * 1024, part * 1024 + 1024)
                    go(w_hi[:, 0:4096].rearrange("p (w n) -> p w n", w=2)[:, :, cols],
                       ring[j][:, 0:4096].rearrange("p (w n) -> p w n", w=2)[:, :, cols], ACT.Copy).then_inc(sem[name], 1)

                def gathered_step(e, i, turn, ahead=2):
                    if ahead > 1:
                        high_half(e + 2, (i + 2) % RING, "hi_a", "half_mm", 0)
                    if ahead > 0:
                        act.wait_ge(sem["gu_mm"], rise(l, "gu_mm", e + 2))
                        go(g_silu[:, (i + 1) % 2], bank((i + 1) % 2, FF), ACT.Silu).then_inc(sem["g_silu"], 1)
                    if ahead > 1:
                        high_half(e + 2, (i + 2) % RING, "hi_b", "gu_mm", 1)
                    if i == PER_GROUP - 1:
                        act.wait_ge(sem["down_mm"], rise(l, "down_mm", e + 1))
                        go(hg_hi[:, :, bass.ds(turn * P, P)], ps[:, 4:6, :].rearrange("p b (k c) -> p (b k) c", c=P), ACT.Copy).then_inc(sem["yg_hi"], 1)

                for n in range(4):
                    act.wait_ge(sem["ht_mm"], rise(l, "ht_mm", n + 1))
                    go(ht_hi[:, n // 2, (n % 2) * 512:(n % 2 + 1) * 512], bank(2 + n), ACT.Copy).then_inc(sem["ht_hi"], 1)
                act.wait_ge(const_in, 32)
                act.wait_ge(sem["flag"], rise(l, "flag", 1))
                fullest = act.value_load(most[0:1, 0:1], min_val=0, max_val=TOK)
                with act.If(fullest < P + 1):
                    for k in range(KT):
                        act.wait_ge(sem["ga_mm"], rise(l, "ga_mm", k + 1))
                        go(hg_hi[:, k, :], bank((6, 7, 0, 1)[k % 4]), ACT.Copy).then_inc(sem["ga_hi"], 1)
                    for n in range(2):
                        act.wait_ge(sem["st_mm"], rise(l, "st_mm", n + 1))
                        go(sel_t[:, 2 * n:2 * n + 2, :].rearrange("p g t -> p (g t)"), bank(2 + n), ACT.Copy).then_inc(sem["st_act"], 1)
                    gathered_step(-1, -1, 0)
                    with act.Fori(0, N_GROUPS - 1) as turn:
                        for i in range(PER_GROUP):
                            gathered_step(turn * PER_GROUP + i, i, turn)
                    for i in range(PER_GROUP):
                        gathered_step(N_EXPERTS - PER_GROUP + i, i, N_GROUPS - 1, ahead=PER_GROUP - 1 - i)
                    for name, n in (("cb_act", 8), ("h_hi", 1), ("silu", 32), ("hi_gate", 31), ("hi_up", 31), ("hi_down", 32), ("act_hi", 32)):
                        act.sem_inc(sem[name], n)
                with act.Else():
                    for q in range(0, N_EXPERTS // 2, 2):
                        act.wait_ge(sem["cb_mm"], rise(l, "cb_mm", q + 1))
                        go(cb[:, 2 * q:2 * q + 2, :].rearrange("p e t -> p (e t)"), bank(q % 4), ACT.Copy).then_inc(sem["cb_act"], 1)
                    act.wait_ge(sem["route_mm"], rise(l, "route_mm", 1))
                    go(h_hi, hT[:], ACT.Copy).then_inc(sem["h_hi"], 1)
                    step(-1, RING - 1, first=-1)
                    step(0, 0, first=0)
                    for e in range(1, RING):
                        step(e, e)
                    with act.Fori(1, N_EXPERTS // RING - 1) as turn:
                        for j in range(RING):
                            step(turn * RING + j, j)
                    for e in range(N_EXPERTS - RING, N_EXPERTS - 1):
                        step(e, e % RING, ahead=N_EXPERTS - 1 - e)
                    for name in ("ga_hi", "st_act", "hi_a", "hi_b", "g_silu", "yg_hi"):
                        act.sem_inc(sem[name], PER[name])

        @block.vector
        def _(dve):
            V = nc.vector
            tt, ts, stt, copy = V.tensor_tensor, V.tensor_scalar, V.scalar_tensor_tensor, V.tensor_copy
            V.memset(natm[:], 0.0).then_inc(sem["layer_done"], 1)
            dve.wait_ge(const_in, 32)
            with dve.Fori(0, DEPTH) as l:
                links = Links()
                dve.wait_ge(sem["layer_done"], rise(l, "layer_done", 1))
                dve.wait_ge(sem["param_dma"], rise(l, "param_dma", 16))
                tt(Q("nat_bias").rearrange("p (a c) -> p a c", c=GRID_W), Q("nat_bias").rearrange("p (a c) -> p a c", c=GRID_W),
                          bc(C("colmask").unsqueeze(1), 2 * HEADS, GRID_W), ALU.add).then_inc(chain_dve, 1)
                dve.wait_ge(chain_dve, links.next())

                def ada_columns(i, bank_out):
                    dve.wait_ge(sem["ada_tr"], rise(l, "ada_tr", i + 1))
                    m = slice(ADA_TILES * i, ADA_TILES * (i + 1))
                    tt(adaT[:, m, :], ps[:, bank_out, 0:2 * ADA_TILES].rearrange("p (m s) -> p m s", s=NS),
                       bc(Q("ada_b")[:, m].unsqueeze(2), ADA_TILES, NS), ALU.add).then_inc(sem["ada_dve"], 1)

                def norm_scale(n, at, name):
                    stt(scale1[:, n], adaT[:, at:at + KT, :], 1.0, bc(Q(name).unsqueeze(2), KT, NS), ALU.add, ALU.mult).then_inc(chain_dve, 1)
                    dve.wait_ge(chain_dve, links.next())

                for i in range(ADA_FIRST):
                    ada_columns(i, 5)
                dve.wait_ge(sem["ada_dve"], rise(l, "ada_dve", ADA_FIRST))
                norm_scale(0, 8, "norm_mix")

                def modulate(n):
                    dve.wait_ge(sem["norm_rs"], rise(l, "norm_rs", n))
                    for half in range(2):
                        k4 = slice(4 * half, 4 * half + 4)
                        tt(hT[:, k4, :], xT[:, k4, :], bc(rstd[:].unsqueeze(1), 4, TOK), ALU.mult).then_inc(sem["h_scaled"], 1)
                    dve.wait_ge(sem["h_scaled"], rise(l, "h_scaled", 2 * n))
                    which, sh = (0, 0) if n == 1 else (1, 24)
                    for k in range(4, KT):
                        for s in range(NS):
                            t = hT[:, k, s * P:(s + 1) * P]
                            last = ts(t, t, scale1[:, which, k, s:s + 1], adaT[:, sh + k, s:s + 1], ALU.mult, ALU.add)
                    last.then_inc(sem["h_dve"], 1)

                modulate(1)
                dve.wait_ge(sem["zeroed"], rise(l, "zeroed", 1))
                for s in range(NS):
                    dve.wait_ge(sem["proj_mm"], rise(l, "proj_mm", 4 + s))
                    v_in = bank(proj_bank(3 + s)).rearrange("p (a i d) -> p a i d", i=2, d=HD)
                    v_out = vp[:, s].rearrange("p r j n -> p (r j) n")
                    copy(v_out[:, :, 0:HD], v_in[:, :, 0, :])
                    copy(v_out[:, :, P + HD:256], v_in[:, :, 1, :]).then_inc(sem["proj_dve"], 1)
                dve.wait_ge(sem["proj_mm"], rise(l, "proj_mm", 6))
                copy(gin, ps[:, proj_bank(5), 0:32].rearrange("p (s n) -> p s n", s=2)).then_inc(sem["proj_dve"], 1)
                dve.wait_ge(sem["proj_dve"], rise(l, "proj_dve", 3))
                tt(spx[:, 0:16].rearrange("p (s n) -> p s n", s=2), gin[:, :, 0:8], bc(Q("dt_bias").unsqueeze(1), 2, 8), ALU.add)
                gam = param[:, PARAM["gamma_cols"].start:PARAM["gamma_rows"].stop]
                ts(spx[:, 16:28], gam, -1.0, None, ALU.mult).then_inc(chain_dve, 1)
                dve.wait_ge(chain_dve, links.next())
                stt(spa, spx[:], -1.0, spx[:], ALU.mult, ALU.max).then_inc(sem["sp_in"], 1)

                def conv(out, inp, taps, tiles, at=0):
                    for tap in range(3):
                        for m in range(tiles):
                            k = taps[:, 3 * m + tap:3 * m + tap + 1]
                            t = inp[:, m, :, tap:tap + P]
                            o = out(m)
                            last = ts(o, t, k, None, ALU.mult) if tap == 0 else stt(o, t, k, o, ALU.mult, ALU.add)
                        if tap < 2:
                            last.then_inc(chain_dve, 1)
                            dve.wait_ge(chain_dve, links.next())
                    return last

                dve.wait_ge(sem["proj_act"], rise(l, "proj_act", 3))
                conv(lambda m: qkv[:, m, :].rearrange("p (s t) -> p s t", s=2), raw, Q("conv_gdn"), 6).then_inc(sem["conv_dve"], 1)
                dve.wait_ge(sem["sp_act"], rise(l, "sp_act", 1))
                stt(spx[:], spx[:], 0.0, spe, ALU.max, ALU.add).then_inc(chain_dve, 1)
                dve.wait_ge(chain_dve, links.next())
                stt(gdec[:], spx[:, 0:16].rearrange("p (s n) -> p s n", s=2), -1.0, bc(nega[:].unsqueeze(1), 2, 8), ALU.mult, ALU.mult)
                tt(gneg[:], spx[:, 0:16].rearrange("p (s n) -> p s n", s=2), bc(nega[:].unsqueeze(1), 2, 8), ALU.mult)
                ts(lg[:], spx[:, 16:28], -1.0, None, ALU.mult)
                ts(beta[:], beta[:], 1.0, None, ALU.add).then_inc(chain_dve, 1)
                dve.wait_ge(chain_dve, links.next())
                V.reciprocal(beta[:], beta[:]).then_inc(chain_dve, 1)
                dve.wait_ge(chain_dve, links.next())
                for d in range(2):
                    last = ts(kdc[:, 4 * d:4 * d + 4], lg[:, 4 * d:4 * d + 4], C("idx")[:, d:d + 1], None, ALU.mult)
                last.then_inc(sem["gates_dve"], 1)
                dve.wait_ge(sem["proj_mm"], rise(l, "proj_mm", 13))
                copy(A("sb"), bank(proj_bank(12))).then_inc(sem["proj_dve"], 1)
                dve.wait_ge(sem["silu_act"], rise(l, "silu_act", 1))
                tt(norm[:, 0:1024], A("qkv")[:, 0:1024], A("qkv")[:, 0:1024], ALU.mult)
                dve.wait_ge(sem["proj_act"], rise(l, "proj_act", 5))
                tt(norm[:, 1024:2048], A("natqk"), A("natqk"), ALU.mult).then_inc(sem["qk_sq"], 1)
                dve.wait_ge(sem["proj_mm"], rise(l, "proj_mm", 15))
                dve.wait_ge(sem["proj_act"], rise(l, "proj_act", 10))
                tt(ub[:, :, :, 1:129].rearrange("p m s t -> p (m s) t"), bank(proj_bank(14)).rearrange("p (m t) -> p m t", m=4),
                   sxT.rearrange("p m s t -> p (m s) t"), ALU.mult).then_inc(sem["proj_dve"], 1)
                dve.wait_ge(sem["proj_dve"], rise(l, "proj_dve", 5))
                conv(lambda m: hT[:, 6 + m, :].rearrange("p (s t) -> p s t", s=2), ub, Q("conv_sc"), 2).then_inc(chain_dve, 1)
                dve.wait_ge(chain_dve, links.next())
                mix_sc = hT[:, 6:8, :].rearrange("p m t -> p (m t)")
                tt(mix_sc, mix_sc, A("sb"), ALU.mult).then_inc(sem["sc_dve"], 1)
                dve.wait_ge(sem["qk_rs"], rise(l, "qk_rs", 1))
                dve.wait_ge(sem["sc_dve"], rise(l, "sc_dve", 1))
                tt(A("qkv")[:, 0:1024], A("qkv")[:, 0:1024], norm[:, 0:1024], ALU.mult)
                stt(A("natqk")[:, 0:512], A("natqk")[:, 0:512], Q("q_norm"), norm[:, 1024:1536], ALU.mult, ALU.mult)
                stt(A("natqk")[:, 512:1024], A("natqk")[:, 512:1024], Q("k_norm"), norm[:, 1536:2048], ALU.mult, ALU.mult).then_inc(sem["qk_dve"], 1)
                ada_columns(ADA_FIRST, 6)
                dve.wait_ge(sem["rope_mm"], rise(l, "rope_mm", 1))
                dve.wait_ge(sem["qk_dve"], rise(l, "qk_dve", 1))
                rsin = norm[:, 0:512].rearrange("p (m t) -> p m t", m=4)
                tt(rsin, bank(4).rearrange("p (m t) -> p m t", m=4), bc(C("sin").unsqueeze(1), 4, P), ALU.mult)
                tt(retqk[:, :, P:TOK], retqk[:, :, P:TOK], bc(C("cos").unsqueeze(1), 4, P), ALU.mult).then_inc(chain_dve, 1)
                dve.wait_ge(chain_dve, links.next())
                tt(retqk[:, :, P:TOK], retqk[:, :, P:TOK], rsin, ALU.add).then_inc(sem["rope_dve"], 1)

                dve.wait_ge(sem["rope_dve"], rise(l, "rope_dve", 1))
                dve.wait_ge(sem["nat_mm"], rise(l, "nat_mm", 1))
                ts(nat_s[:, 0:512], bank(0), QK_SCALE, None, ALU.mult)
                stt(nat_s[:, 512:1024], bank(1), QK_SCALE, Q("nat_bias"), ALU.mult, ALU.add)
                ts(nat_s[:, 1024:1536], bank(2), QK_SCALE, None, ALU.mult).then_inc(chain_dve, 1)
                dve.wait_ge(chain_dve, links.next())
                V.tensor_reduce(natm[:], nat_s.rearrange("p (n k) -> p n k", k=P), AX.X, ALU.max).then_inc(chain_dve, 1)
                dve.wait_ge(chain_dve, links.next())
                tt(natm[:, 4:8], natm[:, 4:8], natm[:, 8:12], ALU.max).then_inc(chain_dve, 1)
                dve.wait_ge(chain_dve, links.next())
                ts(natm[:, 0:8], natm[:, 0:8], -1.0, None, ALU.mult).then_inc(sem["nat_max"], 1)
                dve.wait_ge(sem["nat_exp"], rise(l, "nat_exp", 1))
                tt(natsum[:, 4:8], natsum[:, 4:8], natsum[:, 8:12], ALU.add).then_inc(chain_dve, 1)
                dve.wait_ge(chain_dve, links.next())
                V.reciprocal(natsum[:, 0:8], natsum[:, 0:8]).then_inc(chain_dve, 1)
                dve.wait_ge(chain_dve, links.next())
                for n, r in enumerate((0, 4, 4)):
                    t = heads(nat_s[:, n * 512:(n + 1) * 512])
                    last = tt(t, t, bc(natsum[:, r:r + 4].unsqueeze(2), 4, P), ALU.mult)
                last.then_inc(sem["nat_p"], 1)

                dve.wait_ge(sem["ret_exp"], rise(l, "ret_exp", 1))
                stt(ef, ef, QK_SCALE, bc(upto[0].unsqueeze(1), HEADS, P), ALU.mult, ALU.mult)
                stt(eb, eb, QK_SCALE, bc(upto[1].unsqueeze(1), HEADS, P), ALU.mult, ALU.mult).then_inc(chain_dve, 1)
                dve.wait_ge(chain_dve, links.next())
                tt(ef, ef, eb, ALU.add).then_inc(chain_dve, 1)
                dve.wait_ge(chain_dve, links.next())
                tt(qx, qx, bc(retqk[:, 0:2, P:TOK].unsqueeze(1), 2, 2, P), ALU.mult)
                dve.wait_ge(sem["ret_mm"], rise(l, "ret_mm", 1))
                dve.wait_ge(sem["nat_tr"], rise(l, "nat_tr", 1))
                tt(ret_a.rearrange("p s h c -> p s (h c)"), ps[:, 6:8, :],
                   bc(ef.rearrange("p h c -> p (h c)").unsqueeze(1), 2, 512), ALU.mult).then_inc(sem["ret_a"], 1)
                dve.wait_ge(sem["ret_kt"], rise(l, "ret_kt", 1))
                for d in range(2):
                    last = tt(ret_kd[:, d].rearrange("p (h n) -> p h n", h=HEADS), ps[:, 5, 0:256].rearrange("p (h n) -> p h n", h=HEADS),
                              bc(kdc[:, 4 * d:4 * d + 4].unsqueeze(2), HEADS, HD), ALU.mult)
                last.then_inc(sem["ret_kd"], 1)
                ada_columns(ADA_FIRST + 1, 4)
                dve.wait_ge(sem["ret_o"], rise(l, "ret_o", 1))
                rog, rsq = ef.rearrange("p h c -> p (h c)"), eb.rearrange("p h c -> p (h c)")
                copy(rog, bank(4)).then_inc(sem["ret_og"], 1)
                dve.wait_ge(sem["ret_sf"], rise(l, "ret_sf", 1))

                def states(out, first):
                    for i in range(2):
                        lo = slice(64 * i, 64 * i + 64)
                        last = copy(out[lo], ps[lo, first:first + 2, :].rearrange("p d (j n) -> p d j n", j=2)[:, :, :, 192 * i:192 * i + HD])
                    return last

                states(state, 0).then_inc(sem["ret_st"], 1)
                dve.wait_ge(sem["ret_mean"], rise(l, "ret_mean", 1))
                stt(rog, bank(2), -1.0 / HD, rog, ALU.mult, ALU.add).then_inc(chain_dve, 1)
                dve.wait_ge(chain_dve, links.next())
                tt(rsq, rog, rog, ALU.mult).then_inc(sem["ret_sq"], 1)
                dve.wait_ge(sem["ret_rs"], rise(l, "ret_rs", 1))
                tt(rog, rog, qx.rearrange("p d j c -> p (d j c)"), ALU.mult).then_inc(chain_dve, 1)
                dve.wait_ge(chain_dve, links.next())
                tt(hT[:, 2:4, :].rearrange("p m t -> p (m t)"), rog, zr, ALU.mult).then_inc(sem["ret_out"], 1)
                dve.wait_ge(kv_out, l * 48 + 48)
                dve.wait_ge(sem["ret_out"], rise(l, "ret_out", 1))
                dve.wait_ge(sem["nat_out"], rise(l, "nat_out", 1))
                copy(qdec.rearrange("p d j (i n) -> p (d j i) n", i=2), bc(gdec[:, 1, :].unsqueeze(2), 8, HD)).then_inc(sem["qd_g"], 1)

                for s in range(NS):
                    dve.wait_ge(sem["gr_mm"], rise(l, "gr_mm", s + 1))
                    for d in range(2):
                        ts(group(d, 0).rearrange("p h c -> p (h c)"), bank(2 + d), 0.0, None, ALU.min).then_inc(sem["gr_min"], 1)
                    for d in range(2):
                        dve.wait_ge(sem["gr_exp"], rise(l, "gr_exp", 2 * s + d + 1))
                        tt(group(d, 0), group(d, 0), bc(upto[d].unsqueeze(1), HEADS, P), ALU.mult).then_inc(chain_dve, 1)
                        dve.wait_ge(chain_dve, links.next())
                        m = group(d, 0).rearrange("p (j i) c -> p j (i c)", j=2)
                        tt(group(d, 1).rearrange("p (j i) c -> p j (i c)", j=2), ps[:, 0:2, 0:256], m, ALU.mult)
                        tt(group(d, 2).rearrange("p (j i) c -> p j (i c)", j=2), ps[:, 0:2, 256:512], m, ALU.mult).then_inc(chain_dve, 1)
                        dve.wait_ge(chain_dve, links.next())
                        lt = group(d, 2).rearrange("p h c -> p (h c)")
                        last = tt(lt, lt, bank(4 + d), ALU.mult)
                        if d == 0:
                            last.then_inc(chain_dve, 1)
                            dve.wait_ge(chain_dve, links.next())
                    last.then_inc(sem["gr_dec"], 1)
                    dve.wait_ge(sem["vt_act"], rise(l, "vt_act", s + 1))
                    dve.wait_ge(sem["gcol_exp"], rise(l, "gcol_exp", s + 1))
                    dve.wait_ge(sem["ks_mm"], rise(l, "ks_mm", s + 1))
                    vh = vtok[:, s, :].rearrange("p (h n) -> p h n", h=HEADS)
                    for d in range(2):
                        zd = z[:, d, :].rearrange("p (h n) -> p h n", h=HEADS)
                        bcol = bc(beta[:, s, 4 * d:4 * d + 4].unsqueeze(2), HEADS, HD)
                        if s == 0:
                            last = tt(zd, vh, bcol, ALU.mult)
                            continue
                        ks = ps[:, 6, 256 * d:256 * d + 256].rearrange("p (h n) -> p h n", h=HEADS)
                        tt(zd, ks, bc(egc[:, 4 * d:4 * d + 4].unsqueeze(2), HEADS, HD), ALU.mult).then_inc(chain_dve, 1)
                        dve.wait_ge(chain_dve, links.next())
                        tt(zd, vh, zd, ALU.subtract).then_inc(chain_dve, 1)
                        dve.wait_ge(chain_dve, links.next())
                        last = tt(zd, zd, bcol, ALU.mult)
                    last.then_inc(sem["z_dve"], 1)
                    if s == 0:
                        for d in range(2):
                            last = tt(kdg[:, d, :].rearrange("p (h n) -> p h n", h=HEADS), ps[:, 7, 256:512].rearrange("p (h n) -> p h n", h=HEADS),
                                      bc(egc[:, 8 + 4 * d:12 + 4 * d].unsqueeze(2), HEADS, HD), ALU.mult)
                        last.then_inc(sem["kd_dve"], 1)
                    else:
                        dve.wait_ge(sem["qd_exp"], rise(l, "qd_exp", 1))
                        tt(qdec, qdec, bc(qkv[:, 0:2, P:TOK].unsqueeze(1), 2, 2, P), ALU.mult).then_inc(sem["qd_dve"], 1)
                    for b in range(LEVELS):
                        for g in range(2):
                            n = (s * LEVELS + b) * 2 + g + 1
                            t, t_t = group(g, 3), group(g, 4)
                            if b == 0:
                                dve.wait_ge(sem["inv_dmm"], rise(l, "inv_dmm", n))
                                tt(t, heads(bank(2 + g)), bc(ident.unsqueeze(1), HEADS, P), ALU.add)
                                tt(t_t, group(g, 6), bc(ident.unsqueeze(1), HEADS, P), ALU.add).then_inc(sem["inv_upd"], 1)
                                continue
                            dve.wait_ge(sem["inv_umm"], rise(l, "inv_umm", (s * (LEVELS - 1) + b - 1) * 2 + g + 1))
                            dve.wait_ge(sem["inv_upd"], rise(l, "inv_upd", n - 2))
                            if b < LEVELS - 1:
                                tt(t, t, heads(bank(4 + g)), ALU.add)
                            tt(t_t, t_t, heads(bank(g)), ALU.add).then_inc(sem["inv_upd"], 1)
                        if b == 0:
                            ada_columns(ADA_FIRST + 2 + 2 * s, 7 - s)
                        elif s == 0 and b == LEVELS - 1:
                            ada_columns(ADA_FIRST + 3, 7)
                    dve.wait_ge(sem["vnp_zero"], rise(l, "vnp_zero", 1))
                    for g in range(2):
                        dve.wait_ge(sem["vn_mm"], rise(l, "vn_mm", 2 * s + g + 1))
                        vn = ps[:, 2 + g, 0:256].rearrange("p (j i n) -> p j i n", j=2, i=2)
                        pad = group(g, 7).rearrange("p (j i) c -> p j i c", j=2)
                        copy(pad[:, :, 0, 0:HD], vn[:, :, 0, :])
                        copy(pad[:, :, 1, HD:P], vn[:, :, 1, :]).then_inc(sem["vn_dve"], 1)
                    dve.wait_ge(sem["go_mm"], rise(l, "go_mm", s + 1))
                    copy(og[:, :, s, :], ps[:, 6, 0:256].rearrange("p (j c) -> p j c", j=2)).then_inc(sem["go_dve"], 1)
                    if s == 0:
                        dve.wait_ge(sem["gs_mm"], rise(l, "gs_mm", 1))
                        dve.wait_ge(state_out, l * 32 + 16)
                        states(state, 4).then_inc(sem["gs_st"], 1)
                dve.wait_ge(sem["gn_rs"], rise(l, "gn_rs", 1))
                gn = group(0, 3).rearrange("p h c -> p (h c)")
                stt(gn, og.rearrange("p j s c -> p (j s c)"), Q("gdn_norm"), group(0, 4).rearrange("p h c -> p (h c)"), ALU.mult, ALU.mult).then_inc(chain_dve, 1)
                dve.wait_ge(chain_dve, links.next())
                tt(hT[:, 0:2, :].rearrange("p m t -> p (m t)"), gn, zg, ALU.mult).then_inc(sem["gn_out"], 1)

                def residual(gate, tiles):
                    for f in tiles:
                        for s in range(NS):
                            t = xT[:, f, s * P:(s + 1) * P]
                            last = stt(t, ps[:, f // 2, (f % 2) * TOK + s * P:(f % 2) * TOK + (s + 1) * P],
                                       adaT[:, gate + f, s:s + 1], t, ALU.mult, ALU.add)
                    return last

                def low(e, j, part, name, made):
                    dve.wait_ge(sem[made], rise(l, made, e + 1))
                    at = part * 2048
                    tt(ring_r[j][:, at:at + 2048], ring[j][:, at:at + 2048], w_hi[:, at:at + 2048], ALU.subtract).then_inc(sem[name], 1)

                low(0, 0, 0, "lo_gate", "hi_gate")
                low(0, 0, 1, "lo_up", "hi_up")
                for i, tiles in enumerate(OUT_TILES):
                    dve.wait_ge(sem["out_mm"], rise(l, "out_mm", i + 1))
                    residual(16, range(sum(OUT_TILES[:i]), sum(OUT_TILES[:i]) + tiles)).then_inc(sem["res_dve"], 1)
                dve.wait_ge(sem["ada_dve"], rise(l, "ada_dve", ADA_SLOTS))
                norm_scale(1, 32, "norm_ffn")
                dve.wait_ge(sem["res_dve"], rise(l, "res_dve", OUT_SLOTS))
                modulate(2)

                dve.wait_ge(sem["route_mm"], rise(l, "route_mm", 1))
                gd, tmp4, oh4 = (rs_[:, a:a + 8].rearrange("p (s n) -> p s n", s=2) for a in (0, 20, 28))
                els, oh1, oh2, tmp8, c8 = (rs_[:, a:a + 16].rearrange("p (s n) -> p s n", s=2) for a in (36, 52, 68, 84, 100))
                gm, gs, e2, m1, m2, tw, gw, pick = (rs_[:, a:a + 2] for a in (8, 10, 12, 14, 16, 18, 116, 118))
                prio4, prio8 = C("prio")[:, 4:8], C("prio")
                dve.wait_ge(state_out, l * 32 + 32)
                tt(rt, ps[:, 0, 0:128].rearrange("p (s n) -> p s n", s=2)[:, :, 0:ROUTER], bc(Q("router_b").unsqueeze(1), 2, ROUTER), ALU.add).then_inc(chain_dve, 1)
                dve.wait_ge(chain_dve, links.next())
                V.tensor_reduce(gm, rt[:, :, 0:4], AX.X, ALU.max).then_inc(chain_dve, 1)
                dve.wait_ge(chain_dve, links.next())
                tt(gd, rt[:, :, 0:4], bc(gm.unsqueeze(2), 2, 4), ALU.subtract).then_inc(chain_dve, 1)
                dve.wait_ge(chain_dve, links.next())
                stt(tmp4, gd, 0.0, bc(prio4.unsqueeze(1), 2, 4), ALU.is_ge, ALU.mult).then_inc(sem["route_d1"], 1)
                dve.wait_ge(sem["route_d1"], rise(l, "route_d1", 1))
                V.tensor_reduce(pick, tmp4, AX.X, ALU.max).then_inc(chain_dve, 1)
                dve.wait_ge(chain_dve, links.next())
                tt(oh4, tmp4, bc(pick.unsqueeze(2), 2, 4), ALU.is_equal).then_inc(sem["route_oh"], 1)
                dve.wait_ge(sem["route_oh"], rise(l, "route_oh", 1))
                by_group = comb[:].rearrange("p s (g n) -> p s g n", g=N_GROUPS)
                tt(by_group, rt[:, :, 4:ROUTER].rearrange("p s (g n) -> p s g n", g=N_GROUPS),
                          bc(oh4.unsqueeze(3), 2, N_GROUPS, PER_GROUP), ALU.mult).then_inc(chain_dve, 1)
                dve.wait_ge(chain_dve, links.next())
                V.tensor_reduce(els, by_group.rearrange("p s g n -> p s n g"), AX.X, ALU.add).then_inc(chain_dve, 1)
                dve.wait_ge(chain_dve, links.next())
                for n, (m, oh) in enumerate(((m1, oh1), (m2, oh2))):
                    V.tensor_reduce(m, els, AX.X, ALU.max).then_inc(chain_dve, 1)
                    dve.wait_ge(chain_dve, links.next())
                    for s in range(NS):
                        last = stt(tmp8[:, s], els[:, s], m[:, s:s + 1], prio8, ALU.is_equal, ALU.mult)
                    last.then_inc(chain_dve, 1)
                    dve.wait_ge(chain_dve, links.next())
                    V.tensor_reduce(pick, tmp8, AX.X, ALU.max).then_inc(chain_dve, 1)
                    dve.wait_ge(chain_dve, links.next())
                    tt(oh, tmp8, bc(pick.unsqueeze(2), 2, PER_GROUP), ALU.is_equal).then_inc(chain_dve, 1)
                    dve.wait_ge(chain_dve, links.next())
                    if n == 0:
                        stt(els, oh1, -BIG, els, ALU.mult, ALU.add).then_inc(chain_dve, 1)
                        dve.wait_ge(chain_dve, links.next())
                tt(e2, m2, m1, ALU.subtract).then_inc(sem["route_d2"], 1)
                dve.wait_ge(sem["route_exp1"], rise(l, "route_exp1", 1))
                V.tensor_reduce(gs, gd, AX.X, ALU.add).then_inc(chain_dve, 1)
                dve.wait_ge(chain_dve, links.next())
                V.reciprocal(gw, gs).then_inc(chain_dve, 1)
                dve.wait_ge(chain_dve, links.next())
                dve.wait_ge(sem["route_exp2"], rise(l, "route_exp2", 1))
                ts(tw, e2, 1.0, None, ALU.add).then_inc(chain_dve, 1)
                dve.wait_ge(chain_dve, links.next())
                V.reciprocal(tw, tw).then_inc(chain_dve, 1)
                dve.wait_ge(chain_dve, links.next())
                tt(tw, tw, gw, ALU.mult).then_inc(chain_dve, 1)
                dve.wait_ge(chain_dve, links.next())
                tt(e2, e2, tw, ALU.mult).then_inc(chain_dve, 1)
                dve.wait_ge(chain_dve, links.next())
                tt(oh1, oh1, bc(tw.unsqueeze(2), 2, PER_GROUP), ALU.mult)
                tt(oh2, oh2, bc(e2.unsqueeze(2), 2, PER_GROUP), ALU.mult).then_inc(chain_dve, 1)
                dve.wait_ge(chain_dve, links.next())
                tt(c8, oh1, oh2, ALU.add).then_inc(chain_dve, 1)
                dve.wait_ge(chain_dve, links.next())
                dve.wait_ge(sem["rank_mm"], rise(l, "rank_mm", 1))
                V.tensor_reduce(gs[:, 0:1], ps[:, 1, 8:12], AX.X, ALU.max)
                tt(tmp4, ps[:, 1, 0:8].rearrange("p (s n) -> p s n", s=2), oh4, ALU.mult).then_inc(chain_dve, 1)
                dve.wait_ge(chain_dve, links.next())
                V.tensor_reduce(pick, tmp4, AX.X, ALU.add)
                copy(most[:], gs[:, 0:1]).then_inc(chain_dve, 1)
                dve.wait_ge(chain_dve, links.next())
                dve.sem_clear(chain_dve)
                links.restart()
                tt(by_group, bc(oh4.unsqueeze(3), 2, N_GROUPS, PER_GROUP), bc(c8.unsqueeze(2), 2, N_GROUPS, PER_GROUP), ALU.mult).then_inc(sem["route_dve"], 1)
                dve.wait_ge(sem["route_dve"], rise(l, "route_dve", 1))
                dve.sem_inc(sem["flag"], 1)
                def step(e, j, ahead=2):
                    if ahead > 1:
                        low(e + 2, (j + 2) % RING, 0, "lo_gate", "hi_gate")
                    if ahead > 0:
                        dve.wait_ge(sem["silu"], rise(l, "silu", e + 2))
                        dve.wait_ge(sem["up_mm"], rise(l, "up_mm", e + 2))
                        b = (j + 1) % 2
                        t = sg[:, b].rearrange("p f t -> p (f t)")
                        tt(t, t, bank(5 + 2 * b), ALU.mult).then_inc(sem["prod"], 1)
                        dve.wait_ge(sem["prod"], rise(l, "prod", e + 2))
                        weight = arena[:, bass.ds((e + 1) * TOK, TOK)]
                        tt(sg[:, b], sg[:, b], bc(weight.unsqueeze(1), 2, TOK), ALU.mult).then_inc(sem["act_dve"], 1)
                    if ahead > 1:
                        low(e + 2, (j + 2) % RING, 1, "lo_up", "hi_up")
                    if ahead > 0:
                        dve.wait_ge(sem["act_hi"], rise(l, "act_hi", e + 2))
                        tt(sg_lo[:, b], sg[:, b], gated_hi[:, b], ALU.subtract).then_inc(sem["act_lo"], 1)
                        low(e + 1, (j + 1) % RING, 2, "lo_down", "hi_down")

                def low_half(e, j, name, made, part):
                    dve.wait_ge(sem[made], rise(l, made, e))
                    cols = slice(part * 1024, part * 1024 + 1024)
                    raw_w, low_w, high_w = (a.rearrange("p (w n) -> p w n", w=2)[:, :, cols]
                                            for a in (ring[j][:, 0:4096], ring_r[j][:, 0:4096], w_hi[:, 0:4096]))
                    tt(low_w, raw_w, high_w, ALU.subtract).then_inc(sem[name], 1)

                def gathered_step(e, i, turn, ahead=2):
                    if i >= 0:
                        dve.wait_ge(sem["tr_mm"], rise(l, "tr_mm", e + 1))
                        copy(act_t[:, i % 2], bank(2 + i % 2, FF)).then_inc(sem["act_t"], 1)
                    if ahead > 1:
                        low_half(e + 2, (i + 2) % RING, "lo_a", "hi_a", 0)
                    if ahead > 0:
                        dve.wait_ge(sem["g_silu"], rise(l, "g_silu", e + 2))
                        b = (i + 1) % 2
                        stt(gat[:, b], ps[:, b, FF:2 * FF], cg[:, bass.ds(e + 1, 1)], g_silu[:, b], ALU.mult, ALU.mult).then_inc(sem["g_act"], 1)
                    if ahead > 1:
                        low_half(e + 2, (i + 2) % RING, "lo_b", "hi_b", 1)
                    if i == PER_GROUP - 1:
                        dve.wait_ge(sem["yg_hi"], rise(l, "yg_hi", turn + 1))
                        tt(hg_lo[:, :, bass.ds(turn * P, P)], ps[:, 4:6, :].rearrange("p b (k c) -> p (b k) c", c=P),
                           hg_hi[:, :, bass.ds(turn * P, P)], ALU.subtract).then_inc(sem["yg_lo"], 1)

                fullest = dve.value_load(most[0:1, 0:1], min_val=0, max_val=TOK)
                with dve.If(fullest < P + 1):
                    slot_of = g_silu[:, 0].rearrange("p (s c) -> p s c", s=2)
                    tt(slot_of, bc(C("cross_f").unsqueeze(1), 2, P), bc(pick.unsqueeze(2), 2, P), ALU.is_equal).then_inc(chain_dve, 1)
                    dve.wait_ge(chain_dve, 1)
                    tt(sel_r, bc(slot_of.unsqueeze(2), 2, N_GROUPS, P), bc(oh4.unsqueeze(3), 2, N_GROUPS, P), ALU.mult)
                    copy(c8_hi, c8).then_inc(chain_dve, 1)
                    dve.wait_ge(chain_dve, 2)
                    tt(c8_lo, c8, c8_hi, ALU.subtract).then_inc(sem["sel"], 1)
                    for n in range(4):
                        dve.wait_ge(sem["ht_hi"], rise(l, "ht_hi", n + 1))
                        cols = slice((n % 2) * 512, (n % 2 + 1) * 512)
                        tt(ht_lo[:, n // 2, cols], bank(2 + n), ht_hi[:, n // 2, cols], ALU.subtract).then_inc(sem["ht_lo"], 1)
                    for k in range(KT):
                        dve.wait_ge(sem["ga_hi"], rise(l, "ga_hi", k + 1))
                        tt(hg_lo[:, k, :], bank((6, 7, 0, 1)[k % 4]), hg_hi[:, k, :], ALU.subtract).then_inc(sem["ga_lo"], 1)
                    dve.wait_ge(sem["cg_mm"], rise(l, "cg_mm", 1))
                    copy(cg, ps[:, 4, 0:N_EXPERTS]).then_inc(sem["cg_dve"], 1)
                    dve.wait_ge(const_in, 32)
                    dve.wait_ge(sem["cg_dve"], rise(l, "cg_dve", 1))
                    dve.sem_clear(chain_dve)
                    dve.sem_inc(sem["yg_lo"], 1)
                    gathered_step(-1, -1, 0)
                    with dve.Fori(0, N_GROUPS - 1) as turn:
                        for i in range(PER_GROUP):
                            gathered_step(turn * PER_GROUP + i, i, turn)
                    for i in range(PER_GROUP):
                        gathered_step(N_EXPERTS - PER_GROUP + i, i, N_GROUPS - 1, ahead=PER_GROUP - 1 - i)
                    for name, n in (("cb_dve", 8), ("h_lo", 1), ("lo_gate", 31), ("lo_up", 31), ("lo_down", 32), ("prod", 32),
                                    ("act_dve", 32), ("act_lo", 32)):
                        dve.sem_inc(sem[name], n)
                    for f in range(0, KT, 2):
                        dve.wait_ge(sem["scatter_mm"], rise(l, "scatter_mm", f // 2 + 1))
                        last = residual(40, range(f, f + 2))
                    last.then_inc(sem["layer_done"], 1)
                with dve.Else():
                    for q in range(1, N_EXPERTS // 2, 2):
                        dve.wait_ge(sem["cb_mm"], rise(l, "cb_mm", q + 1))
                        copy(cb[:, 2 * q:2 * q + 2, :].rearrange("p e t -> p (e t)"), bank(q % 4)).then_inc(sem["cb_dve"], 1)
                    dve.wait_ge(sem["h_hi"], rise(l, "h_hi", 1))
                    tt(h_lo, hT[:], h_hi, ALU.subtract).then_inc(sem["h_lo"], 1)
                    dve.wait_ge(const_in, 32)
                    dve.wait_ge(sem["cb_act"], rise(l, "cb_act", 8))
                    dve.wait_ge(sem["cb_dve"], rise(l, "cb_dve", 8))
                    for e in range(-1, RING):
                        step(e, e % RING)
                    with dve.Fori(1, N_EXPERTS // RING - 1) as turn:
                        for j in range(RING):
                            step(turn * RING + j, j)
                    for e in range(N_EXPERTS - RING, N_EXPERTS - 1):
                        step(e, e % RING, ahead=N_EXPERTS - 1 - e)
                    dve.wait_ge(sem["down_mm"], rise(l, "down_mm", N_EXPERTS))
                    residual(40, range(KT)).then_inc(sem["layer_done"], 1)
                    for name in ("sel", "ht_lo", "ga_lo", "cg_dve", "lo_a", "lo_b", "g_act", "act_t", "yg_lo"):
                        dve.sem_inc(sem[name], PER[name])

        @block.gpsimd
        def _(pool):
            G = nc.gpsimd
            G.memset(condp[:], 0.0).then_inc(cond_zero, 1)
            with pool.Fori(0, DEPTH) as l:
                pool.wait_ge(const_in, 32)
                pool.wait_ge(sem["layer_done"], rise(l, "layer_done", 1))
                zeros = C("zeros")
                G.tensor_tensor(raw[:, :, :, 0:130:129].rearrange("p m s t -> p (m s) t"), zeros[:, 0:24].rearrange("p (a b) -> p a b", b=2),
                                zeros[:, 0:24].rearrange("p (a b) -> p a b", b=2), ALU.mult)
                G.memset(A("vp"), 0.0)
                G.memset(ub[:, :, :, 0:130:129].rearrange("p m s t -> p (m s) t"), 0.0)
                G.memset(A("gpad"), 0.0)
                G.memset(arena[:, ARENA["npad"].start:ARENA["rpad"].stop], 0.0).then_inc(sem["zeroed"], 1)
                pool.wait_ge(const_in, 32)
                pool.wait_ge(sem["zeroed"], rise(l, "zeroed", 1))
                pool.wait_ge(const_in, 32)
                pool.wait_ge(sem["qk_dve"], rise(l, "qk_dve", 1))
                G.tensor_copy(gpad[64:P, :, :, 1, :].rearrange("p t s c -> p (t s) c"),
                              qkv[64:P, 0:4, :].rearrange("p m (s c) -> p (m s) c", s=2))
                G.tensor_copy(npad[64:P, :, :, 1, :].rearrange("p j s c -> p (j s) c"),
                              natqk[64:P, 2:4, :].rearrange("p m (s c) -> p (m s) c", s=2)).then_inc(sem["pad_pool"], 1)
                pool.wait_ge(const_in, 32)
                pool.wait_ge(sem["rope_dve"], rise(l, "rope_dve", 1))
                G.tensor_copy(rpad[64:P, :, :, 1, :].rearrange("p j s c -> p (j s) c"),
                              retqk[64:P, 0:2, :].rearrange("p m (s c) -> p (m s) c", s=2)).then_inc(sem["rpad_pool"], 1)
                out = dst["nkT"][bass.ds(l, 1)].rearrange("o p j c -> (o p) j c")
                pool.dma_start(out, natqk[:, 2:4, 0:P]).then_inc(kv_out, 16)
                for i in range(2):
                    out = dst["nv"][bass.ds(l, 1)].rearrange("o p j i d -> (o p) j i d")[:, :, i, :]
                    pool.dma_start(out, vp[:, 0, 1, :, 192 * i:192 * i + HD]).then_inc(kv_out, 16)
                pool.wait_ge(const_in, 32)
                pool.wait_ge(sem["ret_st"], rise(l, "ret_st", 1))
                pool.dma_start(dst["s_ret"][bass.ds(l, 1)].rearrange("o p n -> (o p) n"),
                               state[:].rearrange("p d j n -> p (d j n)")).then_inc(state_out, 16)
                pool.wait_ge(const_in, 32)
                pool.wait_ge(sem["ret_out"], rise(l, "ret_out", 1))
                pool.wait_ge(kv_out, l * 48 + 48)
                pool.wait_ge(const_in, 32)
                pool.wait_ge(sem["nat_out"], rise(l, "nat_out", 1))
                G.tensor_tensor(group(0, 7), bc(zeros.unsqueeze(1), HEADS, P), bc(zeros.unsqueeze(1), HEADS, P), ALU.mult)
                G.memset(group(1, 7).rearrange("p h c -> p (h c)"), 0.0).then_inc(sem["vnp_zero"], 1)
                for s in range(NS):
                    pool.wait_ge(const_in, 32)
                    pool.wait_ge(sem["gr_dec"], rise(l, "gr_dec", s + 1))
                    for b in range(LEVELS):
                        for g in range(2):
                            n = (s * LEVELS + b) * 2 + g + 1
                            if b == 1:
                                pool.wait_ge(const_in, 32)
                                pool.wait_ge(sem["inv_upd"], rise(l, "inv_upd", n - 2))
                            elif n > 2:
                                pool.wait_ge(const_in, 32)
                                pool.wait_ge(sem["inv_dmm"], rise(l, "inv_dmm", n - 2))
                            G.tensor_tensor(group(g, 6), group(g, 2), bc(levels[:, g, b, :].unsqueeze(1), HEADS, P), ALU.mult)\
                             .then_inc(sem["inv_c"], 1)
                    if s == 0:
                        pool.wait_ge(const_in, 32)
                        pool.wait_ge(sem["gs_st"], rise(l, "gs_st", 1))
                        pool.dma_start(dst["s_gdn"][bass.ds(l, 1)].rearrange("o p n -> (o p) n"),
                                       state[:].rearrange("p d j n -> p (d j n)")).then_inc(state_out, 16)
                pool.wait_ge(state_out, l * 32 + 32)


def constants():
    c = np.zeros((P, CONST_W), np.float32)
    t = np.arange(P)
    k, m = t[:, None], t[None, :]

    def put(name, a):
        c[:, CONST[name]] = a

    put("ident", k == m)
    put("ones", 1.0)
    put("blockones", k // HD == m // HD)
    put("upto_f", k <= m)
    put("upto_b", k >= m)
    put("fold", (k % 32 == m)[:, :2 * ADA_TILES])
    put("after_f", k > m)
    put("after_b", k < m)
    half = HD // 4
    put("rot", np.where(m % (2 * half) < half, -1.0 * (k == m + half), 1.0 * (k == m - half)))
    freq = np.float32(10000.0) ** (-np.arange(half, dtype=np.float32) / np.float32(half))
    pos = np.where((t % HD)[:, None] < HD // 2, (t // GRID_W)[None, :], (t % GRID_W)[None, :]).astype(np.float32)
    angle = pos * freq[t % half][:, None]
    put("cos", np.cos(angle))
    put("sin", np.sin(angle))
    put("lag_f", np.maximum(m - k, 0))
    put("lag_b", np.maximum(k - m, 0))
    put("cross_f", np.broadcast_to(m + 1.0, (P, P)))
    put("cross_b", np.broadcast_to(P - 1.0 * m, (P, P)))
    col = t[:GRID_W]
    c0 = np.clip(col - WIN_COLS // 2, 0, GRID_W - WIN_COLS)
    inside = (col[None, :] >= c0[:, None]) & (col[None, :] < c0[:, None] + WIN_COLS)
    put("colmask", np.tile(np.where(inside, 0.0, -BIG), (P // GRID_W, 1)))
    put("idx", np.stack([P - 1 - t, t], 1))
    put("prio", np.arange(PER_GROUP, 0, -1))
    lv = np.zeros((P, 2, LEVELS, P), np.float32)
    for b in range(LEVELS):
        size = 2 ** b
        same = k // (2 * size) == m // (2 * size)
        lv[:, 0, b] = -1.0 * (same & (k // size % 2 == 0) & (m // size % 2 == 1))
        lv[:, 1, b] = -1.0 * (same & (k // size % 2 == 1) & (m // size % 2 == 0))
    put("levels", lv.reshape(P, -1))
    return c


def kernel(x_prompt, x_sample, state_gdn, state_ret, cache_nat_k, cache_nat_v, c, c_ctx,
           ada_w, ada_b, norm_mix_w, norm_ffn_w, w_in, gdn_conv_w, gdn_a_log, gdn_dt_bias, gdn_norm_w,
           ret_gamma_logit, nat_q_norm_w, nat_k_norm_w, nat_rpb, sc_conv_w, w_out,
           router_group_w, router_group_b, router_expert_w, router_expert_b,
           moe_w_gate, moe_w_up, moe_w_down):
    import concourse.bacc as _bacc
    from concourse.bass_utils import run_bass_kernel_spmd as _run

    A = np.asarray

    def feat(a):
        a = A(a)
        return np.swapaxes(a.reshape(*a.shape[:-1], -1, P), -1, -2)

    def rows(a):
        a = A(a)
        return np.moveaxis(a.reshape(*a.shape[:-2], -1, P, a.shape[-1]), -3, -2)

    x = np.stack([A(x_prompt)[0], A(x_sample)[0]])
    xT = np.ascontiguousarray(x.reshape(NS, P, KT, P).transpose(3, 2, 0, 1)).reshape(P, KT, TOK)
    condT = np.ascontiguousarray(feat(np.stack([A(c_ctx), A(c)[0]])).transpose(1, 2, 0))

    ada = np.ascontiguousarray(rows(ada_w).reshape(DEPTH, P, KT, ADA_SLOTS, 768).transpose(0, 3, 1, 2, 4)).reshape(DEPTH, ADA_SLOTS, P, SLOT)
    wi = rows(w_in)
    sizes = (768, 256, 8, 8, 768, 256, 768, 768)
    at = np.concatenate([[0], np.cumsum(sizes)])
    a_qkv, a_z, a_dec, a_beta, r_qkv, r_g, n_qkv, s_bcx = (wi[..., at[i]:at[i + 1]] for i in range(8))
    w_feat = np.stack([
        a_qkv,
        np.concatenate([n_qkv[..., :512], r_g], -1),
        np.concatenate([r_qkv[..., :512], a_z], -1),
        np.concatenate([s_bcx[..., :256], s_bcx[..., 512:], s_bcx[..., 256:512]], -1)], 1).reshape(DEPTH, 4, P, SLOT)
    w_tok = np.concatenate([a_dec, a_beta, r_qkv[..., 512:], n_qkv[..., 512:]], -1).reshape(DEPTH, P, KT * TOKCOLS)
    wo = rows(w_out)
    edge = np.concatenate([[0], np.cumsum(OUT_TILES)]) * P
    w_o = np.concatenate([wo[..., edge[i]:edge[i + 1]].reshape(DEPTH, P, -1) for i in range(OUT_SLOTS)], -1)
    moe = np.concatenate([rows(moe_w_gate).reshape(DEPTH, N_EXPERTS, P, -1), rows(moe_w_up).reshape(DEPTH, N_EXPERTS, P, -1),
                          rows(moe_w_down).reshape(DEPTH, N_EXPERTS, P, -1)], -1)

    par = np.zeros((DEPTH, P, PARAM_W), np.float32)

    def put(name, a):
        par[:, :, PARAM[name]] = a

    def everywhere(a):
        return np.broadcast_to(A(a).reshape(DEPTH, 1, -1), (DEPTH, P, A(a)[0].size))

    def pair(a):
        return np.concatenate([A(a), A(a)], 1)[:, :, None]

    put("norm_mix", feat(norm_mix_w))
    put("norm_ffn", feat(norm_ffn_w))
    put("ada_b", feat(ada_b))
    put("conv_gdn", feat(gdn_conv_w).transpose(0, 2, 3, 1).reshape(DEPTH, P, -1))
    put("conv_sc", feat(sc_conv_w).transpose(0, 2, 3, 1).reshape(DEPTH, P, -1))
    put("gdn_norm", pair(gdn_norm_w))
    put("q_norm", pair(nat_q_norm_w))
    put("k_norm", pair(nat_k_norm_w))
    put("dt_bias", everywhere(gdn_dt_bias))
    put("a_log", everywhere(gdn_a_log))
    put("gamma_cols", everywhere(ret_gamma_logit))
    put("gamma_rows", np.repeat(A(ret_gamma_logit).reshape(DEPTH, 2, 2, 2).transpose(0, 3, 1, 2).reshape(DEPTH, 2, 4), HD, 1))
    put("router_b", np.concatenate([everywhere(router_group_b), everywhere(router_expert_b)], -1))
    put("router_w", np.concatenate([rows(router_group_w), rows(router_expert_w)], -1).reshape(DEPTH, P, -1))
    r = np.arange(P) // GRID_W
    q = np.arange(P) % GRID_W
    i, cc = np.arange(2), np.arange(GRID_W)
    ri = i[None, :, None] - r[:, None, None] + WIN_ROWS - 1
    ci = np.clip(cc[None, None, :] - q[:, None, None], -(WIN_COLS - 1), WIN_COLS - 1) + WIN_COLS - 1
    put("nat_bias", A(nat_rpb)[:, :, ri, ci].transpose(0, 2, 1, 3, 4).reshape(DEPTH, P, -1))
    ck = np.zeros((DEPTH, 2, HD, HEADS, P), np.float32)
    cv = np.zeros((DEPTH, P, HEADS, 2, HD), np.float32)
    states = []
    for h in range(HEADS):
        ck[:, h % 2, :, h] = A(cache_nat_k)[0, :, :, h].transpose(0, 2, 1)
        cv[:, :, h, h % 2] = A(cache_nat_v)[0, :, :, h]
    for st in (state_gdn, state_ret):
        b = np.zeros((DEPTH, 2, HD, 2, 2, 2, HD), np.float32)
        for h in range(HEADS):
            b[:, h % 2, :, :, h // 2, h % 2] = A(st)[0, :, :, h].transpose(0, 2, 1, 3)
        states.append(b.reshape(DEPTH, P, -1))
    put("ck", ck.reshape(DEPTH, P, -1))
    put("cv", cv.reshape(DEPTH, P, -1))
    put("s_gdn", states[0])
    put("s_ret", states[1])

    nc = _bacc.Bacc("TRN2", target_bir_lowering=False, num_devices=1)
    arrays = dict(xT=xT, condT=condT, const=constants(), param=par, ada_w=ada, w_feat=w_feat, w_tok=w_tok, w_out=w_o, moe=moe)
    arrays = {n: np.ascontiguousarray(a) for n, a in arrays.items()}
    src = {n: nc.dram_tensor(f"in_{n}", list(a.shape), F32, kind="ExternalInput").ap() for n, a in arrays.items()}
    outs = dict(yT=(P, KT, TOK), nkT=(DEPTH, P, 2, P), nv=(DEPTH, P, 2, 2, HD), s_ret=(DEPTH, P, 4 * HD), s_gdn=(DEPTH, P, 4 * HD))
    dst = {n: nc.dram_tensor(f"out_{n}", list(shape), F32, kind="ExternalOutput").ap() for n, shape in outs.items()}
    build_trunk(nc, src, dst)
    got = _run(nc, [{f"in_{n}": a for n, a in arrays.items()}], core_ids=[0]).results[0]

    y = np.asarray(got["out_yT"]).reshape(P, KT, NS, P).transpose(2, 3, 1, 0).reshape(NS, P, D_MODEL)

    def state(a):
        return np.asarray(a).reshape(DEPTH, 2, HD, 2, 2, HD).transpose(0, 3, 4, 1, 2, 5).reshape(1, DEPTH, 2, HEADS, HD, HD)

    nk = np.asarray(got["out_nkT"]).reshape(DEPTH, 2, HD, 2, P).transpose(0, 4, 3, 1, 2).reshape(1, DEPTH, P, HEADS, HD)
    nv = np.asarray(got["out_nv"]).reshape(1, DEPTH, P, HEADS, HD)
    return (np.ascontiguousarray(y[0:1]), np.ascontiguousarray(y[1:2]), np.ascontiguousarray(state(got["out_s_gdn"])),
            np.ascontiguousarray(state(got["out_s_ret"])), np.ascontiguousarray(nk), np.ascontiguousarray(nv))
```
